# Optimizing a Trainium2 kernel written in Bass

```python
import jax, jax.numpy as jnp
from jax import lax
import numpy as np

D_MODEL = 2048
BATCH = 1
SEQ = 256
DEPTH = 1

HEAD_DIM = 128
N_ATTN_HEADS = 8
ATTN_WIDTH = N_ATTN_HEADS * HEAD_DIM
N_CONV_GROUPS = 8
CONV_CH = N_CONV_GROUPS * HEAD_DIM
MIX_WIDTH = ATTN_WIDTH + CONV_CH
IN_COLS = 3 * ATTN_WIDTH + 2 * CONV_CH
CONV_K = 31
MOBA_BLOCK = 256
MOBA_TOPK = 3
Q_CHUNK = 128
D_FF = -(-8 * D_MODEL // (3 * 256)) * 256
N_MOD = 6
RMS_EPS = 1e-6
LN_EPS = 1e-5
NEG_INF = -1e30


def rms_norm(x, g):
    x32 = x.astype(jnp.float32)
    y = x32 * lax.rsqrt(jnp.mean(x32 * x32, axis=-1, keepdims=True) + RMS_EPS)
    return (y * g.astype(jnp.float32)).astype(x.dtype)

def layer_norm(x, g, b):
    x32 = x.astype(jnp.float32)
    mu = jnp.mean(x32, axis=-1, keepdims=True)
    var = jnp.mean(jnp.square(x32 - mu), axis=-1, keepdims=True)
    y = (x32 - mu) * lax.rsqrt(var + LN_EPS) * g.astype(jnp.float32) + b.astype(jnp.float32)
    return y.astype(x.dtype)

def causal_depthwise_conv(u, w, b):
    k = w.shape[0]
    y = lax.conv_general_dilated(
        u, w[:, None, :].astype(u.dtype), window_strides=(1,),
        padding=((k - 1, 0),), dimension_numbers=('NWC', 'WIO', 'NWC'),
        feature_group_count=u.shape[-1])
    return y + b.astype(u.dtype)

def moba_attention(q, k, v):
    B, H, S, Dh = q.shape
    nb = -(-S // MOBA_BLOCK)
    n_sel = min(MOBA_TOPK, nb)
    pad = nb * MOBA_BLOCK - S
    kb = jnp.pad(k, ((0, 0), (0, 0), (0, pad), (0, 0))).reshape(B, H, nb, MOBA_BLOCK, Dh)
    vb = jnp.pad(v, ((0, 0), (0, 0), (0, pad), (0, 0))).reshape(B, H, nb, MOBA_BLOCK, Dh)
    k_mean = jnp.mean(kb.astype(jnp.float32), axis=3)
    n_chunks = S // Q_CHUNK
    q_chunks = q.reshape(B, H, n_chunks, Q_CHUNK, Dh).transpose(2, 0, 1, 3, 4)
    scale = HEAD_DIM ** -0.5
    b_idx = jnp.arange(B)[:, None, None]
    h_idx = jnp.arange(H)[None, :, None]
    blk_ids = jnp.arange(nb)

    def one_chunk(args):
        qc, ci = args
        q_pos = ci * Q_CHUNK + jnp.arange(Q_CHUNK)
        blk = (ci * Q_CHUNK) // MOBA_BLOCK
        gate = jnp.einsum('bhqd,bhnd->bhqn', qc.astype(jnp.float32), k_mean)
        gate = jnp.where(blk_ids < blk, gate, NEG_INF)
        _, sel = lax.top_k(gate, n_sel)
        k_own = lax.dynamic_index_in_dim(kb, blk, axis=2, keepdims=False)
        v_own = lax.dynamic_index_in_dim(vb, blk, axis=2, keepdims=False)
        k_pos = blk * MOBA_BLOCK + jnp.arange(MOBA_BLOCK)
        s_own = jnp.einsum('bhqd,bhkd->bhqk', qc, k_own,
                           preferred_element_type=jnp.float32) * scale
        s_own = jnp.where(k_pos[None, :] <= q_pos[:, None], s_own, NEG_INF)
        scores = [s_own]
        for j in range(n_sel):
            k_sel = kb[b_idx, h_idx, sel[..., j]]
            s_j = jnp.einsum('bhqd,bhqkd->bhqk', qc, k_sel,
                             preferred_element_type=jnp.float32) * scale
            scores.append(jnp.where(j < blk, s_j, NEG_INF))
        p = jax.nn.softmax(jnp.concatenate(scores, axis=-1), axis=-1).astype(v.dtype)
        p = p.reshape(B, H, Q_CHUNK, n_sel + 1, MOBA_BLOCK)
        out = jnp.einsum('bhqk,bhkd->bhqd', p[..., 0, :], v_own,
                         preferred_element_type=jnp.float32)
        for j in range(n_sel):
            v_sel = vb[b_idx, h_idx, sel[..., j]]
            out = out + jnp.einsum('bhqk,bhqkd->bhqd', p[..., j + 1, :], v_sel,
                                   preferred_element_type=jnp.float32)
        return out.astype(q.dtype)

    out = lax.map(one_chunk, (q_chunks, jnp.arange(n_chunks)))
    return out.transpose(1, 2, 0, 3, 4).reshape(B, H, S, Dh)

def hybrid_mixer(h, w_in, conv_w, conv_b, conv_ln_g, conv_ln_b, w_out):
    B, S, _ = h.shape
    proj = h @ w_in
    q, k, v, a, g = jnp.split(
        proj, [ATTN_WIDTH, 2 * ATTN_WIDTH, 3 * ATTN_WIDTH, 3 * ATTN_WIDTH + CONV_CH], axis=-1)

    def heads(t):
        return t.reshape(B, S, N_ATTN_HEADS, HEAD_DIM).transpose(0, 2, 1, 3)

    attn = moba_attention(heads(q), heads(k), heads(v))
    attn = attn.transpose(0, 2, 1, 3).reshape(B, S, ATTN_WIDTH)
    u = a * jax.nn.sigmoid(g)
    u = causal_depthwise_conv(u, conv_w, conv_b)
    u = jax.nn.silu(layer_norm(u, conv_ln_g, conv_ln_b))
    mix = jnp.concatenate([attn, u], axis=-1)
    return mix @ w_out

def swiglu_ffn(h, w_gate, w_up, w_down):
    return (jax.nn.silu(h @ w_gate) * (h @ w_up)) @ w_down

def first_inputs(seed: int = 0) -> dict:
    key = jax.random.key(seed)
    ks = jax.random.split(key, 18)

    def nrm(k, shape, s):
        return jax.random.normal(k, shape, jnp.float32) * s

    L, D = DEPTH, D_MODEL
    return {
        'x': nrm(ks[0], (BATCH, SEQ, D), 1.0),
        'c': nrm(ks[1], (BATCH, D), 1.0),
        'ada_w': nrm(ks[2], (L, D, N_MOD * D), 0.5 * D ** -0.5),
        'ada_b': nrm(ks[3], (L, N_MOD * D), 0.02),
        'mix_pre_g': 1.0 + nrm(ks[4], (L, D), 0.02),
        'mix_post_g': 1.0 + nrm(ks[5], (L, D), 0.02),
        'w_in': nrm(ks[6], (L, D, IN_COLS), D ** -0.5),
        'conv_w': nrm(ks[7], (L, CONV_K, CONV_CH), CONV_K ** -0.5),
        'conv_b': nrm(ks[8], (L, CONV_CH), 0.02),
        'conv_ln_g': 1.0 + nrm(ks[9], (L, CONV_CH), 0.02),
        'conv_ln_b': nrm(ks[10], (L, CONV_CH), 0.02),
        'w_out': nrm(ks[11], (L, MIX_WIDTH, D), MIX_WIDTH ** -0.5),
        'ffn_pre_g': 1.0 + nrm(ks[12], (L, D), 0.02),
        'ffn_post_g': 1.0 + nrm(ks[13], (L, D), 0.02),
        'w_gate': nrm(ks[14], (L, D, D_FF), D ** -0.5),
        'w_up': nrm(ks[15], (L, D, D_FF), D ** -0.5),
        'w_down': nrm(ks[16], (L, D_FF, D), D_FF ** -0.5),
    }

def first_block(x, c, ada_w, ada_b, mix_pre_g, mix_post_g, w_in, conv_w, conv_b,
              conv_ln_g, conv_ln_b, w_out, ffn_pre_g, ffn_post_g, w_gate, w_up, w_down):
    c_act = jax.nn.silu(c)
    for l in range(DEPTH):
        mod = c_act @ ada_w[l] + ada_b[l]
        sh1, sc1, g1, sh2, sc2, g2 = jnp.split(mod, N_MOD, axis=-1)
        h = rms_norm(x, mix_pre_g[l]) * (1.0 + sc1[:, None, :]) + sh1[:, None, :]
        y = hybrid_mixer(h, w_in[l], conv_w[l], conv_b[l], conv_ln_g[l], conv_ln_b[l], w_out[l])
        x = x + g1[:, None, :] * rms_norm(y, mix_post_g[l])
        h = rms_norm(x, ffn_pre_g[l]) * (1.0 + sc2[:, None, :]) + sh2[:, None, :]
        y = swiglu_ffn(h, w_gate[l], w_up[l], w_down[l])
        x = x + g2[:, None, :] * rms_norm(y, ffn_post_g[l])
    return x


CTX_LEN = 256
GRID_W = 64
N_MIXERS = 3
MIXER_NA = 0
MIXER_GMLP = 1
MIXER_CONV = 2
NA_HEADS = 16
HEAD_DIM_2 = D_MODEL // NA_HEADS
WIN_H = 8
WIN_W = 16
QROWS = 2
GM_WIDTH = 2 * D_MODEL
GM_GROUPS = 16
GM_GROUP_DIM = GM_WIDTH // GM_GROUPS
GM_CHUNK = 128
FFN_DIM = 5504
EPS = 1e-6


def rms_norm_2(x, g):
    x32 = x.astype(jnp.float32)
    y = x32 * lax.rsqrt(jnp.mean(x32 * x32, axis=-1, keepdims=True) + EPS)
    return (y * g.astype(jnp.float32)).astype(x.dtype)

def adaln(cond, w, b):
    return jnp.split(jax.nn.silu(cond) @ w + b, N_MOD, axis=-1)

def modulate(x, shift, scale):
    return x * (1.0 + scale) + shift

def dwconv3(z, w, b=None):
    zp = jnp.pad(z, ((0, 0), (1, 1), (0, 0)))
    y = zp[:, :-2] * w[0] + zp[:, 1:-1] * w[1] + zp[:, 2:] * w[2]
    return y if b is None else y + b

def neighbourhood_attention(h, hc, w_qkv, q_g, k_g, rpb, w_o, ctx_out):
    bn, n, d = h.shape
    rows = n // GRID_W
    kh = min(WIN_H, rows)
    nb = min(kh + QROWS - 1, rows)
    n_blk = rows // QROWS
    qw = QROWS * GRID_W
    nk = nb * GRID_W
    scale = HEAD_DIM_2 ** -0.5

    def project(t):
        q, k, v = jnp.split(t @ w_qkv, 3, axis=-1)
        sh = (t.shape[0], t.shape[1], NA_HEADS, HEAD_DIM_2)
        return rms_norm_2(q.reshape(sh), q_g), rms_norm_2(k.reshape(sh), k_g), v.reshape(sh)

    q, k, v = project(h)
    qc, kc, vc = project(hc)
    kg = k.reshape(bn, rows, GRID_W, NA_HEADS, HEAD_DIM_2)
    vg = v.reshape(bn, rows, GRID_W, NA_HEADS, HEAD_DIM_2)

    q_row_off = jnp.repeat(jnp.arange(QROWS), GRID_W)
    q_col = jnp.tile(jnp.arange(GRID_W), QROWS)
    k_row_off = jnp.repeat(jnp.arange(nb), GRID_W)
    k_col = jnp.tile(jnp.arange(GRID_W), nb)
    c_start = jnp.clip(q_col - WIN_W // 2, 0, GRID_W - WIN_W)
    col_ok = (k_col[None, :] >= c_start[:, None]) & (k_col[None, :] < c_start[:, None] + WIN_W)
    dc_idx = jnp.clip(k_col[None, :] - q_col[:, None], -(WIN_W - 1), WIN_W - 1) + WIN_W - 1

    def block(args):
        blk, qb = args
        r0 = blk * QROWS
        q_row = r0 + q_row_off
        r_start = jnp.clip(q_row - kh // 2, 0, rows - kh)
        band0 = jnp.minimum(jnp.clip(r0 - kh // 2, 0, rows - kh), rows - nb)
        k_row = band0 + k_row_off
        kb = lax.dynamic_slice_in_dim(kg, band0, nb, axis=1).reshape(bn, nk, NA_HEADS, HEAD_DIM_2)
        vb = lax.dynamic_slice_in_dim(vg, band0, nb, axis=1).reshape(bn, nk, NA_HEADS, HEAD_DIM_2)
        ok = col_ok & (k_row[None, :] >= r_start[:, None]) & (k_row[None, :] < r_start[:, None] + kh)
        dr_idx = jnp.clip(k_row[None, :] - q_row[:, None], -(WIN_H - 1), WIN_H - 1) + WIN_H - 1
        bias = rpb[:, dr_idx, dc_idx].astype(jnp.float32)
        s_lat = jnp.einsum('bqhd,bkhd->bhqk', qb, kb).astype(jnp.float32) * scale + bias
        s_lat = jnp.where(ok, s_lat, -jnp.inf)
        s_ctx = jnp.einsum('bqhd,bchd->bhqc', qb, kc).astype(jnp.float32) * scale
        p = jax.nn.softmax(jnp.concatenate([s_lat, s_ctx], axis=-1), axis=-1).astype(vb.dtype)
        return (jnp.einsum('bhqk,bkhd->bqhd', p[..., :nk], vb)
                + jnp.einsum('bhqc,bchd->bqhd', p[..., nk:], vc))

    q_blocks = q.reshape(bn, n_blk, qw, NA_HEADS, HEAD_DIM_2).transpose(1, 0, 2, 3, 4)
    o = lax.map(block, (jnp.arange(n_blk), q_blocks))
    y = o.transpose(1, 0, 2, 3, 4).reshape(bn, n, d) @ w_o
    yc = None
    if ctx_out:
        s = jnp.einsum('bqhd,bkhd->bhqk', qc, kc).astype(jnp.float32) * scale
        p = jax.nn.softmax(s, axis=-1).astype(vc.dtype)
        yc = jnp.einsum('bhqk,bkhd->bqhd', p, vc).reshape(bn, hc.shape[1], d) @ w_o
    return y, yc

def chunk_gmlp(h, w_in, v_g, w_s, b_s, w_out):
    bn, n, _ = h.shape
    u, v = jnp.split(jax.nn.gelu(h @ w_in), 2, axis=-1)
    v = rms_norm_2(v, v_g)
    vch = v.reshape(bn, n // GM_CHUNK, GM_CHUNK, GM_GROUPS, GM_GROUP_DIM)
    sv = jnp.einsum('gij,bnjgd->bnigd', w_s, vch) + b_s.T[None, None, :, :, None]
    return (u * sv.reshape(bn, n, GM_WIDTH)) @ w_out

def short_conv(h, w_in, conv_w, w_out):
    b_gate, c_gate, xv = jnp.split(h @ w_in, 3, axis=-1)
    return (b_gate * dwconv3(c_gate * xv, conv_w)) @ w_out

def conv_ffn(h, w_up, conv_w, conv_b, w_down):
    gate, up = jnp.split(dwconv3(h @ w_up, conv_w, conv_b), 2, axis=-1)
    return (jax.nn.silu(gate) * up) @ w_down

def second_inputs(seed: int = 0) -> dict:
    key = jax.random.key(seed)
    keys = iter(jax.random.split(key, 40))

    def nrm(shape, s):
        return jax.random.normal(next(keys), shape, jnp.float32) * s

    d = D_MODEL
    n_na = len(range(MIXER_NA, DEPTH, N_MIXERS))
    n_gm = len(range(MIXER_GMLP, DEPTH, N_MIXERS))
    n_sc = len(range(MIXER_CONV, DEPTH, N_MIXERS))
    return {
        'x': nrm((BATCH, SEQ, d), 1.0),
        'c': nrm((BATCH, d), 1.0),
        'ctx': nrm((BATCH, CTX_LEN, d), 1.0),
        'c_ctx': nrm((d,), 1.0),
        'norm_mix_g': 1.0 + nrm((DEPTH, d), 0.1),
        'norm_ffn_g': 1.0 + nrm((DEPTH, d), 0.1),
        'w_ada': nrm((DEPTH, d, N_MOD * d), 0.5 * d ** -0.5),
        'b_ada': nrm((DEPTH, N_MOD * d), 0.02),
        'na_w_qkv': nrm((n_na, d, 3 * d), d ** -0.5),
        'na_q_g': 1.0 + nrm((n_na, HEAD_DIM_2), 0.1),
        'na_k_g': 1.0 + nrm((n_na, HEAD_DIM_2), 0.1),
        'na_rpb': nrm((n_na, NA_HEADS, 2 * WIN_H - 1, 2 * WIN_W - 1), 0.2),
        'na_w_o': nrm((n_na, d, d), d ** -0.5),
        'gm_w_in': nrm((n_gm, d, 2 * GM_WIDTH), d ** -0.5),
        'gm_v_g': 1.0 + nrm((n_gm, GM_WIDTH), 0.1),
        'gm_w_s': nrm((n_gm, GM_GROUPS, GM_CHUNK, GM_CHUNK), GM_CHUNK ** -0.5),
        'gm_b_s': 1.0 + nrm((n_gm, GM_GROUPS, GM_CHUNK), 0.1),
        'gm_w_out': nrm((n_gm, GM_WIDTH, d), GM_WIDTH ** -0.5),
        'sc_w_in': nrm((n_sc, d, 3 * d), d ** -0.5),
        'sc_conv_w': nrm((n_sc, 3, d), 3 ** -0.5),
        'sc_w_out': nrm((n_sc, d, d), d ** -0.5),
        'ffn_w_up': nrm((DEPTH, d, 2 * FFN_DIM), d ** -0.5),
        'ffn_conv_w': nrm((DEPTH, 3, 2 * FFN_DIM), 3 ** -0.5),
        'ffn_conv_b': nrm((DEPTH, 2 * FFN_DIM), 0.02),
        'ffn_w_down': nrm((DEPTH, FFN_DIM, d), FFN_DIM ** -0.5),
    }

def second_block(x, c, ctx, c_ctx, norm_mix_g, norm_ffn_g, w_ada, b_ada,
              na_w_qkv, na_q_g, na_k_g, na_rpb, na_w_o,
              gm_w_in, gm_v_g, gm_w_s, gm_b_s, gm_w_out,
              sc_w_in, sc_conv_w, sc_w_out,
              ffn_w_up, ffn_conv_w, ffn_conv_b, ffn_w_down):
    cond_lat = c[:, None, :]
    cond_ctx = c_ctx[None, None, :]
    for i in range(DEPTH):
        last = i == DEPTH - 1
        m, j = i % N_MIXERS, i // N_MIXERS
        sh1, sc1, g1, sh2, sc2, g2 = adaln(cond_lat, w_ada[i], b_ada[i])
        h = modulate(rms_norm_2(x, norm_mix_g[i]), sh1, sc1)
        hc = None
        if (not last) or m == MIXER_NA:
            csh1, csc1, cg1, csh2, csc2, cg2 = adaln(cond_ctx, w_ada[i], b_ada[i])
            hc = modulate(rms_norm_2(ctx, norm_mix_g[i]), csh1, csc1)
        if m == MIXER_NA:
            y, yc = neighbourhood_attention(h, hc, na_w_qkv[j], na_q_g[j], na_k_g[j],
                                            na_rpb[j], na_w_o[j], not last)
        elif m == MIXER_GMLP:
            y = chunk_gmlp(h, gm_w_in[j], gm_v_g[j], gm_w_s[j], gm_b_s[j], gm_w_out[j])
            yc = None if last else chunk_gmlp(hc, gm_w_in[j], gm_v_g[j], gm_w_s[j], gm_b_s[j], gm_w_out[j])
        else:
            y = short_conv(h, sc_w_in[j], sc_conv_w[j], sc_w_out[j])
            yc = None if last else short_conv(hc, sc_w_in[j], sc_conv_w[j], sc_w_out[j])
        x = x + g1 * y
        hf = modulate(rms_norm_2(x, norm_ffn_g[i]), sh2, sc2)
        x = x + g2 * conv_ffn(hf, ffn_w_up[i], ffn_conv_w[i], ffn_conv_b[i], ffn_w_down[i])
        if not last:
            ctx = ctx + cg1 * yc
            hcf = modulate(rms_norm_2(ctx, norm_ffn_g[i]), csh2, csc2)
            ctx = ctx + cg2 * conv_ffn(hcf, ffn_w_up[i], ffn_conv_w[i], ffn_conv_b[i], ffn_w_down[i])
    return x


def setup_inputs(seed=0):
    out = dict(first_inputs(seed))
    for name, value in second_inputs(seed + 1).items():
        if name != "x":
            out[name + "_2"] = value
    return out


def reference(
    x, c, ada_w, ada_b, mix_pre_g, mix_post_g, w_in, conv_w, conv_b, conv_ln_g, conv_ln_b,
    w_out, ffn_pre_g, ffn_post_g, w_gate, w_up, w_down, c_2, ctx_2, c_ctx_2, norm_mix_g_2,
    norm_ffn_g_2, w_ada_2, b_ada_2, na_w_qkv_2, na_q_g_2, na_k_g_2, na_rpb_2, na_w_o_2,
    gm_w_in_2, gm_v_g_2, gm_w_s_2, gm_b_s_2, gm_w_out_2, sc_w_in_2, sc_conv_w_2, sc_w_out_2,
    ffn_w_up_2, ffn_conv_w_2, ffn_conv_b_2, ffn_w_down_2,
):
    x = first_block(
        x, c, ada_w, ada_b, mix_pre_g, mix_post_g, w_in, conv_w, conv_b, conv_ln_g, conv_ln_b,
        w_out, ffn_pre_g, ffn_post_g, w_gate, w_up, w_down,
    )
    return second_block(
        x, c_2, ctx_2, c_ctx_2, norm_mix_g_2, norm_ffn_g_2, w_ada_2, b_ada_2, na_w_qkv_2,
        na_q_g_2, na_k_g_2, na_rpb_2, na_w_o_2, gm_w_in_2, gm_v_g_2, gm_w_s_2, gm_b_s_2,
        gm_w_out_2, sc_w_in_2, sc_conv_w_2, sc_w_out_2, ffn_w_up_2, ffn_conv_w_2, ffn_conv_b_2,
        ffn_w_down_2,
    )


_drawn_inputs = setup_inputs


def setup_inputs(seed=0):
    import zlib

    import numpy as np

    out = dict(_drawn_inputs(seed))
    spreads = {}
    factors = {'mix_pre_g': 8.0,
     'mix_post_g': 8.0,
     'conv_b': 5.942,
     'conv_ln_g': 8.0,
     'conv_ln_b': 8.0,
     'ffn_pre_g': 7.252,
     'ffn_post_g': 8.0,
     'norm_mix_g_2': 8.0,
     'b_ada_2': 3.362,
     'na_q_g_2': 8.0,
     'na_k_g_2': 8.0,
     'na_rpb_2': 8.0,
     'ffn_conv_b_2': 42.974,
     'norm_ffn_g_2': 8.0}
    for name, (base, spread) in spreads.items():
        noise = np.random.default_rng([zlib.crc32(name.encode()), seed]).standard_normal(out[name].shape)
        drawn = base * np.exp(spread * noise) if base else spread * noise
        out[name] = __import__('jax').numpy.asarray(drawn.astype(out[name].dtype))
    for name, factor in factors.items():
        out[name] = (out[name] * factor).astype(out[name].dtype)
    return out
```

```python
from contextlib import ExitStack

import concourse.bass as bass
from concourse import mybir

F32 = mybir.dt.float32
F32R = mybir.dt.float32r
ALU = mybir.AluOpType
ACT = mybir.ActivationFunctionType
AX = mybir.AxisListType.X

P = 128
D = 2048
KD = D // P
SEQ = 256
NT = SEQ // P
HD = 128
C = 512
GH = C // HD
TILE = 1024
RING = 4
CT = KD * C // TILE
H1 = 8
TAPS = 31
FF1 = 5632
FF2 = 5504
NCH = FF1 // C
TAILC = FF2 - (NCH - 1) * C
H2 = 16
GRID = 64
ROWS = SEQ // GRID
RPB_H, RPB_W = 15, 31
DR = 2 * ROWS - 1
LANES = 2 * GRID
NEG = -1e30
SCALE = float(HD) ** -0.5
RMS_EPS = 1e-6
LN_EPS = 1e-5

T_AG = 0
T_QKV1 = T_AG + 4 * CT
T_OUT1 = T_QKV1 + 6 * CT
T_FF1 = T_OUT1 + 2 * KD
T_DOWN1 = T_FF1 + 2 * NCH * CT
T_QKV2 = T_DOWN1 + 2 * (FF1 // P)
T_OUT2 = T_QKV2 + 12 * CT
T_FF2 = T_OUT2 + 2 * KD
T_DOWN2 = T_FF2 + 2 * NCH * CT
T_END = T_DOWN2 + 2 * (FF2 // P)

UNITS = 2 * KD
(A_SH1, A_SC1, A_G1, A_SH2, A_SC2, A_G2, B_SH1, B_SC1, B_G1, B_SH2, B_SC2, B_G2) = range(12)


def program(nc, ins, out):
    ctx = ExitStack()
    with ctx:
        names = [0]
        base = -(-nc.sbuf_base // 64) * 64

        def at(name, shape, offset, dt=F32):
            return nc.alloc_sbuf_tensor_at(name, shape, dt, offset=base + offset)

        KB = 1024
        x = at("x", [P, NT, D], 0)
        tmp = at("tmp", [P, D], 16 * KB)
        nat_a = at("nat_a", [P, NT, C], 16 * KB)
        nat_b = at("nat_b", [P, NT, C], 20 * KB)
        prob = at("prob", [P, 2, C], 16 * KB)
        h_hi = at("h_hi", [P, KD, SEQ], 24 * KB, F32R)
        h_lo = at("h_lo", [P, KD, SEQ], 40 * KB, F32R)
        raw = at("raw", [P, RING, TILE], 56 * KB)
        w_hi = at("w_hi", [P, RING, TILE], 72 * KB, F32R)
        w_lo = at("w_lo", [P, RING, TILE], 88 * KB, F32R)
        ada = at("ada", [P, 2, TILE], 104 * KB)
        acc0 = at("acc0", [P, D], 112 * KB)
        acc1 = at("acc1", [P, D], 120 * KB)
        ff = at("ff", [P, 48, SEQ], 128 * KB)
        hc_hi = at("hc_hi", [P, KD, SEQ], 144 * KB, F32R)
        hc_lo = at("hc_lo", [P, KD, SEQ], 160 * KB, F32R)
        PADT = TAPS - 1 + SEQ
        u_pad = at("u_pad", [P, H1, PADT], 144 * KB)
        causal = at("causal", [P, NT, SEQ], 154 * KB)
        cvec = at("cvec", [P, 24 + H1 * TAPS], 156 * KB)
        mean1 = at("mean1", [P, P], 158 * KB)
        rstd_ln = at("rstd_ln", [P, SEQ], 159 * KB)
        st_vec = at("st_vec", [112, P], 128 * KB)
        st_c24 = at("st_c24", [24, P], 128 * KB + 512)
        st_cw = at("st_cw", [TAPS, H1 * P], 129 * KB)
        st_fc = at("st_fc", [86, 4, P], 133 * KB)
        junk = at("junk", [P, D], 128 * KB)
        tab = at("tab", [DR * H2, LANES], 161 * KB)
        E = 176 * KB
        q_t = at("q_t", [P, GH, SEQ], E)
        k_t = at("k_t", [P, GH, 2 * SEQ], E + 4 * KB)
        v_n = at("v_n", [P, 2 * NT, C], E + 12 * KB)
        p_t = at("p_t", [P, 2, C], E + 20 * KB)
        bias_t = at("bias_t", [P, 2, SEQ], E + 24 * KB)
        scr = at("scr", [P, D], E)
        sig = at("sig", [P, NT, C], E)
        act_n = at("act_n", [P, NT, C], E + 4 * KB)
        conv_t = at("conv_t", [P, GH, SEQ], E + 8 * KB)
        gate_t = at("gate_t", [P, GH, SEQ], E + 12 * KB)
        f_hi = at("f_hi", [P, 2, SEQ], E + 16 * KB, F32R)
        f_lo = at("f_lo", [P, 2, SEQ], E + 18 * KB, F32R)
        h_f = at("h_f", [P, 2, C], E + 20 * KB)
        skew_s = at("skew_s", [GRID, H2 * DR, GRID], 162 * KB)
        S0 = 202 * KB
        ident = at("ident", [P, P], S0)
        ones = at("ones", [P, P], S0 + 512)
        vecs = at("vecs", [P, 112], S0 + 1024)
        cact = at("cact", [P, 48], S0 + 1472)
        fcw = at("fcw", [P, 4, 86], S0 + 1664)
        qg = at("qg", [P, HD], S0 + 3040)
        kg = at("kg", [P, HD], S0 + 3552)
        cols = at("cols", [P, 10, KD], S0 + 4064)
        stat = at("stat", [P, 64], S0 + 4704)
        eps_rms = at("eps_rms", [P, 1], S0 + 4960)
        eps_ln = at("eps_ln", [P, 1], S0 + 4992)
        assert base + S0 + 5024 <= nc.sbuf_usable_end

        ps = ctx.enter_context(nc.psum_tensor("ps", [P, 8, C], F32))

        table_d = nc.dram_tensor("rpb_table", (H2 * DR, GRID, LANES), F32, kind="Internal").ap()
        skew_d = nc.dram_tensor("rpb_skewed", (GRID, H2 * DR, GRID), F32, kind="Internal").ap()

        def sem(name):
            return ctx.enter_context(nc.semaphore(name))

        raw_landed = [sem(f"raw_landed{i}") for i in range(RING)]
        hi_ready = sem("hi_ready")
        lo_ready = sem("lo_ready")
        tile_used = sem("tile_used")
        ada_landed = [sem(f"ada_landed{i}") for i in range(2)]
        ada_used = sem("ada_used")
        acc_clear = sem("acc_clear")
        acc_bias = [sem(f"acc_bias{i}") for i in range(3)]
        vec_landed = sem("vec_landed")
        small_landed = sem("small_landed")
        x_landed = sem("x_landed")
        ctx_landed = sem("ctx_landed")
        post_landed = sem("post_landed")
        out_landed = sem("out_landed")
        const_ready = sem("const_ready")
        pool_step = sem("pool_step")
        table_landed = sem("table_landed")
        bias_landed = [sem(f"bias_landed{i}") for i in range(2)]
        tr_done = [sem(f"tr_done{i}") for i in range(2)]
        tr_free = [sem(f"tr_free{i}") for i in range(2)]
        pair_free = [sem(f"pair_free{i}") for i in range(3)]
        cact_ready = sem("cact_ready")
        ss_ready = sem("ss_ready")
        xn_ready = sem("xn_ready")
        hf_ready = sem("hf_ready")
        hhi_ready = sem("hhi_ready")
        hlo_ready = sem("hlo_ready")
        sig_ready = sem("sig_ready")
        conv_step = sem("conv_step")
        std_ready = sem("std_ready")
        head_ss = sem("head_ss")
        head_std = sem("head_std")
        dev_ready = sem("dev_ready")
        sq_ready = sem("sq_ready")
        sq_read = sem("sq_read")
        ln_ready = sem("ln_ready")
        s_done = sem("s_done")
        max_ready = sem("max_ready")
        exp_ready = sem("exp_ready")
        p_ready = sem("p_ready")
        o_done = sem("o_done")
        o_used = sem("o_used")
        fhi_ready = sem("fhi_ready")
        flo_ready = sem("flo_ready")
        cv_ready = sem("cv_ready")
        ff_ready = sem("ff_ready")
        x_ready = sem("x_ready")
        dve_step = sem("dve_step")
        act_step = sem("act_step")

        M, m = {}, 0
        for name, n in (("vec", 2), ("a_sh1", 1), ("a_sc1", 1), ("x1", 4), ("u", 2), ("qkv1", 12),
                        ("ln", 1), ("a_g1", 2), ("a_sh2", 1), ("a_sc2", 1), ("x2", 4), ("ffn1", NCH),
                        ("a_g2", 2), ("b_sh1", 2), ("b_sc1", 2), ("lat", 4), ("ctx", 4),
                        ("qkv2", 28), ("b_g1", 2), ("b_sh2", 1), ("b_sc2", 1), ("x7", 4),
                        ("ffn2", 2 * NCH), ("b_g2", 2)):
            M[name] = m
            m += n
        USE0 = {"ag": 0, "k1": 2, "gate1": 4, "qkv2": 4 + NCH, "gate2": 12 + NCH}
        USE1 = {"ag": 0, "v1": 2, "up1": 4, "kc2": 4 + NCH, "up2": 8 + NCH}
        USE2 = {"q1": 0, "qkv2": 2}
        F_OUT1, F_DOWN1 = 0, KD
        F_OUT2 = F_DOWN1 + FF1 // P
        F_DOWN2 = F_OUT2 + KD
        UNITS1 = 16
        PER_GROUP = 2 * GH

        block = ctx.enter_context(nc.Block())

        @block.sync
        def _(sp):
            def tile_cols(T, j, w, j2, col, width=C):
                s = j % RING
                dst = raw[:, s, 0:2 * width].rearrange("p (k n) -> p k n", k=2)
                src = w.rearrange("(k p) n -> p k n", p=P)[:, 2 * j2:2 * j2 + 2, bass.ds(col, width)]
                sp.wait_ge(lo_ready, T + j + 1)
                sp.dma_start(dst, src).then_inc(raw_landed[s], 16)

            def tile_rows(T, j, w, row):
                s = j % RING
                src = w[bass.ds(row, P), j % 2 * TILE:(j % 2 + 1) * TILE]
                sp.wait_ge(lo_ready, T + j + 1)
                sp.dma_start(raw[:, s, :], src).then_inc(raw_landed[s], 16)

            def unit(w, sec, n, row, half):
                src = w[bass.ds(row, P), sec * D + half * TILE:sec * D + (half + 1) * TILE]
                sp.wait_ge(ada_used, n + 1)
                sp.dma_start(ada[:, half, :], src).then_inc(ada_landed[half], 16)

            def bias_row(n, which, b, sec):
                acc = (acc0, acc1, tmp)[which]
                sp.wait_ge(acc_clear, n)
                sp.dma_start(acc[0:1, :], b[0:1, sec * D:(sec + 1) * D]).then_inc(acc_bias[which], 16)

            w_in, w_out1, w_gate, w_up1, w_down1 = (ins[k][0] for k in ("w_in", "w_out", "w_gate", "w_up", "w_down"))
            w_qkv, w_o2, w_up2, w_down2 = (ins[k][0] for k in ("na_w_qkv_2", "na_w_o_2", "ffn_w_up_2", "ffn_w_down_2"))
            ada1, ada2 = ins["ada_w"][0], ins["w_ada_2"][0]
            b1, b2 = ins["ada_b"], ins["b_ada_2"]

            bias_row(1, 1, b1, 0)
            bias_row(2, 0, b1, 1)
            for sec in range(2):
                with sp.Fori(0, KD) as k:
                    for half in range(2):
                        unit(ada1, sec, k * 2 + (UNITS * sec + half), k * P, half)

            def ag(i, j):
                tile_cols(T_AG + 2 * CT * i, j, w_in, j % CT, (3 + j // CT) * H1 * HD + C * i)

            def qkv1(i, j):
                tile_cols(T_QKV1 + 3 * CT * i, j, w_in, j % CT, j // CT * H1 * HD + C * i)

            for j in range(3):
                ag(0, j)
            bias_row(3, 0, b1, 2)
            for i in range(2):
                for n in range(2 * CT):
                    j = n + 3
                    if j < 2 * CT:
                        ag(i, j)
                    elif i == 0:
                        ag(1, j - 2 * CT)
                    else:
                        qkv1(0, j - 2 * CT)
                    unit(ada1, 2, UNITS * 2 + 2 * CT * i + n, (KD // 2 * i + n // 2) * P, n % 2)
            bias_row(4, 1, b1, 3)
            for i in range(2):
                for n in range(3 * CT):
                    j = n + 3
                    if j < 3 * CT:
                        qkv1(i, j)
                    elif i == 0:
                        qkv1(1, j - 3 * CT)
                    else:
                        tile_rows(T_OUT1, j - 3 * CT, w_out1, (j - 3 * CT) // 2 * P)
                    if n < 2 * CT:
                        unit(ada1, 3, UNITS * 3 + 2 * CT * i + n, (KD // 2 * i + n // 2) * P, n % 2)

            def rows_pairs(T0, w, pairs, per_pair=0, sec=0, n0=0, ada_w=None, start=0):
                with sp.Fori(start, pairs) as i:
                    for j in range(4):
                        tile_rows(T0 + i * 4, j + 3, w, i * (2 * P) + (j + 3) // 2 * P)
                        if j < per_pair:
                            unit(ada_w, sec, n0 + i * per_pair + j, i * (per_pair // 2 * P) + j // 2 * P, j % 2)

            bias_row(5, 1, b1, 4)
            rows_pairs(T_OUT1, w_out1, KD // 2 - 1, 4, 4, UNITS * 4, ada1)

            def gate_up(T0, w_g, w_u, off):
                def one(i, j):
                    if j < CT:
                        tile_cols(T0 + CT + i * (2 * CT), j, w_u, j, off + i * C)
                    else:
                        tile_cols(T0 + CT + i * (2 * CT), j, w_g, j - CT, i * C + C)
                return one

            def last_pair_of_rows(T0, w, K, units, head):
                i = K // 2 - 1
                for j in range(4):
                    if j == 0:
                        tile_rows(T0 + 4 * i, 3, w, (2 * i + 1) * P)
                    else:
                        head(j - 1)
                    units(j)

            last_pair_of_rows(T_OUT1, w_out1, KD,
                              lambda j: unit(ada1, 4, UNITS * 5 - 4 + j, (KD - 2 + j // 2) * P, j % 2),
                              lambda j: tile_cols(T_FF1, j, w_gate, j, 0))

            one = gate_up(T_FF1, w_gate, w_up1, 0)
            bias_row(6, 0, b1, 5)
            for j in range(3, CT):
                tile_cols(T_FF1, j, w_gate, j, 0)
            for j in range(3):
                one(0, j)

            def ff1_loop(start, end, w, sec, n0):
                with sp.Fori(start, end) as i:
                    for n in range(2 * CT):
                        j = n + 3
                        if j < 2 * CT:
                            one(i, j)
                        else:
                            one(i + 1, j - 2 * CT)
                        if w is not None and n % 2 == 0:
                            u = n // 2
                            unit(w, sec, n0 + (i - start) * 8 + u, (i - start) * (4 * P) + u // 2 * P, u % 2)

            ff1_loop(0, 4, ada1, 5, UNITS * 5)
            bias_row(7, 1, b2, 0)
            bias_row(8, 2, b2, 0)
            ff1_loop(4, 8, ada2, 0, UNITS * 6)
            ff1_loop(8, NCH - 1, None, 0, 0)
            for j in range(3, CT):
                one(NCH - 1, j)
            for j in range(3):
                tile_rows(T_DOWN1, j, w_down1, j // 2 * P)
            bias_row(9, 1, b2, 1)
            bias_row(10, 2, b2, 1)
            rows_pairs(T_DOWN1, w_down1, 16, 2, 1, UNITS * 7, ada2)
            rows_pairs(T_DOWN1, w_down1, FF1 // P // 2 - 1, start=16)

            def qkv2(i, j):
                tile_cols(T_QKV2 + i * (3 * CT), j, w_qkv, j % CT, i * C + j // CT * D)

            last_pair_of_rows(T_DOWN1, w_down1, FF1 // P, lambda j: None, lambda j: qkv2(0, j))
            bias_row(11, 0, b2, 2)
            bias_row(12, 1, b2, 3)

            def qkv2_group(i, following):
                for n in range(3 * CT):
                    j = n + 3
                    if j < 3 * CT:
                        qkv2(i, j)
                    else:
                        following(j - 3 * CT)
                    if n < 2 * CT:
                        unit(ada2, 2 + n // 2 % 2, i * 16 + (UNITS * 8 + n), i * (4 * P) + n // 4 * P, n % 2)

            with sp.Fori(0, 3) as i:
                qkv2_group(i, lambda j: qkv2(i + 1, j))
            qkv2_group(3, lambda j: tile_rows(T_OUT2, j, w_o2, j // 2 * P))
            bias_row(13, 1, b2, 4)
            rows_pairs(T_OUT2, w_o2, KD // 2 - 1, 4, 4, UNITS * 10, ada2)
            last_pair_of_rows(T_OUT2, w_o2, KD,
                              lambda j: unit(ada2, 4, UNITS * 11 - 4 + j, (KD - 2 + j // 2) * P, j % 2),
                              lambda j: tile_cols(T_FF2, j, w_up2, j, 0))
            one = gate_up(T_FF2, w_up2, w_up2, FF2)
            bias_row(14, 0, b2, 5)
            for j in range(3, CT):
                tile_cols(T_FF2, j, w_up2, j, 0)
            for j in range(3):
                one(0, j)
            ff1_loop(0, 4, ada2, 5, UNITS * 11)
            ff1_loop(4, NCH - 2, None, 0, 0)
            LASTP = NCH - 2
            TT = T_FF2 + CT + LASTP * 2 * CT

            def tail(j):
                if j < CT:
                    one(LASTP, j)
                elif j < 2 * CT:
                    tile_cols(TT, j, w_up2, j - CT, (NCH - 1) * C, TAILC)
                elif j < 3 * CT:
                    tile_cols(TT, j, w_up2, j - 2 * CT, FF2 + (NCH - 1) * C, TAILC)

            for j in range(3, 3 * CT):
                tail(j)
            for j in range(3):
                tile_rows(T_DOWN2, j, w_down2, j // 2 * P)
            rows_pairs(T_DOWN2, w_down2, FF2 // P // 2 - 1)
            LP = FF2 // P // 2 - 1
            for j in range(3, 6):
                tile_rows(T_DOWN2 + 4 * LP, j, w_down2, (2 * LP + j // 2) * P)
            for t in range(NT):
                sp.wait_ge(x_ready, 3 * NT + t + 1)
                sp.dma_start(out[0, t * P:(t + 1) * P, :], x[:, t, :]).then_inc(out_landed, 16)
            sp.wait_ge(out_landed, 16 * NT)

        @block.gpsimd
        def _(pool):
            steps = [0]

            def link(ins_):
                steps[0] += 1
                ins_.then_inc(pool_step, 1)
                pool.wait_ge(pool_step, steps[0])

            link(pool.memset(ident[:, :], 0.0))
            pool.memset(eps_rms[:, :], RMS_EPS)
            pool.memset(eps_ln[:, :], LN_EPS)
            pool.memset(ones[:, :], 1.0).then_inc(const_ready, 1)
            pool.affine_select(out=ident[:, :], in_=ident[:, :], compare_op=ALU.not_equal, fill=1.0, base=0,
                               pattern=[[-1, P]], channel_multiplier=1).then_inc(const_ready, 1)
            pool.memset(mean1[:, :], 1.0 / (H1 * HD)).then_inc(const_ready, 1)
            pool.memset(u_pad[:, :, :], 0.0).then_inc(const_ready, 1)
            link(pool.memset(causal[:, :, :], 0.0))
            pool.affine_select(out=causal[:, :, :], in_=causal[:, :, :], compare_op=ALU.is_ge, fill=NEG, base=0,
                               pattern=[[P, NT], [-1, SEQ]], channel_multiplier=1).then_inc(const_ready, 1)

            link(pool.memset(tab[:, :], 0.0))
            rpb = ins["na_rpb_2"][0]
            lo_dr, lane = RPB_H // 2 - (ROWS - 1), GRID - 1 - RPB_W // 2
            for h in range(H2):
                pool.dma_start(tab[h * DR:(h + 1) * DR, lane:lane + RPB_W],
                               rpb[h, lo_dr:lo_dr + DR, :]).then_inc(table_landed, 16)
            pool.wait_ge(table_landed, 16 * H2)
            pool.dma_start(table_d, tab[:, :].unsqueeze(1).broadcast_to([H2 * DR, GRID, LANES])).then_inc(table_landed, 16)
            pool.wait_ge(table_landed, 16 * (H2 + 1))
            pool.dma_start(skew_s[:, :, :], bass.AP(table_d.tensor, GRID - 1,
                                                          [[LANES - 1, GRID], [GRID * LANES, H2 * DR], [1, GRID]]))\
                .then_inc(table_landed, 16)
            pool.wait_ge(table_landed, 16 * (H2 + 2))
            W, WH = 16, 8
            v = skew_s[:, :, 0:GRID - W]
            link(pool.affine_select(out=v, in_=v, compare_op=ALU.is_ge, fill=NEG, base=WH,
                                    pattern=[[0, H2 * DR], [1, GRID - W]], channel_multiplier=-1))
            v = skew_s[:, :, W:GRID]
            link(pool.affine_select(out=v, in_=v, compare_op=ALU.is_gt, fill=NEG, base=WH - W,
                                    pattern=[[0, H2 * DR], [-1, GRID - W]], channel_multiplier=1))
            pool.dma_start(skew_d, skew_s[:, :, :]).then_inc(table_landed, 16)
            pool.wait_ge(table_landed, 16 * (H2 + 3))
            def unit_bias(i, u):
                c = u % 2
                pool.wait_ge(max_ready, i * PER_GROUP + (UNITS1 + u - 1))
                for r in range(2):
                    src = skew_d[:, bass.ds(i * (GH * DR) + (u // 2 * DR + ROWS - 1 - 2 * c - r), ROWS), :]
                    pool.dma_start(bias_t[r * GRID:(r + 1) * GRID, c, :],
                                   src.rearrange("p a b -> p (a b)")).then_inc(bias_landed[c], 16)

            with pool.Fori(0, 4) as i:
                for u in range(PER_GROUP):
                    unit_bias(i, u)

        @block.scalar
        def _(act):
            steps = [0]

            def link(ins_):
                steps[0] += 1
                ins_.then_inc(act_step, 1)
                act.wait_ge(act_step, steps[0])

            def hi(T, j):
                s = j % RING
                act.wait_ge(raw_landed[s], T * (16 // RING) + 16 * (j // RING + 1))
                act.wait_ge(tile_used, T + j + 1)
                act.activation(w_hi[:, s, :], raw[:, s, :], ACT.Copy).then_inc(hi_ready, 1)

            def chunk_wait(T, j):
                act.wait_ge(tile_used, T + (j + RING))

            act.wait_ge(const_ready, 1)
            rows = ("c", "c_2", "c_ctx_2", "mix_pre_g", "ffn_pre_g", "norm_mix_g_2", "norm_ffn_g_2")
            for n, name in enumerate(rows):
                v = ins[name]
                v = v.rearrange("(r n) -> r n", n=P) if len(v.shape) == 1 else v.rearrange("a (r n) -> (a r) n", n=P)
                act.dma_start(st_vec[KD * n:KD * (n + 1), :], v).then_inc(vec_landed, 16)
            act.dma_start(x[:, :, :], ins["x"][0].rearrange("(t p) d -> p t d", p=P)).then_inc(x_landed, 16)
            for n, name in enumerate(("conv_b", "conv_ln_g", "conv_ln_b")):
                act.dma_start(st_c24[H1 * n:H1 * (n + 1), :], ins[name].rearrange("a (r n) -> (a r) n", n=P))\
                    .then_inc(small_landed, 16)
            act.dma_start(st_cw[:, :], ins["conv_w"][0]).then_inc(small_landed, 16)
            act.dma_start(st_fc[:, 0:3, :], ins["ffn_conv_w_2"][0].rearrange("t (r n) -> r t n", n=P)).then_inc(small_landed, 16)
            act.dma_start(st_fc[:, 3, :], ins["ffn_conv_b_2"][0].rearrange("(r n) -> r n", n=P)).then_inc(small_landed, 16)
            act.dma_start(qg[:, :], ins["na_q_g_2"][0:1, :].to_broadcast([P, HD])).then_inc(small_landed, 16)
            act.dma_start(kg[:, :], ins["na_k_g_2"][0:1, :].to_broadcast([P, HD])).then_inc(small_landed, 16)

            act.wait_ge(tr_done[0], 1)
            act.activation(cact[:, :], ps[:, 6, 0:48], ACT.Silu).then_inc(cact_ready, 1)
            act.activation(vecs[:, :], ps[:, 6, 0:112], ACT.Copy).then_inc(tr_free[0], 1)
            act.wait_ge(tr_done[1], 1)
            act.activation(cvec[:, :], ps[:, 7, 0:24 + H1 * TAPS], ACT.Copy).then_inc(tr_free[1], 1)
            act.wait_ge(tr_done[0], 2)
            act.activation(fcw[:, 0:3, :], ps[:, 6, 0:258].rearrange("p (t r) -> p t r", t=3), ACT.Copy).then_inc(tr_free[0], 1)
            act.wait_ge(tr_done[1], 2)
            act.activation(fcw[:, 3, :], ps[:, 7, 0:86], ACT.Copy).then_inc(tr_free[1], 1)
            link(act.activation(stat[:, 63:64], ones[:, 0:1], ACT.Copy))

            def row_squares(n, src, hold=None):
                if hold is not None:
                    act.wait_ge(*hold)
                act.activation(junk[:, :], src, ACT.Square, accum_out=stat[:, 56 + n % 2:57 + n % 2]).then_inc(ss_ready, 1)
                act.wait_ge(ss_ready, n + 1)
                act.activation(stat[:, 58 + n % 2:59 + n % 2], stat[:, 56 + n % 2:57 + n % 2], ACT.Sqrt,
                               scale=1.0 / D, bias=eps_rms[:, :]).then_inc(std_ready, 1)

            def h_hi_parts(n0, dst):
                for n in range(4 * NT):
                    act.wait_ge(hf_ready, n0 + n + 1)
                    t, e = n // 4, n % 4
                    act.activation(dst[:, 4 * e:4 * e + 4, t * P:(t + 1) * P],
                                   h_f[:, n % 2, :].rearrange("p (k n) -> p k n", k=4), ACT.Copy).then_inc(hhi_ready, 1)

            act.wait_ge(x_landed, 16)
            for t in range(NT):
                row_squares(t, x[:, t, :])
            for j in range(3):
                hi(T_AG, j)
            h_hi_parts(0, h_hi)
            act.wait_ge(const_ready, 5)
            with act.Fori(0, 2) as i:
                T = T_AG + i * (2 * CT)
                for n in range(2 * CT):
                    hi(T, n + 3)
                chunk_wait(T, 2 * CT)
                for t in range(NT):
                    s = act.activation(nat_a[:, t, :], ps[:, 2 + t, :], ACT.Sigmoid)
                s.then_inc(pair_free[1], 1)
                for b in range(2):
                    act.wait_ge(tr_done[b], i + (M["u"] + 1))
                    act.activation(u_pad[:, bass.ds(i * GH + 2 * b, 2), TAPS - 1:PADT],
                                   ps[:, 6 + b, :].rearrange("p (g n) -> p g n", g=2), ACT.Copy).then_inc(tr_free[b], 1)

            def attention(U, Mb, nkt, head):
                for n in range(PER_GROUP + 2):
                    if n < PER_GROUP:
                        act.wait_ge(max_ready, U + (n + 1))
                        act.activation(prob[:, n % 2, 0:nkt * P], prob[:, n % 2, 0:nkt * P], ACT.Exp,
                                       bias=stat[:, n % 2:n % 2 + 1], accum_out=stat[:, 4 + n % 2:5 + n % 2]).then_inc(exp_ready, 1)
                    if 1 <= n <= PER_GROUP:
                        u = n - 1
                        act.wait_ge(tr_done[u % 2], Mb + (u // 2 + 1))
                        act.activation(p_t[:, u % 2, 0:nkt * P], ps[:, 6 + u % 2, 0:nkt * P], ACT.Copy).then_inc(tr_free[u % 2], 1)
                    if n >= 2:
                        u = n - 2
                        act.wait_ge(o_done, U + (u + 1))
                        act.activation(ff[:, head(u // 2), u % 2 * P:(u % 2 + 1) * P],
                                       ps[:, 2 + u % 2, 0:P].unsqueeze(1), ACT.Copy).then_inc(o_used, 1)

            act.wait_ge(table_landed, 16 * (H2 + 3))
            with act.Fori(0, 2) as i:
                T = T_QKV1 + i * (3 * CT)
                Mb = i * 6 + M["qkv1"]

                def evacuate(dst, b):
                    for t in range(NT):
                        s = act.activation(dst[:, t, :], ps[:, 2 * b + t, :], ACT.Copy)
                    s.then_inc(pair_free[b], 1)

                def transposed(dst, m_):
                    for b in range(2):
                        act.wait_ge(tr_done[b], m_ + 1)
                        act.activation(dst[:, 2 * b:2 * b + 2, 0:SEQ],
                                       ps[:, 6 + b, :].rearrange("p (g n) -> p g n", g=2), ACT.Copy).then_inc(tr_free[b], 1)

                for n in range(CT):
                    hi(T, n + 3)
                chunk_wait(T, CT)
                evacuate(nat_a, 2)
                for n in range(CT, 2 * CT):
                    if n == CT + 4:
                        transposed(q_t, Mb)
                    hi(T, n + 3)
                chunk_wait(T, 2 * CT)
                evacuate(nat_b, 0)
                for n in range(2 * CT, 3 * CT):
                    if n == 2 * CT + 4:
                        transposed(k_t, Mb + 1)
                    hi(T, n + 3)
                chunk_wait(T, 3 * CT)
                evacuate(v_n, 1)
                attention(i * PER_GROUP, Mb + 2, NT, lambda h: bass.ds(i * GH + h, 1))

            act.wait_ge(dev_ready, 1)
            act.activation(tmp[:, :], ff[:, 8:16, :].rearrange("p g n -> p (g n)"), ACT.Square).then_inc(sq_ready, 1)
            act.wait_ge(tr_done[1], M["ln"] + 1)
            act.activation(rstd_ln[:, :], ps[:, 7, 0:SEQ], ACT.Sqrt, bias=eps_ln[:, :]).then_inc(tr_free[1], 1)
            act.wait_ge(o_used, UNITS1)
            act.dma_start(scr[:, :], ins["mix_post_g"][0:1, :].to_broadcast([P, D])).then_inc(post_landed, 16)
            act.wait_ge(ln_ready, 1)
            for g in range(H1):
                s = act.activation(ff[:, 8 + g, :], ff[:, 8 + g, :], ACT.Silu,
                                   scale=cvec[:, H1 + g:H1 + g + 1], bias=cvec[:, 2 * H1 + g:2 * H1 + g + 1])
            link(s)

            def stage_hi(F, k, src):
                act.activation(f_hi[:, k % 2, :], src, ACT.Copy).then_inc(fhi_ready, 1)

            def rows_phase(T0, F0, K):
                def one_k(k):
                    return ff[:, bass.ds(k, 1), :].rearrange("p o n -> p (o n)")

                act.wait_ge(tile_used, T0 + RING)
                stage_hi(F0, 0, one_k(0))
                with act.Fori(0, K // 2 - 1) as i:
                    T = T0 + i * 4
                    hi(T, 3)
                    stage_hi(F0, 1, one_k(i * 2 + 1))
                    hi(T, 4)
                    hi(T, 5)
                    stage_hi(F0, 0, one_k(i * 2 + 2))
                    hi(T, 6)
                T = T0 + 4 * (K // 2 - 1)
                hi(T, 3)
                stage_hi(F0, 1, one_k(K // 2 * 2 - 1))
                if K % 2 == 0:
                    for j in range(4, 7):
                        hi(T, j)
                else:
                    hi(T, 4)
                    hi(T, 5)
                    stage_hi(F0, 0, one_k(K - 1))

            def y_squares(n, Tend):
                act.wait_ge(tile_used, Tend + RING)
                for t in range(NT):
                    row_squares(n + t, ps[:, 4 * t:4 * t + 4, :].rearrange("p b n -> p (b n)"))

            rows_phase(T_OUT1, F_OUT1, KD)
            y_squares(2, T_FF1)

            for t in range(NT):
                row_squares(4 + t, x[:, t, :], (x_ready, t + 1))
            h_hi_parts(8, h_hi)

            def gate_act():
                for t in range(NT):
                    s = act.activation(sig[:, t, :], ps[:, t, :], ACT.Silu)
                s.then_inc(pair_free[0], 1)

            def act_transposed(i):
                for b in range(2):
                    act.wait_ge(tr_done[b], i + (M["ffn1"] + 1))
                    act.activation(ff[:, bass.ds(i * GH + 2 * b, 2), :],
                                   ps[:, 6 + b, :].rearrange("p (g n) -> p g n", g=2), ACT.Copy).then_inc(tr_free[b], 1)

            for n in range(CT):
                hi(T_FF1, n + 3)
            chunk_wait(T_FF1, CT)
            gate_act()
            with act.Fori(0, NCH - 1) as i:
                T = T_FF1 + CT + i * (2 * CT)
                for n in range(2 * CT):
                    if n == CT + 4:
                        act_transposed(i)
                    hi(T, n + 3)
                chunk_wait(T, 2 * CT)
                gate_act()
            T = T_FF1 + CT + (NCH - 1) * 2 * CT
            for n in range(CT):
                hi(T, n + 3)
            act_transposed(NCH - 1)
            act.dma_start(scr[:, :], ins["ffn_post_g"][0:1, :].to_broadcast([P, D])).then_inc(post_landed, 16)
            rows_phase(T_DOWN1, F_DOWN1, FF1 // P)
            y_squares(6, T_QKV2)

            for t in range(NT):
                row_squares(8 + t, x[:, t, :], (x_ready, NT + t + 1))
            h_hi_parts(16, h_hi)
            for t in range(NT):
                act.wait_ge(tr_done[1], M["ctx"] + 2 * t)
                act.dma_start(tmp[:, :], ins["ctx_2"][0, t * P:(t + 1) * P, :]).then_inc(ctx_landed, 16)
                row_squares(10 + t, tmp[:, :], (ctx_landed, 16 * (t + 1)))
                for n in range(4):
                    act.wait_ge(hf_ready, 24 + 4 * t + n + 1)
                    act.activation(hc_hi[:, 4 * n:4 * n + 4, t * P:(t + 1) * P],
                                   h_f[:, n % 2, :].rearrange("p (k n) -> p k n", k=4), ACT.Copy).then_inc(hhi_ready, 1)

            with act.Fori(0, 4) as i:
                T = T_QKV2 + i * (3 * CT)
                Mb = i * 7 + M["qkv2"]
                SQ = i * 3 + 1

                def squares(b, n):
                    act.wait_ge(sq_read, SQ + n)
                    act.activation(p_t[:, :, :], ps[:, 2 * b:2 * b + 2, :], ACT.Square).then_inc(sq_ready, 1)
                    act.wait_ge(head_ss, i * 3 + (n + 1))
                    act.activation(stat[:, 16:24], stat[:, 8:16], ACT.Sqrt, scale=1.0 / HD,
                                   bias=eps_rms[:, :]).then_inc(head_std, 1)

                def transposed(dst, m_, at_):
                    for b in range(2):
                        act.wait_ge(tr_done[b], m_ + 1)
                        act.activation(dst[:, 2 * b:2 * b + 2, at_:at_ + SEQ],
                                       ps[:, 6 + b, :].rearrange("p (g n) -> p g n", g=2), ACT.Copy).then_inc(tr_free[b], 1)

                for n in range(CT):
                    hi(T, n + 3)
                chunk_wait(T, CT)
                squares(2, 0)
                for n in range(CT, 2 * CT):
                    if n == CT + 4:
                        transposed(q_t, Mb, 0)
                    hi(T, n + 3)
                chunk_wait(T, 2 * CT)
                squares(0, 1)
                squares(1, 2)
                for n in range(2 * CT, 3 * CT):
                    if n == 2 * CT + 4:
                        transposed(k_t, Mb + 1, 0)
                        transposed(k_t, Mb + 2, SEQ)
                    hi(T, n + 3)
                chunk_wait(T, 3 * CT)
                for half, b in ((0, 2), (1, 0)):
                    for t in range(NT):
                        s = act.activation(v_n[:, NT * half + t, :], ps[:, 2 * b + t, :], ACT.Copy)
                    s.then_inc(pair_free[b], 1)
                attention(i * PER_GROUP + UNITS1, Mb + 3, 2 * NT, lambda h: bass.ds(i * GH + h, 1))

            act.wait_ge(o_used, UNITS1 + 32)
            rows_phase(T_OUT2, F_OUT2, KD)

            for t in range(NT):
                row_squares(12 + t, x[:, t, :], (x_ready, 2 * NT + t + 1))
            h_hi_parts(32, h_hi)

            def plain(dst, b):
                for t in range(NT):
                    s = act.activation(dst[:, t, :], ps[:, 2 * b + t, :], ACT.Copy)
                s.then_inc(pair_free[b], 1)

            def middle_tap(m_, col, groups, silu, CV):
                for b in range(2):
                    act.wait_ge(tr_done[b], m_ + 1)
                    for g in range(2 * b, min(2 * b + 2, groups)):
                        act.activation(conv_t[:, g, :], ps[:, 6 + b, g % 2 * SEQ:(g % 2 + 1) * SEQ], ACT.Identity,
                                       scale=fcw[:, 1, bass.ds(col + g, 1)],
                                       bias=fcw[:, 3, bass.ds(col + g, 1)]).then_inc(cv_ready, 1)
                if silu:
                    for b in range(2):
                        act.wait_ge(tr_free[b], m_ + 1)
                        act.activation(gate_t[:, 2 * b:min(2 * b + 2, groups), :],
                                       conv_t[:, 2 * b:min(2 * b + 2, groups), :], ACT.Silu).then_inc(sig_ready, 1)

            GC, UC = 0, FF2 // P
            for n in range(CT):
                hi(T_FF2, n + 3)
            chunk_wait(T_FF2, CT)
            plain(sig, 0)
            with act.Fori(0, NCH - 1) as i:
                T = T_FF2 + CT + i * (2 * CT)
                m_ = i * 2 + M["ffn2"]
                for n in range(CT):
                    if n == 4:
                        act.wait_ge(ff_ready, i * 2 + 1)
                        middle_tap(m_, i * GH, GH, True, 0)
                    hi(T, n + 3)
                chunk_wait(T, CT)
                plain(act_n, 1)
                for n in range(CT, 2 * CT):
                    if n == CT + 4:
                        middle_tap(m_ + 1, i * GH + UC, GH, False, 0)
                    hi(T, n + 3)
                chunk_wait(T, 2 * CT)
                plain(sig, 0)
            T = T_FF2 + CT + (NCH - 1) * 2 * CT
            m_ = M["ffn2"] + 2 * (NCH - 1)
            for n in range(CT):
                if n == 4:
                    act.wait_ge(ff_ready, 2 * (NCH - 1) + 1)
                    middle_tap(m_, GH * (NCH - 1), TAILC // P, True, 0)
                hi(T, n + 3)
            chunk_wait(T, CT)
            plain(act_n, 1)
            middle_tap(m_ + 1, GH * (NCH - 1) + UC, TAILC // P, False, 0)
            act.wait_ge(ff_ready, 2 * NCH + 1)
            rows_phase(T_DOWN2, F_DOWN2, FF2 // P)

        @block.vector
        def _(dve):
            steps = [0]

            def link(ins_, off=0):
                steps[0] += 1
                ins_.then_inc(dve_step, 1)
                dve.wait_ge(dve_step, off + steps[0])

            def lo(T, j):
                s = j % RING
                dve.wait_ge(hi_ready, T + (j + 1))
                dve.tensor_tensor(w_lo[:, s, :], raw[:, s, :], w_hi[:, s, :].bitcast(F32), ALU.subtract).then_inc(lo_ready, 1)

            def unit(n, k, half, vec, acc, then_ctx=None):
                dve.wait_ge(ada_landed[half], n * 8 + (16 - 8 * half))
                dve.wait_ge(ada_used, n + 1)
                a = acc[:, half * TILE:(half + 1) * TILE]
                ins_ = dve.scalar_tensor_tensor(out=a, in0=ada[:, half, :], scalar=cact[:, bass.ds(k + vec * KD, 1)],
                                                in1=a, op0=ALU.mult, op1=ALU.add)
                if then_ctx is not None:
                    a2 = then_ctx[:, half * TILE:(half + 1) * TILE]
                    ins_ = dve.scalar_tensor_tensor(out=a2, in0=ada[:, half, :], scalar=cact[:, bass.ds(k + 2 * KD, 1)],
                                                    in1=a2, op0=ALU.mult, op1=ALU.add)
                ins_.then_inc(ada_used, 1)

            def clear(acc):
                dve.memset(acc[:, :], 0.0).then_inc(acc_clear, 1)

            def shift_cols(M_, idx):
                for b in range(2):
                    dve.wait_ge(tr_done[b], M_ + 1)
                    dve.tensor_copy(cols[:, idx, 8 * b:8 * b + 8], ps[:, 6 + b, 0:8]).then_inc(tr_free[b], 1)

            def scale_cols(M_, idx, g):
                for b in range(2):
                    dve.wait_ge(tr_done[b], M_ + 1)
                    dve.scalar_tensor_tensor(out=cols[:, idx, 8 * b:8 * b + 8], in0=ps[:, 6 + b, 0:8], scalar=1.0,
                                             in1=vecs[:, g + 8 * b:g + 8 * b + 8], op0=ALU.add, op1=ALU.mult)\
                        .then_inc(tr_free[b], 1)

            def gate_rows(M_, post):
                for c in range(4):
                    b = c % 2
                    dve.wait_ge(tr_done[b], M_ + c // 2 + 1)
                    dst = acc0[:, c * C:(c + 1) * C]
                    if post:
                        ins_ = dve.tensor_tensor(dst, ps[:, 6 + b, :], scr[:, c * C:(c + 1) * C], ALU.mult)
                    else:
                        ins_ = dve.tensor_copy(dst, ps[:, 6 + b, :])
                    ins_.then_inc(tr_free[b], 1)

            def rows_rstd(n):
                dve.wait_ge(std_ready, n + 1)
                r = stat[:, 60 + n % 2:61 + n % 2]
                link(dve.reciprocal(r, stat[:, 58 + n % 2:59 + n % 2]))
                return r

            def normalise(n, src):
                r = rows_rstd(n)
                dve.tensor_scalar(tmp[:, :], src, r, None, ALU.mult).then_inc(xn_ready, 1)

            def modulate(n0, M_, idx, dst, t):
                for e in range(4):
                    n = n0 + e
                    b = e % 2
                    f = h_f[:, e % 2, :]
                    fv = f.rearrange("p (k n) -> p k n", k=4)
                    dve.wait_ge(tr_done[b], M_ + e // 2 + 1)
                    dve.tensor_tensor(fv, ps[:, 6 + b, :].rearrange("p (k n) -> p k n", k=4),
                                      cols[:, idx, 4 * e:4 * e + 4].unsqueeze(2).to_broadcast([P, 4, P]), ALU.mult)\
                        .then_inc(tr_free[b], 1)
                    dve.wait_ge(tr_free[b], M_ + e // 2 + 1)
                    dve.tensor_tensor(fv, fv, cols[:, idx + 1, 4 * e:4 * e + 4].unsqueeze(2).to_broadcast([P, 4, P]),
                                      ALU.add).then_inc(hf_ready, 1)
                    dve.wait_ge(hhi_ready, n + 1)
                    d = dst[:, 4 * e:4 * e + 4, t * P:(t + 1) * P]
                    s = (h_hi if dst is h_lo else hc_hi)[:, 4 * e:4 * e + 4, t * P:(t + 1) * P]
                    dve.tensor_tensor(d, fv, s.bitcast(F32), ALU.subtract).then_inc(hlo_ready, 1)

            clear(acc1)
            clear(acc0)
            dve.wait_ge(cact_ready, 1)
            normalise(0, x[:, 0, :])
            for sec, acc in ((0, acc1), (1, acc0)):
                dve.wait_ge(acc_bias[1 - sec], 16)
                with dve.Fori(0, KD) as k:
                    for half in range(2):
                        unit(k * 2 + (UNITS * sec + half), k, half, 0, acc)
            shift_cols(M["a_sh1"], 1)
            scale_cols(M["a_sc1"], 0, 48)
            dve.wait_ge(tr_free[1], M["a_sc1"] + 1)
            clear(acc0)
            for t in range(NT):
                if t:
                    dve.wait_ge(xn_ready, 1)
                    dve.wait_ge(tr_done[1], M["x1"] + 2)
                    normalise(1, x[:, 1, :])
                if t == 0:
                    for j in range(3):
                        lo(T_AG, j)
                modulate(4 * t, M["x1"] + 2 * t, 0, h_lo, t)
            dve.wait_ge(acc_bias[0], 32)
            with dve.Fori(0, 2) as i:
                T = T_AG + i * (2 * CT)
                for n in range(2 * CT):
                    lo(T, n + 3)
                    unit(i * (2 * CT) + (UNITS * 2 + n), i * (KD // 2) + n // 2, n % 2, 0, acc0)
                dve.wait_ge(pair_free[1], i + 2)
                for t in range(NT):
                    s = dve.tensor_tensor(nat_b[:, t, :], ps[:, t, :], nat_a[:, t, :], ALU.mult)
                s.then_inc(pair_free[0], 1)
            clear(acc1)

            def softmax(U, nkt, bias, landed):
                for n in range(PER_GROUP + 1):
                    if n < PER_GROUP:
                        b = n % 2
                        dve.wait_ge(s_done, U + (n + 1))
                        if landed is not None:
                            dve.wait_ge(bias_landed[b], landed + 32 * (n // 2 + 1))
                        pr = prob[:, b, 0:nkt * P]
                        if nkt > NT:
                            dve.tensor_scalar(prob[:, b, SEQ:2 * SEQ], ps[:, b, SEQ:2 * SEQ], SCALE, None, ALU.mult)
                        link(dve.scalar_tensor_tensor(out=prob[:, b, 0:SEQ], in0=ps[:, b, 0:SEQ], scalar=SCALE,
                                                      in1=bias[:, b, :], op0=ALU.mult, op1=ALU.add), off[0])
                        link(dve.tensor_reduce(stat[:, 2 + b:3 + b], pr, AX, ALU.max), off[0])
                        dve.tensor_scalar(stat[:, b:b + 1], stat[:, 2 + b:3 + b], -1.0, None, ALU.mult).then_inc(max_ready, 1)
                    if n >= 1:
                        b = (n - 1) % 2
                        dve.wait_ge(exp_ready, U + n)
                        link(dve.reciprocal(stat[:, 6 + b:7 + b], stat[:, 4 + b:5 + b]), off[0])
                        pr = prob[:, b, 0:nkt * P]
                        dve.tensor_scalar(pr, pr, stat[:, 6 + b:7 + b], None, ALU.mult).then_inc(p_ready, 1)

            off = [0]
            TAP_OPS = GH * TAPS
            dve.wait_ge(const_ready, 5)
            dve.wait_ge(acc_bias[1], 32)
            for i in range(2):
                T = T_QKV1 + i * (3 * CT)
                for b in range(2):
                    dve.wait_ge(tr_free[b], i + (M["u"] + 1))
                for n in range(3 * CT):
                    lo(T, n + 3)
                    if n < 2 * CT:
                        unit(i * (2 * CT) + (UNITS * 3 + n), i * (KD // 2) + n // 2, n % 2, 0, acc1)
                    for o in range(TAP_OPS * n // (3 * CT), TAP_OPS * (n + 1) // (3 * CT)):
                        tap, g = o // GH, o % GH
                        dst = ff[:, bass.ds(i * GH + (H1 + g), 1), :].rearrange("p o n -> p (o n)")
                        src = u_pad[:, bass.ds(i * GH + g, 1), tap:tap + SEQ].rearrange("p o n -> p (o n)")
                        wv = cvec[:, bass.ds(i * (GH * TAPS) + (3 * H1 + g * TAPS + tap), 1)]
                        if tap == 0:
                            s = dve.tensor_scalar(dst, src, wv, cvec[:, bass.ds(i * GH + g, 1)], ALU.mult, ALU.add)
                        else:
                            dve.wait_ge(conv_step, i * TAP_OPS + (o - GH + 1))
                            s = dve.scalar_tensor_tensor(out=dst, in0=src, scalar=wv, in1=dst, op0=ALU.mult, op1=ALU.add)
                        s.then_inc(conv_step, 1)
                softmax(i * PER_GROUP, NT, causal, None)

            dve.wait_ge(tr_done[0], M["ln"] + 1)
            dve.wait_ge(conv_step, 2 * TAP_OPS)
            cv = ff[:, H1:2 * H1, :]
            dve.tensor_tensor(cv, cv, ps[:, 6, 0:SEQ].unsqueeze(1).to_broadcast([P, H1, SEQ]), ALU.subtract)\
                .then_inc(dev_ready, 1)
            dve.wait_ge(dev_ready, 1)
            dve.tensor_copy(stat[:, 62:63], ps[:, 6, 0:1]).then_inc(tr_free[0], 1)
            dve.wait_ge(tr_free[1], M["ln"] + 1)
            link(dve.reciprocal(rstd_ln[:, :], rstd_ln[:, :]))
            dve.tensor_tensor(cv, cv, rstd_ln[:, :].unsqueeze(1).to_broadcast([P, H1, SEQ]), ALU.mult).then_inc(ln_ready, 1)

            dve.wait_ge(post_landed, 16)
            gate_rows(M["a_g1"], True)
            shift_cols(M["a_sh2"], 3)
            clear(acc1)
            dve.wait_ge(acc_bias[1], 48)

            def stage_lo(F, k, src):
                dve.wait_ge(fhi_ready, F + 1)
                dve.tensor_tensor(f_lo[:, k % 2, :], src, f_hi[:, k % 2, :].bitcast(F32), ALU.subtract).then_inc(flo_ready, 1)

            def rows_pair(T, F, k0, units, last=False):
                def one_k(k):
                    return ff[:, bass.ds(k, 1), :].rearrange("p o n -> p (o n)")

                lo(T, 3)
                units(0)
                stage_lo(F + 1, 1, one_k(k0 + 1))
                lo(T, 4)
                units(1)
                lo(T, 5)
                units(2)
                if not last:
                    stage_lo(F + 2, 0, one_k(k0 + 2))
                lo(T, 6)
                units(3)

            def rows_first(F0):
                stage_lo(F0, 0, ff[:, 0, :])

            none = lambda j: None
            rows_first(F_OUT1)
            with dve.Fori(0, KD // 2 - 1) as i:
                rows_pair(T_OUT1 + i * 4, F_OUT1 + i * 2, i * 2,
                          lambda j: unit(i * 4 + (UNITS * 4 + j), i * 2 + j // 2, j % 2, 0, acc1))
            i = KD // 2 - 1
            rows_pair(T_OUT1 + 4 * i, F_OUT1 + 2 * i, 2 * i,
                      lambda j: unit(4 * i + UNITS * 4 + j, 2 * i + j // 2, j % 2, 0, acc1), last=True)

            def update(done, norm, n=0):
                for t in range(NT):
                    y = ps[:, 4 * t:4 * t + 4, :].rearrange("p b n -> p (b n)")
                    if t:
                        dve.wait_ge(x_ready, done + t)
                    if norm:
                        r = rows_rstd(n + t)
                        link(dve.scalar_tensor_tensor(out=scr[:, :], in0=y, scalar=r, in1=acc0[:, :],
                                                      op0=ALU.mult, op1=ALU.mult))
                    else:
                        link(dve.tensor_tensor(scr[:, :], y, acc0[:, :], ALU.mult))
                    xt = x[:, t, :]
                    dve.tensor_tensor(xt, xt, scr[:, :], ALU.add).then_inc(x_ready, 1)

            update(0, True, 2)
            dve.wait_ge(x_ready, NT)
            scale_cols(M["a_sc2"], 2, 64)

            def new_h(n, M_, idx, hf0, xr):
                for t in range(NT):
                    if t:
                        dve.wait_ge(tr_done[1], M_ + 2)
                    normalise(n + t, x[:, t, :])
                    modulate(hf0 + 4 * t, M_ + 2 * t, idx, h_lo, t)

            new_h(4, M["x2"], 2, 8, 0)

            def gate_up_1(start, end, units):
                with dve.Fori(start, end) as i:
                    T = T_FF1 + CT + i * (2 * CT)
                    for n in range(CT):
                        lo(T, n + 3)
                        units(i, n)
                    up_act(i)
                    for n in range(CT, 2 * CT):
                        lo(T, n + 3)
                        units(i, n)

            def up_act(i):
                dve.wait_ge(tile_used, T_FF1 + 2 * CT + RING + i * (2 * CT))
                dve.wait_ge(pair_free[0], i + (USE0["gate1"] + 2))
                for t in range(NT):
                    s = dve.tensor_tensor(act_n[:, t, :], ps[:, 2 + t, :], sig[:, t, :], ALU.mult)
                s.then_inc(pair_free[1], 1)

            clear(acc0)
            for n in range(CT):
                lo(T_FF1, n + 3)
            dve.wait_ge(acc_bias[0], 48)

            def u_g2(i, n):
                if n % 2 == 0:
                    u = n // 2
                    unit(i * 8 + (UNITS * 5 + u), i * 4 + u // 2, u % 2, 0, acc0)

            gate_up_1(0, 4, u_g2)
            clear(acc1)
            clear(tmp)
            dve.wait_ge(acc_bias[1], 64)
            dve.wait_ge(acc_bias[2], 16)

            def u_sh1(i, n):
                if n % 2 == 0:
                    u = n // 2
                    unit(i * 8 + (UNITS * 6 + u - 32), i * 4 + (u // 2 - 16), u % 2, 1, acc1, tmp)

            gate_up_1(4, 8, u_sh1)
            gate_up_1(8, NCH - 1, lambda i, n: None)
            T = T_FF1 + CT + (NCH - 1) * 2 * CT
            for n in range(CT):
                lo(T, n + 3)
            up_act(NCH - 1)
            dve.wait_ge(post_landed, 32)
            gate_rows(M["a_g2"], True)
            shift_cols(M["b_sh1"], 5)
            shift_cols(M["b_sh1"] + 1, 7)
            clear(acc1)
            clear(tmp)
            dve.wait_ge(acc_bias[1], 80)
            dve.wait_ge(acc_bias[2], 32)

            rows_first(F_DOWN1)
            with dve.Fori(0, 16) as i:
                rows_pair(T_DOWN1 + i * 4, F_DOWN1 + i * 2, i * 2,
                          lambda j: unit(i * 2 + (UNITS * 7 + j), i, j, 1, acc1, tmp) if j < 2 else None)
            with dve.Fori(16, FF1 // P // 2 - 1) as i:
                rows_pair(T_DOWN1 + i * 4, F_DOWN1 + i * 2, i * 2, none)
            i = FF1 // P // 2 - 1
            rows_pair(T_DOWN1 + 4 * i, F_DOWN1 + 2 * i, 2 * i, none, last=True)
            update(NT, True, 6)
            dve.wait_ge(x_ready, 2 * NT)
            clear(acc0)
            scale_cols(M["b_sc1"], 4, 80)
            scale_cols(M["b_sc1"] + 1, 6, 80)
            dve.wait_ge(tr_free[1], M["b_sc1"] + 1)
            clear(acc1)

            dve.wait_ge(tr_free[1], M["b_sc1"] + 2)
            new_h(8, M["lat"], 4, 16, 0)
            for t in range(NT):
                dve.wait_ge(ctx_landed, 16 * (t + 1))
                normalise(10 + t, tmp[:, :])
                modulate(24 + 4 * t, M["ctx"] + 2 * t, 6, hc_lo, t)
            dve.wait_ge(acc_bias[0], 64)
            dve.wait_ge(acc_bias[1], 96)
            dve.tensor_copy(stat[:, 62:63], stat[:, 63:64]).then_inc(sq_read, 1)
            with dve.Fori(0, 4) as i:
                T = T_QKV2 + i * (3 * CT)
                S = 3 + 3 * PER_GROUP
                off[0] = i * S
                before = steps[0]

                def head_norm(dst, b, n, g):
                    dve.wait_ge(sq_ready, i * 3 + (n + 2))
                    ss = stat[:, 8:16]
                    dve.tensor_reduce(ss, p_t[:, :, :].rearrange("p t (h n) -> p (t h) n", n=HD), AX, ALU.add)\
                        .then_inc(head_ss, 1)
                    dve.wait_ge(head_std, i * 3 + (n + 1))
                    link(dve.reciprocal(stat[:, 24:32], stat[:, 16:24]), off[0])
                    for t in range(NT):
                        for h in range(GH):
                            c = t * GH + h
                            s = dve.scalar_tensor_tensor(out=dst[:, t, h * HD:(h + 1) * HD],
                                                         in0=ps[:, 2 * b + t, h * HD:(h + 1) * HD],
                                                         scalar=stat[:, 24 + c:25 + c], in1=g[:, :],
                                                         op0=ALU.mult, op1=ALU.mult)
                            if c == 0:
                                s.then_inc(sq_read, 1)
                    s.then_inc(pair_free[b], 1)

                def steps_of(n0):
                    for n in range(n0, n0 + CT):
                        lo(T, n + 3)
                        if n < 2 * CT:
                            which = n // 2 % 2
                            unit(i * 16 + (UNITS * 8 + n), i * 4 + n // 4, n % 2, 1, (acc0, acc1)[which])

                steps_of(0)
                head_norm(nat_a, 2, 0, qg)
                steps_of(CT)
                head_norm(nat_b, 0, 1, kg)
                dve.wait_ge(tr_done[1], i * 7 + (M["qkv2"] + 1))
                head_norm(nat_a, 1, 2, kg)
                steps_of(2 * CT)
                softmax(i * PER_GROUP + UNITS1, 2 * NT, bias_t, i * (32 * GH))
                assert steps[0] - before == S
            steps[0] += 3 * S
            off[0] = 0
            gate_rows(M["b_g1"], False)
            shift_cols(M["b_sh2"], 9)
            clear(acc1)
            dve.wait_ge(acc_bias[1], 112)
            rows_first(F_OUT2)
            with dve.Fori(0, KD // 2 - 1) as i:
                rows_pair(T_OUT2 + i * 4, F_OUT2 + i * 2, i * 2,
                          lambda j: unit(i * 4 + (UNITS * 10 + j), i * 2 + j // 2, j % 2, 1, acc1))
            i = KD // 2 - 1
            rows_pair(T_OUT2 + 4 * i, F_OUT2 + 2 * i, 2 * i,
                      lambda j: unit(4 * i + UNITS * 10 + j, 2 * i + j // 2, j % 2, 1, acc1), last=True)
            dve.wait_ge(tile_used, T_FF2 + RING)
            update(2 * NT, False)
            dve.wait_ge(x_ready, 3 * NT)
            scale_cols(M["b_sc2"], 8, 96)
            new_h(12, M["x7"], 8, 32, 0)

            clear(acc0)
            for n in range(CT):
                lo(T_FF2, n + 3)
            dve.wait_ge(acc_bias[0], 80)
            dve.tensor_copy(stat[:, 62:63], stat[:, 63:64]).then_inc(ff_ready, 1)

            def outer_taps(m_, col, groups, CV):
                for b in range(2):
                    gs = range(2 * b, min(2 * b + 2, groups))
                    dve.wait_ge(cv_ready, CV + gs[-1] + 1)
                    for g in gs:
                        z = ps[:, 6 + b, g % 2 * SEQ:(g % 2 + 1) * SEQ]
                        y = conv_t[:, g, 1:SEQ]
                        s = dve.scalar_tensor_tensor(out=y, in0=z[:, 0:SEQ - 1], scalar=fcw[:, 0, bass.ds(col + g, 1)],
                                                     in1=y, op0=ALU.mult, op1=ALU.add)
                    link(s, off[0])
                    for g in gs:
                        z = ps[:, 6 + b, g % 2 * SEQ:(g % 2 + 1) * SEQ]
                        y = conv_t[:, g, 0:SEQ - 1]
                        s = dve.scalar_tensor_tensor(out=y, in0=z[:, 1:SEQ], scalar=fcw[:, 2, bass.ds(col + g, 1)],
                                                     in1=y, op0=ALU.mult, op1=ALU.add)
                    s.then_inc(tr_free[b], 1)

            def times_gate(m_, i, groups):
                for b in range(2):
                    n = min(2, groups - 2 * b)
                    dve.wait_ge(tr_free[b], m_ + 1)
                    dve.wait_ge(sig_ready, i * 2 + (b + 1))
                    dve.tensor_tensor(ff[:, bass.ds(i * GH + 2 * b, n), :], conv_t[:, 2 * b:2 * b + n, :],
                                      gate_t[:, 2 * b:2 * b + n, :], ALU.mult).then_inc(ff_ready, 1)

            def gate_up_2(start, end, units):
                S = 4
                with dve.Fori(start, end) as i:
                    off[0] = (i - start) * S
                    before = steps[0]
                    T = T_FF2 + CT + i * (2 * CT)
                    m_ = i * 2 + M["ffn2"]
                    for n in range(CT):
                        if n == 4:
                            outer_taps(m_, i * GH, GH, i * (2 * GH))
                        lo(T, n + 3)
                        units(i, n)
                    for n in range(CT, 2 * CT):
                        if n == CT + 4:
                            outer_taps(m_ + 1, i * GH + FF2 // P, GH, i * (2 * GH) + GH)
                            times_gate(m_ + 1, i, GH)
                        lo(T, n + 3)
                        units(i, n)
                    assert steps[0] - before == S
                steps[0] += (end - start - 1) * S
                off[0] = 0

            def u_g2b(i, n):
                if n % 2 == 0:
                    u = n // 2
                    unit(i * 8 + (UNITS * 11 + u), i * 4 + u // 2, u % 2, 1, acc0)

            gate_up_2(0, 4, u_g2b)
            gate_up_2(4, NCH - 1, lambda i, n: None)
            i = NCH - 1
            T = T_FF2 + CT + i * 2 * CT
            m_ = M["ffn2"] + 2 * i
            for n in range(CT):
                if n == 4:
                    outer_taps(m_, i * GH, TAILC // P, i * 2 * GH)
                lo(T, n + 3)
            outer_taps(m_ + 1, i * GH + FF2 // P, TAILC // P, i * 2 * GH + TAILC // P)
            times_gate(m_ + 1, i, TAILC // P)
            gate_rows(M["b_g2"], False)
            K = FF2 // P
            dve.wait_ge(ff_ready, 2 * NCH + 1)
            rows_first(F_DOWN2)
            with dve.Fori(0, K // 2 - 1) as i:
                rows_pair(T_DOWN2 + i * 4, F_DOWN2 + i * 2, i * 2, none)
            i = K // 2 - 1
            lo(T_DOWN2 + 4 * i, 3)
            stage_lo(F_DOWN2 + 2 * i + 1, 1, ff[:, 2 * i + 1, :])
            lo(T_DOWN2 + 4 * i, 4)
            lo(T_DOWN2 + 4 * i, 5)
            stage_lo(F_DOWN2 + 2 * i + 2, 0, ff[:, 2 * i + 2, :])
            dve.wait_ge(tile_used, T_END + RING)
            update(3 * NT, False)

        @block.tensor
        def _(pe):
            pe.sem_inc(lo_ready, RING)
            pe.sem_inc(tile_used, RING)
            pe.sem_inc(ada_used, 2)
            for s in pair_free:
                pe.sem_inc(s, 1)

            def bank_free(b, m_):
                if not (isinstance(m_, int) and m_ == 0):
                    pe.wait_ge(tr_free[b], m_)

            def chunk(T, j0, targets, width=C, middle=None):
                for j in range(CT):
                    if j == 4 and middle is not None:
                        middle()
                    s = (j0 + j) % RING
                    pe.wait_ge(lo_ready, T + (j0 + j + 1 + RING))
                    for (hi_, lo_, pair, use) in targets:
                        if j == 0:
                            pe.wait_ge(pair_free[pair], use + 1)
                        for kk in range(2):
                            k = 2 * j + kk
                            wh = w_hi[:, s, kk * width:(kk + 1) * width]
                            wl = w_lo[:, s, kk * width:(kk + 1) * width]
                            for t in range(NT):
                                o = ps[:, 2 * pair + t, 0:width]
                                a = slice(t * P, (t + 1) * P)
                                pe.matmul(o, hi_[:, k, a], wh, start=(k == 0), stop=False)
                                pe.matmul(o, hi_[:, k, a], wl, start=False, stop=False)
                                mm = pe.matmul(o, lo_[:, k, a], wh, start=False, stop=(k == KD - 1))
                    mm.then_inc(tile_used, 1)

            def to_columns(src, m_, groups=GH):
                for b in range(2):
                    bank_free(b, m_)
                    for g in range(2 * b, min(2 * b + 2, groups)):
                        for t in range(NT):
                            mm = pe.transpose(ps[:, 6 + b, (g % 2 * NT + t) * P:(g % 2 * NT + t + 1) * P],
                                              src[:, t, g * P:(g + 1) * P], ident[:, :])
                    mm.then_inc(tr_done[b], 1)

            def sum_columns(acc, m_):
                for b in range(2):
                    bank_free(b, m_)
                    for k in range(8):
                        kk = 8 * b + k
                        mm = pe.matmul(ps[:, 6 + b, k:k + 1], acc[:, kk * P:(kk + 1) * P], ones[:, 0:1],
                                       start=True, stop=True)
                    mm.then_inc(tr_done[b], 1)

            def sum_rows(m_):
                for c in range(4):
                    b = c % 2
                    bank_free(b, m_ + c // 2)
                    pe.matmul(ps[:, 6 + b, :], ones[:, :], acc0[:, c * C:(c + 1) * C], start=True, stop=True)\
                        .then_inc(tr_done[b], 1)

            def transpose_rows(m_, xn):
                pe.wait_ge(xn_ready, xn)
                for e in range(4):
                    b = e % 2
                    bank_free(b, m_ + e // 2)
                    for k in range(4):
                        kk = 4 * e + k
                        mm = pe.transpose(ps[:, 6 + b, k * P:(k + 1) * P], tmp[:, kk * P:(kk + 1) * P], ident[:, :])
                    mm.then_inc(tr_done[b], 1)

            lat = (h_hi, h_lo)
            con = (hc_hi, hc_lo)

            pe.wait_ge(const_ready, 2)
            pe.wait_ge(vec_landed, 16 * 7)
            pe.transpose(ps[:, 6, 0:112], st_vec[:, :], ident[0:112, 0:112]).then_inc(tr_done[0], 1)
            pe.wait_ge(small_landed, 16 * 8)
            pe.transpose(ps[:, 7, 0:24], st_c24[:, :], ident[0:24, 0:24])
            for g in range(H1):
                mm = pe.transpose(ps[:, 7, 24 + g * TAPS:24 + (g + 1) * TAPS], st_cw[:, g * P:(g + 1) * P],
                                  ident[0:TAPS, 0:TAPS])
            mm.then_inc(tr_done[1], 1)
            bank_free(0, 1)
            for t in range(3):
                mm = pe.transpose(ps[:, 6, t * 86:(t + 1) * 86], st_fc[:, t, :], ident[0:86, 0:86])
            mm.then_inc(tr_done[0], 1)
            bank_free(1, 1)
            pe.transpose(ps[:, 7, 0:86], st_fc[:, 3, :], ident[0:86, 0:86]).then_inc(tr_done[1], 1)

            pe.wait_ge(ada_used, 2 + UNITS)
            sum_columns(acc1, M["a_sh1"])
            pe.wait_ge(ada_used, 2 + 2 * UNITS)
            sum_columns(acc0, M["a_sc1"])
            for t in range(NT):
                transpose_rows(M["x1"] + 2 * t, t + 1)
            pe.wait_ge(hlo_ready, 8)
            with pe.Fori(0, 2) as i:
                T = T_AG + i * (2 * CT)
                chunk(T, 0, [(*lat, 0, i + USE0["ag"])])
                chunk(T, CT, [(*lat, 1, i + USE1["ag"])])
                pe.wait_ge(pair_free[0], i + 2)
                to_columns(nat_b, i + M["u"])

            def attention(U, Mb, nkt, first):
                for n in range(PER_GROUP + 2):
                    if n < PER_GROUP:
                        h, c = n // 2, n % 2
                        if n == 0:
                            for b in range(2):
                                pe.wait_ge(tr_free[b], Mb)
                            first()
                        pe.matmul(ps[:, n % 2, 0:nkt * P], q_t[:, h, c * P:(c + 1) * P], k_t[:, h, 0:nkt * P],
                                  start=True, stop=True).then_inc(s_done, 1)
                    if 1 <= n <= PER_GROUP:
                        u = n - 1
                        pe.wait_ge(p_ready, U + n)
                        bank_free(u % 2, Mb + u // 2)
                        for k in range(nkt):
                            mm = pe.transpose(ps[:, 6 + u % 2, k * P:(k + 1) * P], prob[:, u % 2, k * P:(k + 1) * P],
                                              ident[:, :])
                        mm.then_inc(tr_done[u % 2], 1)
                    if n >= 2:
                        u = n - 2
                        pe.wait_ge(tr_free[u % 2], Mb + (u // 2 + 1))
                        if u >= 2:
                            pe.wait_ge(o_used, U + (u - 1))
                        for k in range(nkt):
                            mm = pe.matmul(ps[:, 2 + u % 2, 0:P], v_n[:, k, u // 2 * HD:(u // 2 + 1) * HD],
                                           p_t[:, u % 2, k * P:(k + 1) * P], start=(k == 0), stop=(k == nkt - 1))
                        mm.then_inc(o_done, 1)
                pe.wait_ge(o_used, U + PER_GROUP)

            with pe.Fori(0, 2) as i:
                T = T_QKV1 + i * (3 * CT)
                Mb = i * 6 + M["qkv1"]
                chunk(T, 0, [(*lat, 2, i + USE2["q1"])])

                def q_columns():
                    pe.wait_ge(pair_free[2], i + (USE2["q1"] + 2))
                    to_columns(nat_a, Mb)

                def k_columns():
                    pe.wait_ge(pair_free[0], i + (USE0["k1"] + 2))
                    to_columns(nat_b, Mb + 1)

                def v_written():
                    pe.wait_ge(pair_free[1], i + (USE1["v1"] + 2))

                chunk(T, CT, [(*lat, 0, i + USE0["k1"])], middle=q_columns)
                chunk(T, 2 * CT, [(*lat, 1, i + USE1["v1"])], middle=k_columns)
                attention(i * PER_GROUP, Mb + 2, NT, v_written)

            pe.wait_ge(conv_step, 2 * GH * TAPS)
            bank_free(0, M["ln"])
            for g in range(H1):
                mm = pe.matmul(ps[:, 6, 0:SEQ], mean1[:, :], ff[:, H1 + g, :], start=(g == 0), stop=(g == H1 - 1))
            mm.then_inc(tr_done[0], 1)
            pe.wait_ge(sq_ready, 1)
            bank_free(1, M["ln"])
            for g in range(H1):
                mm = pe.matmul(ps[:, 7, 0:SEQ], mean1[:, :], tmp[:, g * SEQ:(g + 1) * SEQ], start=(g == 0), stop=(g == H1 - 1))
            mm.then_inc(tr_done[1], 1)
            pe.wait_ge(ada_used, 2 + 4 * UNITS)
            sum_rows(M["a_g1"])
            sum_columns(acc1, M["a_sh2"])

            def row_tile(T, k, F, first, last):
                pe.wait_ge(flo_ready, F + 1)
                for half in range(2):
                    s = (2 * k + half) % RING
                    pe.wait_ge(lo_ready, T + (half + 1 + RING))
                    for t in range(NT):
                        a = slice(t * P, (t + 1) * P)
                        for c in range(2):
                            o = ps[:, 4 * t + 2 * half + c, :]
                            wh, wl = w_hi[:, s, c * C:(c + 1) * C], w_lo[:, s, c * C:(c + 1) * C]
                            pe.matmul(o, f_hi[:, k % 2, a], wh, start=first, stop=False)
                            pe.matmul(o, f_hi[:, k % 2, a], wl, start=False, stop=False)
                            mm = pe.matmul(o, f_lo[:, k % 2, a], wh, start=False, stop=last)
                    mm.then_inc(tile_used, 1)

            def rows_phase(T0, F0, K, m_, uses):
                for b in range(2):
                    pe.wait_ge(tr_free[b], m_)
                for p_, u in enumerate(uses):
                    pe.wait_ge(pair_free[p_], u + 1)
                row_tile(T0, 0, F0, True, False)
                row_tile(T0 + 2, 1, F0 + 1, False, False)
                with pe.Fori(1, (K - 1) // 2) as i:
                    for k in range(2):
                        row_tile(T0 + 2 * k + i * 4, k, F0 + k + i * 2, False, False)
                for k in range((K - 1) // 2 * 2, K):
                    row_tile(T0 + 2 * k, k, F0 + k, False, k == K - 1)

            rows_phase(T_OUT1, F_OUT1, KD, M["a_sc2"], (4, 4, 2))

            pe.wait_ge(x_ready, NT)
            sum_columns(acc1, M["a_sc2"])
            for t in range(NT):
                transpose_rows(M["x2"] + 2 * t, NT + t + 1)
            pe.wait_ge(hlo_ready, 16)
            chunk(T_FF1, 0, [(*lat, 0, USE0["gate1"])])
            with pe.Fori(0, NCH - 1) as i:
                T = T_FF1 + CT + i * (2 * CT)

                def act_columns():
                    pe.wait_ge(pair_free[1], i + (USE1["up1"] + 2))
                    to_columns(act_n, i + M["ffn1"])

                chunk(T, 0, [(*lat, 1, i + USE1["up1"])])
                chunk(T, CT, [(*lat, 0, i + (USE0["gate1"] + 1))], middle=act_columns)
            chunk(T_FF1 + CT + (NCH - 1) * 2 * CT, 0, [(*lat, 1, USE1["up1"] + NCH - 1)])
            pe.wait_ge(pair_free[1], USE1["up1"] + NCH + 1)
            to_columns(act_n, M["ffn1"] + NCH - 1)
            sum_rows(M["a_g2"])
            sum_columns(acc1, M["b_sh1"])
            sum_columns(tmp, M["b_sh1"] + 1)
            rows_phase(T_DOWN1, F_DOWN1, FF1 // P, M["b_sc1"], (USE0["gate1"] + NCH, USE1["up1"] + NCH, 2))

            pe.wait_ge(x_ready, 2 * NT)
            sum_columns(acc1, M["b_sc1"])
            sum_columns(tmp, M["b_sc1"] + 1)
            for t in range(NT):
                transpose_rows(M["lat"] + 2 * t, 2 * NT + t + 1)
            for t in range(NT):
                transpose_rows(M["ctx"] + 2 * t, 3 * NT + t + 1)
            pe.wait_ge(hlo_ready, 32)
            with pe.Fori(0, 4) as i:
                T = T_QKV2 + i * (3 * CT)
                Mb = i * 7 + M["qkv2"]

                def q_columns():
                    pe.wait_ge(pair_free[2], i * 2 + (USE2["qkv2"] + 2))
                    to_columns(nat_a, Mb)

                def k_columns():
                    pe.wait_ge(pair_free[0], i * 2 + (USE0["qkv2"] + 2))
                    to_columns(nat_b, Mb + 1)
                    pe.wait_ge(pair_free[1], i + (USE1["kc2"] + 2))
                    to_columns(nat_a, Mb + 2)

                def v_written():
                    pe.wait_ge(pair_free[2], i * 2 + (USE2["qkv2"] + 3))
                    pe.wait_ge(pair_free[0], i * 2 + (USE0["qkv2"] + 3))

                chunk(T, 0, [(*lat, 2, i * 2 + USE2["qkv2"])])
                chunk(T, CT, [(*lat, 0, i * 2 + USE0["qkv2"]), (*con, 1, i + USE1["kc2"])], middle=q_columns)
                chunk(T, 2 * CT, [(*lat, 2, i * 2 + (USE2["qkv2"] + 1)), (*con, 0, i * 2 + (USE0["qkv2"] + 1))],
                      middle=k_columns)
                attention(i * PER_GROUP + UNITS1, Mb + 3, 2 * NT, v_written)
            sum_rows(M["b_g1"])
            sum_columns(acc1, M["b_sh2"])
            rows_phase(T_OUT2, F_OUT2, KD, M["b_sc2"], (USE0["gate2"], USE1["up2"], USE2["qkv2"] + 8))

            pe.wait_ge(x_ready, 3 * NT)
            sum_columns(acc1, M["b_sc2"])
            for t in range(NT):
                transpose_rows(M["x7"] + 2 * t, 4 * NT + t + 1)
            pe.wait_ge(hlo_ready, 40)
            chunk(T_FF2, 0, [(*lat, 0, USE0["gate2"])])

            def gate_columns(i, groups=GH):
                pe.wait_ge(pair_free[0], i + (USE0["gate2"] + 2))
                to_columns(sig, i * 2 + M["ffn2"], groups)

            def up_columns(i, groups=GH):
                pe.wait_ge(pair_free[1], i + (USE1["up2"] + 2))
                to_columns(act_n, i * 2 + (M["ffn2"] + 1), groups)

            with pe.Fori(0, NCH - 2) as i:
                T = T_FF2 + CT + i * (2 * CT)
                chunk(T, 0, [(*lat, 1, i + USE1["up2"])], middle=lambda: gate_columns(i))
                chunk(T, CT, [(*lat, 0, i + (USE0["gate2"] + 1))], middle=lambda: up_columns(i))
            i = NCH - 2
            T = T_FF2 + CT + i * 2 * CT
            chunk(T, 0, [(*lat, 1, i + USE1["up2"])], middle=lambda: gate_columns(i))
            chunk(T, CT, [(*lat, 0, i + USE0["gate2"] + 1)], TAILC, middle=lambda: up_columns(i))
            chunk(T + 2 * CT, 0, [(*lat, 1, i + 1 + USE1["up2"])], TAILC, middle=lambda: gate_columns(i + 1, TAILC // P))
            up_columns(NCH - 1, TAILC // P)
            sum_rows(M["b_g2"])
            rows_phase(T_DOWN2, F_DOWN2, FF2 // P, M["b_g2"] + 2,
                       (USE0["gate2"] + NCH, USE1["up2"] + NCH, USE2["qkv2"] + 8))


_INS = ["x", "c", "ada_w", "ada_b", "mix_pre_g", "mix_post_g", "w_in", "conv_w", "conv_b", "conv_ln_g", "conv_ln_b",
        "w_out", "ffn_pre_g", "ffn_post_g", "w_gate", "w_up", "w_down", "c_2", "ctx_2", "c_ctx_2", "norm_mix_g_2",
        "norm_ffn_g_2", "w_ada_2", "b_ada_2", "na_w_qkv_2", "na_q_g_2", "na_k_g_2", "na_rpb_2", "na_w_o_2",
        "ffn_w_up_2", "ffn_conv_w_2", "ffn_conv_b_2", "ffn_w_down_2"]


def kernel(**inputs):
    import numpy as np
    import concourse.bacc as bacc
    from concourse.bass_utils import run_bass_kernel_spmd

    nc = bacc.Bacc("TRN2", target_bir_lowering=False, num_devices=1)
    arrays, ins = {}, {}
    for name in _INS:
        a = np.ascontiguousarray(inputs[name])
        arrays[f"in_{name}"] = a
        ins[name] = nc.dram_tensor(f"in_{name}", a.shape, mybir.dt.from_np(a.dtype), kind="ExternalInput").ap()
    out = nc.dram_tensor("out", (1, SEQ, D), F32, kind="ExternalOutput").ap()
    program(nc, ins, out)
    r = run_bass_kernel_spmd(nc, [arrays], core_ids=[0])
    return r.results[0]["out"]
```

```python
from contextlib import ExitStack

import concourse.bass as bass
from concourse import mybir

F32 = mybir.dt.float32
F32R = mybir.dt.float32r
ALU = mybir.AluOpType
ACT = mybir.ActivationFunctionType
AX = mybir.AxisListType.X

P = 128
D = 2048
KD = D // P
SEQ = 256
NT = SEQ // P
HD = 128
C = 512
GH = C // HD
TILE = 1024
RING = 4
CT = KD * C // TILE
H1 = 8
TAPS = 31
FF1 = 5632
FF2 = 5504
NCH = FF1 // C
TAILC = FF2 - (NCH - 1) * C
H2 = 16
GRID = 64
ROWS = SEQ // GRID
RPB_H, RPB_W = 15, 31
DR = 2 * ROWS - 1
LANES = 2 * GRID
NEG = -1e30
SCALE = float(HD) ** -0.5
RMS_EPS = 1e-6
LN_EPS = 1e-5

T_AG = 0
T_QKV1 = T_AG + 4 * CT
T_OUT1 = T_QKV1 + 6 * CT
T_FF1 = T_OUT1 + 2 * KD
T_DOWN1 = T_FF1 + 2 * NCH * CT
T_QKV2 = T_DOWN1 + 2 * (FF1 // P)
T_OUT2 = T_QKV2 + 12 * CT
T_FF2 = T_OUT2 + 2 * KD
T_DOWN2 = T_FF2 + 2 * NCH * CT
T_END = T_DOWN2 + 2 * (FF2 // P)

UNITS = 2 * KD
(A_SH1, A_SC1, A_G1, A_SH2, A_SC2, A_G2, B_SH1, B_SC1, B_G1, B_SH2, B_SC2, B_G2) = range(12)


def program(nc, ins, out):
    ctx = ExitStack()
    with ctx:
        names = [0]
        base = -(-nc.sbuf_base // 64) * 64

        def at(name, shape, offset, dt=F32):
            return nc.alloc_sbuf_tensor_at(name, shape, dt, offset=base + offset)

        KB = 1024
        x = at("x", [P, NT, D], 0)
        tmp = at("tmp", [P, D], 16 * KB)
        nat_a = at("nat_a", [P, NT, C], 16 * KB)
        nat_b = at("nat_b", [P, NT, C], 20 * KB)
        prob = at("prob", [P, 2, C], 20 * KB)
        h_hi = at("h_hi", [P, KD, SEQ], 24 * KB, F32R)
        h_lo = at("h_lo", [P, KD, SEQ], 40 * KB, F32R)
        junk = at("junk", [P, D], 40 * KB)
        raw = at("raw", [P, RING, TILE], 56 * KB)
        w_hi = at("w_hi", [P, RING, TILE], 72 * KB, F32R)
        w_lo = at("w_lo", [P, RING, TILE], 88 * KB, F32R)
        ada = at("ada", [P, 2, TILE], 104 * KB)
        start = at("start", [P, 4, D], 80 * KB)
        acc0 = at("acc0", [P, D], 112 * KB)
        acc1 = at("acc1", [P, D], 120 * KB)
        ff = at("ff", [P, 48, SEQ], 128 * KB)
        hc_hi = at("hc_hi", [P, KD, SEQ], 144 * KB, F32R)
        hc_lo = at("hc_lo", [P, KD, SEQ], 160 * KB, F32R)
        PADT = TAPS - 1 + SEQ
        u_pad = at("u_pad", [P, H1, PADT], 144 * KB)
        causal = at("causal", [P, NT, SEQ], 154 * KB)
        cvec = at("cvec", [P, 24 + H1 * TAPS], 156 * KB)
        mean1 = at("mean1", [P, P], 158 * KB)
        rstd_ln = at("rstd_ln", [P, SEQ], 159 * KB)
        st_vec = at("st_vec", [112, P], 128 * KB)
        st_c24 = at("st_c24", [24, P], 128 * KB + 512)
        st_cw = at("st_cw", [TAPS, H1 * P], 129 * KB)
        st_fc = at("st_fc", [86, 4, P], 133 * KB)
        taps = at("taps", [P, 3, SEQ], 170 * KB)
        tab = at("tab", [DR * H2, LANES], 161 * KB)
        E = 176 * KB
        q_t = at("q_t", [P, GH, SEQ], E)
        k_t = at("k_t", [P, GH, 2 * SEQ], E + 4 * KB)
        v_n = at("v_n", [P, 2 * NT, C], E + 12 * KB)
        p_t = at("p_t", [P, 2, C], E + 20 * KB)
        bias_t = at("bias_t", [P, 2, SEQ], E + 24 * KB)
        diag = at("diag", [P, 4, P], E + 24 * KB)
        ctx_n = [at("ctx_n0", [P, D], E + 8 * KB), at("ctx_n1", [P, D], E - 4 * KB)]
        scr = [at("scr0", [P, TILE], E + 4 * KB), at("scr1", [P, TILE], E + 20 * KB)]
        post1 = at("post1", [P, D], 162 * KB)
        post2 = at("post2", [P, D], E + 8 * KB)
        sig = at("sig", [P, NT, C], E)
        act_n = at("act_n", [P, NT, C], E + 4 * KB)
        conv_t = at("conv_t", [P, GH, SEQ], E + 8 * KB)
        gate_t = at("gate_t", [P, GH, SEQ], E + 12 * KB)
        f_hi = at("f_hi", [P, 2, SEQ], E + 16 * KB, F32R)
        f_lo = at("f_lo", [P, 2, SEQ], E + 18 * KB, F32R)
        h_f = at("h_f", [P, 2, C], E + 20 * KB)
        skew_s = at("skew_s", [GRID, H2 * DR, GRID], 162 * KB)
        S0 = 202 * KB
        ident = at("ident", [P, P], S0)
        ones = at("ones", [P, P], S0 + 512)
        vecs = at("vecs", [P, 112], S0 + 1024)
        cact = at("cact", [P, 48], S0 + 1472)
        fcw = at("fcw", [P, 4, 86], S0 + 1664)
        qg = at("qg", [P, HD], S0 + 3040)
        kg = at("kg", [P, HD], S0 + 3552)
        cols = at("cols", [P, 10, KD], S0 + 4064)
        stat = at("stat", [P, 64], S0 + 4704)
        eps_rms = at("eps_rms", [P, 1], S0 + 4960)
        eps_ln = at("eps_ln", [P, 1], S0 + 4992)
        assert base + S0 + 5024 <= nc.sbuf_usable_end

        ps = ctx.enter_context(nc.psum_tensor("ps", [P, 8, C], F32))

        table_d = nc.dram_tensor("rpb_table", (H2 * DR, GRID, LANES), F32, kind="Internal").ap()
        skew_d = nc.dram_tensor("rpb_skewed", (GRID, H2 * DR, GRID), F32, kind="Internal").ap()

        def sem(name):
            return ctx.enter_context(nc.semaphore(name))

        raw_landed = [sem(f"raw_landed{i}") for i in range(RING)]
        hi_ready = sem("hi_ready")
        lo_ready = sem("lo_ready")
        tile_used = sem("tile_used")
        ada_landed = [sem(f"ada_landed{i}") for i in range(2)]
        start_landed = [sem(f"start_landed{i}") for i in range(4)]
        ada_used = sem("ada_used")
        acc_clear = sem("acc_clear")
        acc_bias = [sem(f"acc_bias{i}") for i in range(3)]
        vec_landed = sem("vec_landed")
        small_landed = sem("small_landed")
        x_landed = sem("x_landed")
        ctx_landed = sem("ctx_landed")
        post_landed = sem("post_landed")
        out_landed = sem("out_landed")
        const_ready = sem("const_ready")
        pool_step = sem("pool_step")
        table_landed = sem("table_landed")
        bias_landed = [sem(f"bias_landed{i}") for i in range(2)]
        tr_done = [sem(f"tr_done{i}") for i in range(2)]
        tr_free = [sem(f"tr_free{i}") for i in range(2)]
        pair_free = [sem(f"pair_free{i}") for i in range(3)]
        cact_ready = sem("cact_ready")
        ss_ready = sem("ss_ready")
        xn_ready = sem("xn_ready")
        hhi_ready = sem("hhi_ready")
        hlo_ready = sem("hlo_ready")
        sig_ready = sem("sig_ready")
        conv_step = sem("conv_step")
        conv_pool = sem("conv_pool")
        std_ready = sem("std_ready")
        head_ss = sem("head_ss")
        head_std = sem("head_std")
        dev_ready = sem("dev_ready")
        sq_ready = sem("sq_ready")
        sq_read = sem("sq_read")
        ln_ready = sem("ln_ready")
        silu_done = sem("silu_done")
        s_done = sem("s_done")
        max_ready = sem("max_ready")
        exp_ready = sem("exp_ready")
        p_ready = sem("p_ready")
        o_done = sem("o_done")
        o_used = sem("o_used")
        fhi_ready = sem("fhi_ready")
        flo_ready = sem("flo_ready")
        cv_ready = sem("cv_ready")
        ff_ready = sem("ff_ready")
        x_ready = sem("x_ready")
        dve_step = sem("dve_step")
        act_step = sem("act_step")

        M, m = {}, 0
        for name, n in (("vec", 2), ("a_sh1", 1), ("a_sc1", 1), ("x1", 4), ("u", 2), ("a_g1", 2), ("qkv1", 8),
                        ("ln", 1), ("att1", 4), ("a_sh2", 1), ("a_sc2", 1), ("x2", 4), ("ffn1a", 4), ("a_g2", 2),
                        ("ffn1b", 4), ("b_sh1", 2), ("ffn1c", NCH - 8), ("b_sc1", 2), ("lat", 4), ("ctx", 4),
                        ("qkv2", 28), ("b_g1", 2), ("b_sh2", 1), ("b_sc2", 1), ("x7", 4),
                        ("ffn2a", 8), ("b_g2", 2), ("ffn2b", 2 * NCH - 8)):
            M[name] = m
            m += n
        USE0 = {"ag": 0, "k1": 2, "gate1": 4, "qkv2": 4 + NCH, "gate2": 12 + NCH}
        USE1 = {"ag": 0, "v1": 2, "up1": 4, "kc2": 4 + NCH, "up2": 8 + NCH}
        USE2 = {"q1": 0, "qkv2": 2}
        F_OUT1, F_DOWN1 = 0, KD
        F_OUT2 = F_DOWN1 + FF1 // P
        F_DOWN2 = F_OUT2 + KD
        UNITS1 = 16
        PER_GROUP = 2 * GH

        POOL_CONV = ((0, 1, 2), (4, 5))
        DVE_CONV = (3, 6, 7)
        POOL_CONV_OPS = sum(len(g) * (2 * TAPS - 1) for g in POOL_CONV)
        DVE_CONV_OPS = len(DVE_CONV) * TAPS

        def conv_operands(c, tap):
            return (ff[:, H1 + c, :], u_pad[:, c, tap:tap + SEQ],
                    cvec[:, 3 * H1 + c * TAPS + tap:3 * H1 + c * TAPS + tap + 1])

        block = ctx.enter_context(nc.Block())

        @block.sync
        def _(sp):
            def tile_cols(T, j, w, j2, col, width=C):
                s = j % RING
                dst = raw[:, s, 0:2 * width].rearrange("p (k n) -> p k n", k=2)
                src = w.rearrange("(k p) n -> p k n", p=P)[:, 2 * j2:2 * j2 + 2, bass.ds(col, width)]
                sp.wait_ge(lo_ready, T + j + 1)
                sp.dma_start(dst, src).then_inc(raw_landed[s], 16)

            def tile_rows(T, j, w, row):
                s = j % RING
                src = w[bass.ds(row, P), j % 2 * TILE:(j % 2 + 1) * TILE]
                sp.wait_ge(lo_ready, T + j + 1)
                sp.dma_start(raw[:, s, :], src).then_inc(raw_landed[s], 16)

            def unit(w, sec, n, row, half):
                src = w[bass.ds(row, P), sec * D + half * TILE:sec * D + (half + 1) * TILE]
                sp.wait_ge(ada_used, n + 1)
                sp.dma_start(ada[:, half, :], src).then_inc(ada_landed[half], 16)

            def bias_row(n, which, b, sec):
                acc = (acc0, acc1, tmp)[which]
                sp.wait_ge(acc_clear, n)
                sp.dma_start(acc[0:1, :], b[0:1, sec * D:(sec + 1) * D]).then_inc(acc_bias[which], 16)

            w_in, w_out1, w_gate, w_up1, w_down1 = (ins[k][0] for k in ("w_in", "w_out", "w_gate", "w_up", "w_down"))
            w_qkv, w_o2, w_up2, w_down2 = (ins[k][0] for k in ("na_w_qkv_2", "na_w_o_2", "ffn_w_up_2", "ffn_w_down_2"))
            ada1, ada2 = ins["ada_w"][0], ins["w_ada_2"][0]
            b1, b2 = ins["ada_b"], ins["b_ada_2"]

            bias_row(1, 1, b1, 0)
            bias_row(2, 0, b1, 1)
            def start_rows(sec, i, s):
                sp.dma_start(start[:, s, :], ada1[bass.ds(i * (4 * P) + s * P, P), sec * D:(sec + 1) * D])\
                    .then_inc(start_landed[s], 16)

            sp.wait_ge(vec_landed, 16 * 7)
            for s in range(4):
                start_rows(0, 0, s)
            for sec in range(2):
                with sp.Fori(1 - sec, KD // 4) as i:
                    for s in range(4):
                        sp.wait_ge(ada_used, i * 8 + (UNITS * sec + 2 * s - 4))
                        start_rows(sec, i, s)

            def ag(i, j):
                tile_cols(T_AG + 2 * CT * i, j, w_in, j % CT, (3 + j // CT) * H1 * HD + C * i)

            def qkv1(i, j):
                tile_cols(T_QKV1 + 3 * CT * i, j, w_in, j % CT, j // CT * H1 * HD + C * i)

            for j in range(3):
                ag(0, j)
            bias_row(3, 0, b1, 2)
            for i in range(2):
                for n in range(2 * CT):
                    j = n + 3
                    if j < 2 * CT:
                        ag(i, j)
                    elif i == 0:
                        ag(1, j - 2 * CT)
                    else:
                        qkv1(0, j - 2 * CT)
                    unit(ada1, 2, UNITS * 2 + 2 * CT * i + n, (KD // 2 * i + n // 2) * P, n % 2)
            bias_row(4, 1, b1, 3)
            for i in range(2):
                for n in range(3 * CT):
                    j = n + 3
                    if j < 3 * CT:
                        qkv1(i, j)
                    elif i == 0:
                        qkv1(1, j - 3 * CT)
                    else:
                        tile_rows(T_OUT1, j - 3 * CT, w_out1, (j - 3 * CT) // 2 * P)
                    if n >= CT:
                        u = n - CT
                        unit(ada1, 3, UNITS * 3 + 2 * CT * i + u, (KD // 2 * i + u // 2) * P, u % 2)

            def rows_pairs(T0, w, pairs, per_pair=0, sec=0, n0=0, ada_w=None, start=0):
                with sp.Fori(start, pairs) as i:
                    for j in range(4):
                        tile_rows(T0 + i * 4, j + 3, w, i * (2 * P) + (j + 3) // 2 * P)
                        if j < per_pair:
                            unit(ada_w, sec, n0 + i * per_pair + j, i * (per_pair // 2 * P) + j // 2 * P, j % 2)

            bias_row(5, 1, b1, 4)
            rows_pairs(T_OUT1, w_out1, KD // 2 - 1, 4, 4, UNITS * 4, ada1)

            def gate_up(T0, w_g, w_u, off):
                def one(i, j):
                    if j < CT:
                        tile_cols(T0 + CT + i * (2 * CT), j, w_u, j, off + i * C)
                    else:
                        tile_cols(T0 + CT + i * (2 * CT), j, w_g, j - CT, i * C + C)
                return one

            def last_pair_of_rows(T0, w, K, units, head):
                i = K // 2 - 1
                for j in range(4):
                    if j == 0:
                        tile_rows(T0 + 4 * i, 3, w, (2 * i + 1) * P)
                    else:
                        head(j - 1)
                    units(j)

            last_pair_of_rows(T_OUT1, w_out1, KD,
                              lambda j: unit(ada1, 4, UNITS * 5 - 4 + j, (KD - 2 + j // 2) * P, j % 2),
                              lambda j: tile_cols(T_FF1, j, w_gate, j, 0))

            one = gate_up(T_FF1, w_gate, w_up1, 0)
            for j in range(3, CT):
                tile_cols(T_FF1, j, w_gate, j, 0)
            for j in range(3):
                one(0, j)
            bias_row(6, 0, b1, 5)

            def ff1_loop(start, end, w, sec, n0):
                with sp.Fori(start, end) as i:
                    for n in range(2 * CT):
                        j = n + 3
                        if j < 2 * CT:
                            one(i, j)
                        else:
                            one(i + 1, j - 2 * CT)
                        if w is not None and n % 2 == 0:
                            u = n // 2
                            unit(w, sec, n0 + (i - start) * 8 + u, (i - start) * (4 * P) + u // 2 * P, u % 2)

            ff1_loop(0, 4, ada1, 5, UNITS * 5)
            bias_row(7, 1, b2, 0)
            bias_row(8, 2, b2, 0)
            ff1_loop(4, 8, ada2, 0, UNITS * 6)
            ff1_loop(8, NCH - 1, None, 0, 0)
            for j in range(3, CT):
                one(NCH - 1, j)
            for j in range(3):
                tile_rows(T_DOWN1, j, w_down1, j // 2 * P)
            bias_row(9, 1, b2, 1)
            bias_row(10, 2, b2, 1)
            rows_pairs(T_DOWN1, w_down1, 16, 2, 1, UNITS * 7, ada2)
            rows_pairs(T_DOWN1, w_down1, FF1 // P // 2 - 1, start=16)

            def qkv2(i, j):
                tile_cols(T_QKV2 + i * (3 * CT), j, w_qkv, j % CT, i * C + j // CT * D)

            last_pair_of_rows(T_DOWN1, w_down1, FF1 // P, lambda j: None, lambda j: qkv2(0, j))

            def qkv2_group(i, following, n0=0):
                for n in range(n0, 3 * CT):
                    j = n + 3
                    if j < 3 * CT:
                        qkv2(i, j)
                    else:
                        following(j - 3 * CT)
                    if n >= CT:
                        u = n - CT
                        unit(ada2, 2 + u // 2 % 2, i * 16 + (UNITS * 8 + u), i * (4 * P) + u // 4 * P, u % 2)

            for n in range(CT):
                qkv2(0, n + 3)
            bias_row(11, 0, b2, 2)
            bias_row(12, 1, b2, 3)
            qkv2_group(0, lambda j: qkv2(1, j), CT)
            with sp.Fori(1, 3) as i:
                qkv2_group(i, lambda j: qkv2(i + 1, j))
            qkv2_group(3, lambda j: tile_rows(T_OUT2, j, w_o2, j // 2 * P))
            bias_row(13, 1, b2, 4)
            rows_pairs(T_OUT2, w_o2, KD // 2 - 1, 4, 4, UNITS * 10, ada2)
            last_pair_of_rows(T_OUT2, w_o2, KD,
                              lambda j: unit(ada2, 4, UNITS * 11 - 4 + j, (KD - 2 + j // 2) * P, j % 2),
                              lambda j: tile_cols(T_FF2, j, w_up2, j, 0))
            one = gate_up(T_FF2, w_up2, w_up2, FF2)
            for j in range(3, CT):
                tile_cols(T_FF2, j, w_up2, j, 0)
            for j in range(3):
                one(0, j)
            bias_row(14, 0, b2, 5)
            ff1_loop(0, 4, ada2, 5, UNITS * 11)
            ff1_loop(4, NCH - 2, None, 0, 0)
            LASTP = NCH - 2
            TT = T_FF2 + CT + LASTP * 2 * CT

            def tail(j):
                if j < CT:
                    one(LASTP, j)
                elif j < 2 * CT:
                    tile_cols(TT, j, w_up2, j - CT, (NCH - 1) * C, TAILC)
                elif j < 3 * CT:
                    tile_cols(TT, j, w_up2, j - 2 * CT, FF2 + (NCH - 1) * C, TAILC)

            for j in range(3, 3 * CT):
                tail(j)
            for j in range(3):
                tile_rows(T_DOWN2, j, w_down2, j // 2 * P)
            rows_pairs(T_DOWN2, w_down2, FF2 // P // 2 - 1)
            LP = FF2 // P // 2 - 1
            for j in range(3, 6):
                tile_rows(T_DOWN2 + 4 * LP, j, w_down2, (2 * LP + j // 2) * P)
            for o in range(NT):
                t = NT - 1 - o
                sp.wait_ge(x_ready, 3 * NT + o + 1)
                sp.dma_start(out[0, t * P:(t + 1) * P, :], x[:, t, :]).then_inc(out_landed, 16)
            sp.wait_ge(out_landed, 16 * NT)

        @block.gpsimd
        def _(pool):
            steps = [0]

            def link(ins_):
                steps[0] += 1
                ins_.then_inc(pool_step, 1)
                pool.wait_ge(pool_step, steps[0])

            link(pool.memset(ident[:, :], 0.0))
            pool.memset(eps_rms[:, :], RMS_EPS)
            pool.memset(eps_ln[:, :], LN_EPS)
            pool.memset(ones[:, :], 1.0).then_inc(const_ready, 1)
            pool.affine_select(out=ident[:, :], in_=ident[:, :], compare_op=ALU.not_equal, fill=1.0, base=0,
                               pattern=[[-1, P]], channel_multiplier=1).then_inc(const_ready, 1)
            pool.memset(mean1[:, :], 1.0 / (H1 * HD)).then_inc(const_ready, 1)
            pool.memset(u_pad[:, :, :], 0.0).then_inc(const_ready, 1)
            link(pool.memset(causal[:, :, :], 0.0))
            pool.affine_select(out=causal[:, :, :], in_=causal[:, :, :], compare_op=ALU.is_ge, fill=NEG, base=0,
                               pattern=[[P, NT], [-1, SEQ]], channel_multiplier=1).then_inc(const_ready, 1)

            link(pool.memset(tab[:, :], 0.0))
            rpb = ins["na_rpb_2"][0]
            pool.wait_ge(ada_used, 2 + 2 * UNITS)
            lo_dr, lane = RPB_H // 2 - (ROWS - 1), GRID - 1 - RPB_W // 2
            for h in range(H2):
                pool.dma_start(tab[h * DR:(h + 1) * DR, lane:lane + RPB_W],
                               rpb[h, lo_dr:lo_dr + DR, :]).then_inc(table_landed, 16)
            pool.wait_ge(table_landed, 16 * H2)
            pool.dma_start(table_d, tab[:, :].unsqueeze(1).broadcast_to([H2 * DR, GRID, LANES])).then_inc(table_landed, 16)
            pool.wait_ge(table_landed, 16 * (H2 + 1))
            pool.dma_start(skew_s[:, :, :], bass.AP(table_d.tensor, GRID - 1,
                                                          [[LANES - 1, GRID], [GRID * LANES, H2 * DR], [1, GRID]]))\
                .then_inc(table_landed, 16)
            pool.wait_ge(table_landed, 16 * (H2 + 2))
            W, WH = 16, 8
            v = skew_s[:, :, 0:GRID - W]
            link(pool.affine_select(out=v, in_=v, compare_op=ALU.is_ge, fill=NEG, base=WH,
                                    pattern=[[0, H2 * DR], [1, GRID - W]], channel_multiplier=-1))
            v = skew_s[:, :, W:GRID]
            link(pool.affine_select(out=v, in_=v, compare_op=ALU.is_gt, fill=NEG, base=WH - W,
                                    pattern=[[0, H2 * DR], [-1, GRID - W]], channel_multiplier=1))
            pool.dma_start(skew_d, skew_s[:, :, :]).then_inc(table_landed, 16)
            pool.wait_ge(table_landed, 16 * (H2 + 3))

            ops = 0
            for i, groups in enumerate(POOL_CONV):
                for b in range(2):
                    pool.wait_ge(tr_free[b], i + (M["u"] + 1))
                for tap in range(TAPS):
                    for n, c in enumerate(groups):
                        dst, src, wv = conv_operands(c, tap)
                        if tap >= 2 or (tap and i):
                            pool.wait_ge(conv_pool, ops - len(groups) + 1)
                        if tap == 0:
                            s = pool.tensor_scalar(dst, src, wv, cvec[:, c:c + 1], ALU.mult, ALU.add)
                        else:
                            s = pool.tensor_scalar(taps[:, n, :], src, wv, None, ALU.mult)
                        s.then_inc(conv_pool, 1)
                        ops += 1
                    for n, c in enumerate(groups if tap else ()):
                        dst = ff[:, H1 + c, :]
                        pool.wait_ge(conv_pool, ops - len(groups) + 1)
                        pool.tensor_tensor(dst, dst, taps[:, n, :], ALU.add).then_inc(conv_pool, 1)
                        ops += 1

            pool.wait_ge(hlo_ready, 32)

            def unit_bias(i, u):
                c = u % 2
                pool.wait_ge(max_ready, i * PER_GROUP + (UNITS1 + u - 1))
                for r in range(2):
                    src = skew_d[:, bass.ds(i * (GH * DR) + (u // 2 * DR + ROWS - 1 - 2 * c - r), ROWS), :]
                    pool.dma_start(bias_t[r * GRID:(r + 1) * GRID, c, :],
                                   src.rearrange("p a b -> p (a b)")).then_inc(bias_landed[c], 16)

            with pool.Fori(0, 4) as i:
                for u in range(PER_GROUP):
                    unit_bias(i, u)

        @block.scalar
        def _(act):
            steps = [0]

            def link(ins_):
                steps[0] += 1
                ins_.then_inc(act_step, 1)
                act.wait_ge(act_step, steps[0])

            def hi(T, j):
                s = j % RING
                act.wait_ge(raw_landed[s], T * (16 // RING) + 16 * (j // RING + 1))
                act.wait_ge(tile_used, T + j + 1)
                act.activation(w_hi[:, s, :], raw[:, s, :], ACT.Copy).then_inc(hi_ready, 1)

            def chunk_wait(T, j):
                act.wait_ge(tile_used, T + (j + RING))

            act.wait_ge(const_ready, 1)
            rows = ("c", "c_2", "c_ctx_2", "mix_pre_g", "ffn_pre_g", "norm_mix_g_2", "norm_ffn_g_2")
            for n, name in enumerate(rows):
                v = ins[name]
                v = v.rearrange("(r n) -> r n", n=P) if len(v.shape) == 1 else v.rearrange("a (r n) -> (a r) n", n=P)
                act.dma_start(st_vec[KD * n:KD * (n + 1), :], v).then_inc(vec_landed, 16)
            act.dma_start(x[:, :, :], ins["x"][0].rearrange("(t p) d -> p t d", p=P)).then_inc(x_landed, 16)
            for n, name in enumerate(("conv_b", "conv_ln_g", "conv_ln_b")):
                act.dma_start(st_c24[H1 * n:H1 * (n + 1), :], ins[name].rearrange("a (r n) -> (a r) n", n=P))\
                    .then_inc(small_landed, 16)
            act.dma_start(st_cw[:, :], ins["conv_w"][0]).then_inc(small_landed, 16)
            act.dma_start(st_fc[:, 0:3, :], ins["ffn_conv_w_2"][0].rearrange("t (r n) -> r t n", n=P)).then_inc(small_landed, 16)
            act.dma_start(st_fc[:, 3, :], ins["ffn_conv_b_2"][0].rearrange("(r n) -> r n", n=P)).then_inc(small_landed, 16)
            act.dma_start(qg[:, :], ins["na_q_g_2"][0:1, :].to_broadcast([P, HD])).then_inc(small_landed, 16)
            act.dma_start(kg[:, :], ins["na_k_g_2"][0:1, :].to_broadcast([P, HD])).then_inc(small_landed, 16)

            act.wait_ge(tr_done[0], 1)
            act.activation(cact[:, :], ps[:, 6, 0:48], ACT.Silu).then_inc(cact_ready, 1)
            act.activation(vecs[:, :], ps[:, 6, 0:112], ACT.Copy).then_inc(tr_free[0], 1)
            act.wait_ge(tr_done[1], 1)
            act.activation(cvec[:, :], ps[:, 7, 0:24 + H1 * TAPS], ACT.Copy).then_inc(tr_free[1], 1)
            act.wait_ge(tr_done[0], 2)
            act.activation(fcw[:, 0:3, :], ps[:, 6, 0:258].rearrange("p (t r) -> p t r", t=3), ACT.Copy).then_inc(tr_free[0], 1)
            act.wait_ge(tr_done[1], 2)
            act.activation(fcw[:, 3, :], ps[:, 7, 0:86], ACT.Copy).then_inc(tr_free[1], 1)
            link(act.activation(stat[:, 63:64], ones[:, 0:1], ACT.Copy))

            def row_squares(n, src, hold=None):
                if hold is not None:
                    act.wait_ge(*hold)
                act.activation(junk[:, :], src, ACT.Square, accum_out=stat[:, 32 + n % 4:33 + n % 4]).then_inc(ss_ready, 1)
                act.wait_ge(ss_ready, n + 1)
                act.activation(stat[:, 36 + n % 4:37 + n % 4], stat[:, 32 + n % 4:33 + n % 4], ACT.Sqrt,
                               scale=1.0 / D, bias=eps_rms[:, :]).then_inc(std_ready, 1)

            def modulated(n0, m_, e, idx):
                for o in range(NT):
                    t = NT - 1 - o
                    n = n0 + 2 * e + o
                    act.wait_ge(tr_done[t], m_ + e + 1)
                    if n >= 2:
                        act.wait_ge(hlo_ready, n - 1)
                    for k in range(4):
                        kk = 4 * e + k
                        s = act.activation(h_f[:, o, k * P:(k + 1) * P], ps[:, 6 + t, k * P:(k + 1) * P], ACT.Identity,
                                           scale=cols[:, idx, kk:kk + 1], bias=cols[:, idx + 1, kk:kk + 1])
                    s.then_inc(tr_free[t], 1)

            def first_chunk(T, n0, m_, idx, extra=lambda n: None):
                modulated(n0, m_, 0, idx)
                for n in range(CT):
                    if n < 3:
                        modulated(n0, m_, n + 1, idx)
                    extra(n)
                    hi(T, n + 3)

            act.wait_ge(x_landed, 16)
            for t in range(NT):
                row_squares(t, x[:, NT - 1 - t, :])
            for j in range(3):
                if j == 2:
                    act.wait_ge(ada_used, 2 + 2 * UNITS)
                hi(T_AG, j)
            act.wait_ge(const_ready, 5)
            for i in range(2):
                T = T_AG + i * (2 * CT)
                if i == 0:
                    first_chunk(T, 0, M["x1"], 0)
                for n in range(CT * (1 - i), 2 * CT):
                    hi(T, n + 3)
                chunk_wait(T, 2 * CT)
                for t in range(NT):
                    s = act.activation(nat_a[:, t, :], ps[:, 2 + t, :], ACT.Sigmoid)
                s.then_inc(pair_free[1], 1)
                for b in range(2):
                    act.wait_ge(tr_done[b], i + (M["u"] + 1))
                    act.activation(u_pad[:, bass.ds(i * GH + 2 * b, 2), TAPS - 1:PADT],
                                   ps[:, 6 + b, :].rearrange("p (g n) -> p g n", g=2), ACT.Copy).then_inc(tr_free[b], 1)

            def attention(U, Mb, nkt, head, beside):
                def exp(u):
                    act.wait_ge(max_ready, U + (u + 1))
                    act.activation(prob[:, u % 2, 0:nkt * P], prob[:, u % 2, 0:nkt * P], ACT.Exp,
                                   bias=stat[:, u % 2:u % 2 + 1], accum_out=stat[:, 4 + u % 2:5 + u % 2]).then_inc(exp_ready, 1)

                def out_of(u):
                    act.wait_ge(o_done, U + (u + 1))
                    act.activation(ff[:, head(u // 2), u % 2 * P:(u % 2 + 1) * P],
                                   ps[:, 2 + u % 2, 0:P].unsqueeze(1), ACT.Copy).then_inc(o_used, 1)

                exp(0)
                for u in range(PER_GROUP):
                    if u + 1 < PER_GROUP:
                        exp(u + 1)
                    beside(u)
                    act.wait_ge(tr_done[u % 2], Mb + (u // 2 + 1))
                    act.activation(p_t[:, u % 2, 0:nkt * P], ps[:, 6 + u % 2, 0:nkt * P], ACT.Copy).then_inc(tr_free[u % 2], 1)
                    if u >= 1:
                        out_of(u - 1)
                out_of(PER_GROUP - 1)

            act.wait_ge(table_landed, 16 * (H2 + 3))
            act.dma_start(post1[:, :], ins["mix_post_g"][0:1, :].to_broadcast([P, D])).then_inc(post_landed, 16)
            for n in range(CT):
                hi(T_QKV1, n + 3)
            for i in range(2):
                T = T_QKV1 + i * (3 * CT)
                Mb = i * 6 + M["qkv1"]

                def evacuate(dst, b):
                    for t in range(NT):
                        s = act.activation(dst[:, t, :], ps[:, 2 * b + t, :], ACT.Copy)
                    s.then_inc(pair_free[b], 1)

                def transposed(dst, m_):
                    for b in range(2):
                        act.wait_ge(tr_done[b], m_ + 1)
                        act.activation(dst[:, 2 * b:2 * b + 2, 0:SEQ],
                                       ps[:, 6 + b, :].rearrange("p (g n) -> p g n", g=2), ACT.Copy).then_inc(tr_free[b], 1)

                chunk_wait(T, CT)
                evacuate(nat_a, 2)
                for n in range(CT, 2 * CT):
                    if n == CT + 4:
                        transposed(q_t, Mb)
                    hi(T, n + 3)
                chunk_wait(T, 2 * CT)
                evacuate(nat_b, 0)
                for n in range(2 * CT, 3 * CT):
                    if n == 2 * CT + 4:
                        transposed(k_t, Mb + 1)
                    if i == 1 and n == 3 * CT - 1:
                        act.wait_ge(dev_ready, 1)
                        act.activation(tmp[:, :], ff[:, 8:16, :].rearrange("p g n -> p (g n)"), ACT.Square).then_inc(sq_ready, 1)
                    hi(T, n + 3)
                chunk_wait(T, 3 * CT)
                evacuate(v_n, 1)
                if i == 0:
                    attention(0, Mb + 2, NT, lambda h: slice(h, h + 1), lambda u: hi(T, 3 * CT + u + 3))
                    continue
                act.wait_ge(tr_done[1], M["ln"] + 1)
                act.activation(rstd_ln[:, :], ps[:, 7, 0:SEQ], ACT.Sqrt, bias=eps_ln[:, :]).then_inc(tr_free[1], 1)

                def scaled_silu(u):
                    if u < PER_GROUP - 1:
                        return
                    act.wait_ge(ln_ready, 1)
                    for g in range(H1):
                        act.activation(ff[:, 8 + g, :], ff[:, 8 + g, :], ACT.Silu,
                                       scale=cvec[:, H1 + g:H1 + g + 1], bias=cvec[:, 2 * H1 + g:2 * H1 + g + 1])\
                            .then_inc(silu_done, 1)

                attention(PER_GROUP, M["att1"], NT, lambda h: slice(GH + h, GH + h + 1), scaled_silu)

            def stage_hi(F, k, src):
                act.activation(f_hi[:, k % 2, :], src, ACT.Copy).then_inc(fhi_ready, 1)

            def rows_phase(T0, F0, K):
                def one_k(k):
                    return ff[:, bass.ds(k, 1), :].rearrange("p o n -> p (o n)")

                act.wait_ge(tile_used, T0 + RING)
                if F0 == F_OUT1:
                    act.wait_ge(silu_done, H1)
                stage_hi(F0, 0, one_k(0))
                with act.Fori(0, K // 2 - 1) as i:
                    T = T0 + i * 4
                    hi(T, 3)
                    stage_hi(F0, 1, one_k(i * 2 + 1))
                    hi(T, 4)
                    hi(T, 5)
                    stage_hi(F0, 0, one_k(i * 2 + 2))
                    hi(T, 6)
                T = T0 + 4 * (K // 2 - 1)
                hi(T, 3)
                stage_hi(F0, 1, one_k(K // 2 * 2 - 1))
                if K % 2 == 0:
                    for j in range(4, 7):
                        hi(T, j)
                else:
                    hi(T, 4)
                    hi(T, 5)
                    stage_hi(F0, 0, one_k(K - 1))

            def y_squares(n, Tend):
                act.wait_ge(tile_used, Tend + RING)
                for o in range(NT):
                    t = NT - 1 - o
                    row_squares(n + o, ps[:, 4 * t:4 * t + 4, :].rearrange("p b n -> p (b n)"))

            def x_squares(n, done):
                for o in range(NT):
                    row_squares(n + o, x[:, NT - 1 - o, :], (x_ready, done + o + 1))

            rows_phase(T_OUT1, F_OUT1, KD)
            y_squares(2, T_FF1)

            x_squares(4, 0)
            first_chunk(T_FF1, 8, M["x2"], 2)

            def gate_act():
                for t in range(NT):
                    s = act.activation(sig[:, t, :], ps[:, t, :], ACT.Silu)
                s.then_inc(pair_free[0], 1)

            def act_transposed(i, m_):
                for b in range(2):
                    act.wait_ge(tr_done[b], i + (m_ + 1))
                    act.activation(ff[:, bass.ds(i * GH + 2 * b, 2), :],
                                   ps[:, 6 + b, :].rearrange("p (g n) -> p g n", g=2), ACT.Copy).then_inc(tr_free[b], 1)

            chunk_wait(T_FF1, CT)
            gate_act()
            act.dma_start(post2[:, :], ins["ffn_post_g"][0:1, :].to_broadcast([P, D])).then_inc(post_landed, 16)
            for start_, end, m_ in ((0, 4, M["ffn1a"]), (4, 8, M["ffn1b"] - 4), (8, NCH - 1, M["ffn1c"] - 8)):
                with act.Fori(start_, end) as i:
                    T = T_FF1 + CT + i * (2 * CT)
                    for n in range(2 * CT):
                        if n == CT + 4:
                            act_transposed(i, m_)
                        hi(T, n + 3)
                    chunk_wait(T, 2 * CT)
                    gate_act()
            T = T_FF1 + CT + (NCH - 1) * 2 * CT
            for n in range(CT):
                hi(T, n + 3)
            act_transposed(NCH - 1, M["ffn1c"] - 8)
            for t in range(NT):
                act.dma_start(ctx_n[t][:, :], ins["ctx_2"][0, t * P:(t + 1) * P, :]).then_inc(ctx_landed, 16)
            rows_phase(T_DOWN1, F_DOWN1, FF1 // P)
            y_squares(6, T_QKV2)

            x_squares(8, NT)
            row_squares(10, ctx_n[1][:, :], (ctx_landed, 16 * NT))
            row_squares(11, ctx_n[0][:, :])
            first_chunk(T_QKV2, 16, M["lat"], 4, lambda n: modulated(24, M["ctx"], n - 4, 6) if n >= 4 else None)

            def qkv2(i, following):
                T = T_QKV2 + i * (3 * CT)
                Mb = i * 7 + M["qkv2"]
                SQ = i * 3 + 1

                def squares(b, n):
                    act.wait_ge(sq_read, SQ + n)
                    act.activation(p_t[:, :, :], ps[:, 2 * b:2 * b + 2, :], ACT.Square).then_inc(sq_ready, 1)
                    act.wait_ge(head_ss, i * 3 + (n + 1))
                    act.activation(stat[:, 16:24], stat[:, 8:16], ACT.Sqrt, scale=1.0 / HD,
                                   bias=eps_rms[:, :]).then_inc(head_std, 1)

                def transposed(dst, m_, at_):
                    for b in range(2):
                        act.wait_ge(tr_done[b], m_ + 1)
                        act.activation(dst[:, 2 * b:2 * b + 2, at_:at_ + SEQ],
                                       ps[:, 6 + b, :].rearrange("p (g n) -> p g n", g=2), ACT.Copy).then_inc(tr_free[b], 1)

                chunk_wait(T, CT)
                squares(2, 0)
                for n in range(CT, 2 * CT):
                    if n == CT + 4:
                        transposed(q_t, Mb, 0)
                    hi(T, n + 3)
                chunk_wait(T, 2 * CT)
                squares(0, 1)
                squares(1, 2)
                for n in range(2 * CT, 3 * CT):
                    if n == 2 * CT + 4:
                        transposed(k_t, Mb + 1, 0)
                        transposed(k_t, Mb + 2, SEQ)
                    hi(T, n + 3)
                chunk_wait(T, 3 * CT)
                for half, b in ((0, 2), (1, 0)):
                    for t in range(NT):
                        s = act.activation(v_n[:, NT * half + t, :], ps[:, 2 * b + t, :], ACT.Copy)
                    s.then_inc(pair_free[b], 1)
                attention(i * PER_GROUP + UNITS1, Mb + 3, 2 * NT, lambda h: bass.ds(i * GH + h, 1),
                          lambda u: hi(T, 3 * CT + u + 3) if following else None)

            with act.Fori(0, 3) as i:
                qkv2(i, True)
            qkv2(3, False)

            act.wait_ge(o_used, UNITS1 + 32)
            rows_phase(T_OUT2, F_OUT2, KD)

            x_squares(12, 2 * NT)
            first_chunk(T_FF2, 32, M["x7"], 8)

            def plain(dst, b):
                for t in range(NT):
                    s = act.activation(dst[:, t, :], ps[:, 2 * b + t, :], ACT.Copy)
                s.then_inc(pair_free[b], 1)

            def middle_tap(m_, col, groups, silu, CV):
                for b in range(2):
                    act.wait_ge(tr_done[b], m_ + 1)
                    for g in range(2 * b, min(2 * b + 2, groups)):
                        act.activation(conv_t[:, g, :], ps[:, 6 + b, g % 2 * SEQ:(g % 2 + 1) * SEQ], ACT.Identity,
                                       scale=fcw[:, 1, bass.ds(col + g, 1)],
                                       bias=fcw[:, 3, bass.ds(col + g, 1)]).then_inc(cv_ready, 1)
                if silu:
                    for b in range(2):
                        act.wait_ge(tr_free[b], m_ + 1)
                        act.activation(gate_t[:, 2 * b:min(2 * b + 2, groups), :],
                                       conv_t[:, 2 * b:min(2 * b + 2, groups), :], ACT.Silu).then_inc(sig_ready, 1)

            GC, UC = 0, FF2 // P
            chunk_wait(T_FF2, CT)
            plain(sig, 0)
            for start_, end, M_ in ((0, 4, M["ffn2a"]), (4, NCH - 1, M["ffn2b"] - 8)):
                with act.Fori(start_, end) as i:
                    T = T_FF2 + CT + i * (2 * CT)
                    m_ = i * 2 + M_
                    for n in range(CT):
                        if n == 4:
                            act.wait_ge(ff_ready, i * 2 + 1)
                            middle_tap(m_, i * GH, GH, True, 0)
                        hi(T, n + 3)
                    chunk_wait(T, CT)
                    plain(act_n, 1)
                    for n in range(CT, 2 * CT):
                        if n == CT + 4:
                            middle_tap(m_ + 1, i * GH + UC, GH, False, 0)
                        hi(T, n + 3)
                    chunk_wait(T, 2 * CT)
                    plain(sig, 0)
            T = T_FF2 + CT + (NCH - 1) * 2 * CT
            m_ = M["ffn2b"] - 8 + 2 * (NCH - 1)
            for n in range(CT):
                if n == 4:
                    act.wait_ge(ff_ready, 2 * (NCH - 1) + 1)
                    middle_tap(m_, GH * (NCH - 1), TAILC // P, True, 0)
                hi(T, n + 3)
            chunk_wait(T, CT)
            plain(act_n, 1)
            middle_tap(m_ + 1, GH * (NCH - 1) + UC, TAILC // P, False, 0)
            act.wait_ge(ff_ready, 2 * NCH + 1)
            rows_phase(T_DOWN2, F_DOWN2, FF2 // P)

        @block.vector
        def _(dve):
            steps = [0]

            def link(ins_, off=0):
                steps[0] += 1
                ins_.then_inc(dve_step, 1)
                dve.wait_ge(dve_step, off + steps[0])

            def lo(T, j):
                s = j % RING
                dve.wait_ge(hi_ready, T + (j + 1))
                dve.tensor_tensor(w_lo[:, s, :], raw[:, s, :], w_hi[:, s, :].bitcast(F32), ALU.subtract).then_inc(lo_ready, 1)

            def unit(n, k, half, vec, acc, then_ctx=None):
                dve.wait_ge(ada_landed[half], n * 8 + (16 - 8 * half - 16 * UNITS))
                dve.wait_ge(ada_used, n + 1)
                a = acc[:, half * TILE:(half + 1) * TILE]
                ins_ = dve.scalar_tensor_tensor(out=a, in0=ada[:, half, :], scalar=cact[:, bass.ds(k + vec * KD, 1)],
                                                in1=a, op0=ALU.mult, op1=ALU.add)
                if then_ctx is not None:
                    a2 = then_ctx[:, half * TILE:(half + 1) * TILE]
                    ins_ = dve.scalar_tensor_tensor(out=a2, in0=ada[:, half, :], scalar=cact[:, bass.ds(k + 2 * KD, 1)],
                                                    in1=a2, op0=ALU.mult, op1=ALU.add)
                ins_.then_inc(ada_used, 1)

            def clear(acc):
                dve.memset(acc[:, :], 0.0).then_inc(acc_clear, 1)

            def shift_cols(M_, idx):
                for b in range(2):
                    dve.wait_ge(tr_done[b], M_ + 1)
                    dve.tensor_copy(cols[:, idx, 8 * b:8 * b + 8], ps[:, 6 + b, 0:8]).then_inc(tr_free[b], 1)

            def scale_cols(M_, idx, g):
                for b in range(2):
                    dve.wait_ge(tr_done[b], M_ + 1)
                    dve.scalar_tensor_tensor(out=cols[:, idx, 8 * b:8 * b + 8], in0=ps[:, 6 + b, 0:8], scalar=1.0,
                                             in1=vecs[:, g + 8 * b:g + 8 * b + 8], op0=ALU.add, op1=ALU.mult)\
                        .then_inc(tr_free[b], 1)

            def gate_rows(M_, post=None):
                for c in range(4):
                    b = c % 2
                    dve.wait_ge(tr_done[b], M_ + c // 2 + 1)
                    dst = acc0[:, c * C:(c + 1) * C]
                    if post is not None:
                        ins_ = dve.tensor_tensor(dst, ps[:, 6 + b, :], post[:, c * C:(c + 1) * C], ALU.mult)
                    else:
                        ins_ = dve.tensor_copy(dst, ps[:, 6 + b, :])
                    ins_.then_inc(tr_free[b], 1)

            def rows_rstd(n):
                dve.wait_ge(std_ready, n + 1)
                r = stat[:, 40 + n % 4:41 + n % 4]
                link(dve.reciprocal(r, stat[:, 36 + n % 4:37 + n % 4]))
                return r

            def make_diag(n, slot):
                r = rows_rstd(n)
                dve.tensor_scalar(diag[:, slot, :], ident[:, :], r, None, ALU.mult).then_inc(xn_ready, 1)

            def split(n0, m_, e, hi_, lo_):
                for o in range(NT):
                    t = NT - 1 - o
                    n = n0 + 2 * e + o
                    f = h_f[:, o, :].rearrange("p (k n) -> p k n", k=4)
                    at_ = (slice(None), slice(4 * e, 4 * e + 4), slice(t * P, (t + 1) * P))
                    dve.wait_ge(tr_free[t], m_ + e + 1)
                    dve.tensor_copy(hi_[at_], f).then_inc(hhi_ready, 1)
                    dve.wait_ge(hhi_ready, n + 1)
                    dve.tensor_tensor(lo_[at_], f, hi_[at_].bitcast(F32), ALU.subtract).then_inc(hlo_ready, 1)

            def first_chunk(T, n0, m_, units, extra=lambda n: None):
                split(n0, m_, 0, h_hi, h_lo)
                for n in range(CT):
                    if n < 3:
                        split(n0, m_, n + 1, h_hi, h_lo)
                    extra(n)
                    lo(T, n + 3)
                    units(n)

            clear(acc1)
            clear(acc0)
            dve.wait_ge(cact_ready, 1)
            for sec, acc in ((0, acc1), (1, acc0)):
                dve.wait_ge(acc_bias[1 - sec], 16)
                with dve.Fori(0, KD // 4) as i:
                    for s in range(4):
                        dve.wait_ge(start_landed[s], i * 16 + (16 * (4 * sec + 1)))
                        dve.wait_ge(ada_used, i * 8 + (UNITS * sec + 2 * s + 2))
                        dve.scalar_tensor_tensor(out=acc[:, :], in0=start[:, s, :], scalar=cact[:, bass.ds(i * 4 + s, 1)],
                                                 in1=acc[:, :], op0=ALU.mult, op1=ALU.add).then_inc(ada_used, 2)
            dve.wait_ge(const_ready, 2)
            make_diag(0, 1)
            make_diag(1, 0)
            shift_cols(M["a_sh1"], 1)
            scale_cols(M["a_sc1"], 0, 48)
            dve.wait_ge(tr_free[1], M["a_sc1"] + 1)
            clear(acc0)
            for j in range(3):
                lo(T_AG, j)
            split(0, M["x1"], 0, h_hi, h_lo)
            for i in range(2):
                T = T_AG + i * (2 * CT)
                for n in range(2 * CT):
                    if i == 0 and n < 3:
                        split(0, M["x1"], n + 1, h_hi, h_lo)
                    lo(T, n + 3)
                    if i == 0 and n == 0:
                        dve.wait_ge(acc_bias[0], 32)
                    unit(i * (2 * CT) + (UNITS * 2 + n), i * (KD // 2) + n // 2, n % 2, 0, acc0)
                dve.wait_ge(pair_free[1], i + 2)
                for t in range(NT):
                    s = dve.tensor_tensor(nat_b[:, t, :], ps[:, t, :], nat_a[:, t, :], ALU.mult)
                s.then_inc(pair_free[0], 1)
            clear(acc1)

            def softmax(U, Mb, nkt, bias, landed, beside):
                def max_of(u):
                    b = u % 2
                    dve.wait_ge(s_done, U + (u + 1))
                    if u >= 2:
                        dve.wait_ge(tr_done[b], Mb + u // 2)
                    if landed is not None:
                        dve.wait_ge(bias_landed[b], landed + 32 * (u // 2 + 1))
                    if nkt > NT:
                        dve.tensor_scalar(prob[:, b, SEQ:2 * SEQ], ps[:, b, SEQ:2 * SEQ], SCALE, None, ALU.mult)
                    link(dve.scalar_tensor_tensor(out=prob[:, b, 0:SEQ], in0=ps[:, b, 0:SEQ], scalar=SCALE,
                                                  in1=bias[:, b, :], op0=ALU.mult, op1=ALU.add), off[0])
                    link(dve.tensor_reduce(stat[:, 2 + b:3 + b], prob[:, b, 0:nkt * P], AX, ALU.max), off[0])
                    dve.tensor_scalar(stat[:, b:b + 1], stat[:, 2 + b:3 + b], -1.0, None, ALU.mult).then_inc(max_ready, 1)

                max_of(0)
                for u in range(PER_GROUP):
                    if u + 1 < PER_GROUP:
                        max_of(u + 1)
                    b = u % 2
                    dve.wait_ge(exp_ready, U + u + 1)
                    link(dve.reciprocal(stat[:, 6 + b:7 + b], stat[:, 4 + b:5 + b]), off[0])
                    pr = prob[:, b, 0:nkt * P]
                    dve.tensor_scalar(pr, pr, stat[:, 6 + b:7 + b], None, ALU.mult).then_inc(p_ready, 1)
                    beside(u)

            off = [0]
            dve.wait_ge(const_ready, 5)
            dve.wait_ge(acc_bias[1], 32)
            for b in range(2):
                dve.wait_ge(tr_free[b], M["u"] + 2)
            taps_done = [0]

            def conv_taps():
                o = taps_done[0]
                if o == DVE_CONV_OPS:
                    return
                taps_done[0] += 1
                tap, c = o // len(DVE_CONV), DVE_CONV[o % len(DVE_CONV)]
                dst, src, wv = conv_operands(c, tap)
                if tap == 0:
                    s = dve.tensor_scalar(dst, src, wv, cvec[:, c:c + 1], ALU.mult, ALU.add)
                else:
                    dve.wait_ge(conv_step, o - len(DVE_CONV) + 1)
                    s = dve.scalar_tensor_tensor(out=dst, in0=src, scalar=wv, in1=dst, op0=ALU.mult, op1=ALU.add)
                s.then_inc(conv_step, 1)

            for n in range(CT):
                conv_taps()
                lo(T_QKV1, n + 3)
                conv_taps()
                conv_taps()
            dve.wait_ge(post_landed, 16)
            gate_rows(M["a_g1"], post1)
            cv = ff[:, H1:2 * H1, :]
            for i in range(2):
                T = T_QKV1 + i * (3 * CT)
                for n in range(CT, 3 * CT):
                    u = n - CT
                    if i == 1 and n == 2 * CT + 6:
                        dve.wait_ge(tr_done[0], M["ln"] + 1)
                        dve.tensor_tensor(cv, cv, ps[:, 6, 0:SEQ].unsqueeze(1).to_broadcast([P, H1, SEQ]), ALU.subtract)\
                            .then_inc(dev_ready, 1)
                        dve.wait_ge(dev_ready, 1)
                        dve.tensor_copy(stat[:, 62:63], ps[:, 6, 0:1]).then_inc(tr_free[0], 1)
                    conv_taps()
                    lo(T, n + 3)
                    conv_taps()
                    if i == 0:
                        conv_taps()
                    unit(i * (2 * CT) + (UNITS * 3 + u), i * (KD // 2) + u // 2, u % 2, 0, acc1)
                if i == 0:
                    softmax(0, M["qkv1"] + 2, NT, causal, None, lambda u: lo(T, 3 * CT + u + 3))
            assert taps_done[0] == DVE_CONV_OPS
            dve.wait_ge(tr_free[1], M["ln"] + 1)
            link(dve.reciprocal(rstd_ln[:, :], rstd_ln[:, :]))
            dve.tensor_tensor(cv, cv, rstd_ln[:, :].unsqueeze(1).to_broadcast([P, H1, SEQ]), ALU.mult).then_inc(ln_ready, 1)
            softmax(PER_GROUP, M["att1"], NT, causal, None, lambda u: None)

            shift_cols(M["a_sh2"], 3)
            clear(acc1)

            def stage_lo(F, k, src):
                dve.wait_ge(fhi_ready, F + 1)
                dve.tensor_tensor(f_lo[:, k % 2, :], src, f_hi[:, k % 2, :].bitcast(F32), ALU.subtract).then_inc(flo_ready, 1)

            def rows_pair(T, F, k0, units, last=False):
                def one_k(k):
                    return ff[:, bass.ds(k, 1), :].rearrange("p o n -> p (o n)")

                lo(T, 3)
                units(0)
                stage_lo(F + 1, 1, one_k(k0 + 1))
                lo(T, 4)
                units(1)
                lo(T, 5)
                units(2)
                if not last:
                    stage_lo(F + 2, 0, one_k(k0 + 2))
                lo(T, 6)
                units(3)

            def rows_first(F0):
                stage_lo(F0, 0, ff[:, 0, :])

            none = lambda j: None
            rows_first(F_OUT1)
            dve.wait_ge(acc_bias[1], 48)
            with dve.Fori(0, KD // 2 - 1) as i:
                rows_pair(T_OUT1 + i * 4, F_OUT1 + i * 2, i * 2,
                          lambda j: unit(i * 4 + (UNITS * 4 + j), i * 2 + j // 2, j % 2, 0, acc1))
            i = KD // 2 - 1
            rows_pair(T_OUT1 + 4 * i, F_OUT1 + 2 * i, 2 * i,
                      lambda j: unit(4 * i + UNITS * 4 + j, 2 * i + j // 2, j % 2, 0, acc1), last=True)

            def update(done, norm, n=0):
                for o in range(NT):
                    t = NT - 1 - o
                    if norm:
                        r = rows_rstd(n + o)
                    if o:
                        dve.wait_ge(x_ready, done + o)
                    for half in range(2):
                        y = ps[:, 4 * t + 2 * half:4 * t + 2 * half + 2, :].rearrange("p b n -> p (b n)")
                        g = acc0[:, half * TILE:(half + 1) * TILE]
                        if norm:
                            s = dve.scalar_tensor_tensor(out=scr[half][:, :], in0=y, scalar=r, in1=g,
                                                         op0=ALU.mult, op1=ALU.mult)
                        else:
                            s = dve.tensor_tensor(scr[half][:, :], y, g, ALU.mult)
                    link(s)
                    for half in range(2):
                        xt = x[:, t, half * TILE:(half + 1) * TILE]
                        s = dve.tensor_tensor(xt, xt, scr[half][:, :], ALU.add)
                    s.then_inc(x_ready, 1)

            update(0, True, 2)
            make_diag(4, 1)
            scale_cols(M["a_sc2"], 2, 64)
            make_diag(5, 0)
            first_chunk(T_FF1, 8, M["x2"], lambda n: None)

            def gate_up_1(start, end, units):
                with dve.Fori(start, end) as i:
                    T = T_FF1 + CT + i * (2 * CT)
                    for n in range(CT):
                        lo(T, n + 3)
                        units(i, n)
                    up_act(i)
                    for n in range(CT, 2 * CT):
                        lo(T, n + 3)
                        units(i, n)

            def up_act(i):
                dve.wait_ge(tile_used, T_FF1 + 2 * CT + RING + i * (2 * CT))
                dve.wait_ge(pair_free[0], i + (USE0["gate1"] + 2))
                for t in range(NT):
                    s = dve.tensor_tensor(act_n[:, t, :], ps[:, 2 + t, :], sig[:, t, :], ALU.mult)
                s.then_inc(pair_free[1], 1)

            clear(acc0)
            dve.wait_ge(acc_bias[0], 48)

            def u_g2(i, n):
                if n % 2 == 0:
                    u = n // 2
                    unit(i * 8 + (UNITS * 5 + u), i * 4 + u // 2, u % 2, 0, acc0)

            gate_up_1(0, 4, u_g2)
            dve.wait_ge(post_landed, 32)
            gate_rows(M["a_g2"], post2)
            clear(acc1)
            clear(tmp)
            dve.wait_ge(acc_bias[1], 64)
            dve.wait_ge(acc_bias[2], 16)

            def u_sh1(i, n):
                if n % 2 == 0:
                    u = n // 2
                    unit(i * 8 + (UNITS * 6 + u - 32), i * 4 + (u // 2 - 16), u % 2, 1, acc1, tmp)

            gate_up_1(4, 8, u_sh1)
            shift_cols(M["b_sh1"], 5)
            shift_cols(M["b_sh1"] + 1, 7)
            clear(acc1)
            clear(tmp)
            gate_up_1(8, NCH - 1, lambda i, n: None)
            T = T_FF1 + CT + (NCH - 1) * 2 * CT
            for n in range(CT):
                lo(T, n + 3)
            up_act(NCH - 1)
            dve.wait_ge(acc_bias[1], 80)
            dve.wait_ge(acc_bias[2], 32)

            rows_first(F_DOWN1)
            with dve.Fori(0, 16) as i:
                rows_pair(T_DOWN1 + i * 4, F_DOWN1 + i * 2, i * 2,
                          lambda j: unit(i * 2 + (UNITS * 7 + j), i, j, 1, acc1, tmp) if j < 2 else None)
            with dve.Fori(16, FF1 // P // 2 - 1) as i:
                rows_pair(T_DOWN1 + i * 4, F_DOWN1 + i * 2, i * 2, none)
            i = FF1 // P // 2 - 1
            rows_pair(T_DOWN1 + 4 * i, F_DOWN1 + 2 * i, 2 * i, none, last=True)
            update(NT, True, 6)
            make_diag(8, 1)
            scale_cols(M["b_sc1"], 4, 80)
            scale_cols(M["b_sc1"] + 1, 6, 80)
            make_diag(9, 0)

            def ctx_rows(n):
                if n == 0:
                    make_diag(10, 3)
                    make_diag(11, 2)
                elif n >= 4:
                    split(24, M["ctx"], n - 4, hc_hi, hc_lo)

            first_chunk(T_QKV2, 16, M["lat"], lambda n: None, ctx_rows)
            clear(acc0)
            clear(acc1)
            dve.wait_ge(acc_bias[0], 64)
            dve.wait_ge(acc_bias[1], 96)
            dve.tensor_copy(stat[:, 62:63], stat[:, 63:64]).then_inc(sq_read, 1)

            def qkv2(i, following):
                T = T_QKV2 + i * (3 * CT)
                Mb = i * 7 + M["qkv2"]
                S = 3 + 3 * PER_GROUP
                off[0] = i * S if following else 0
                before = steps[0]

                def head_norm(dst, b, n, g):
                    dve.wait_ge(sq_ready, i * 3 + (n + 2))
                    ss = stat[:, 8:16]
                    dve.tensor_reduce(ss, p_t[:, :, :].rearrange("p t (h n) -> p (t h) n", n=HD), AX, ALU.add)\
                        .then_inc(head_ss, 1)
                    dve.wait_ge(head_std, i * 3 + (n + 1))
                    link(dve.reciprocal(stat[:, 24:32], stat[:, 16:24]), off[0])
                    for t in range(NT):
                        for h in range(GH):
                            c = t * GH + h
                            s = dve.scalar_tensor_tensor(out=dst[:, t, h * HD:(h + 1) * HD],
                                                         in0=ps[:, 2 * b + t, h * HD:(h + 1) * HD],
                                                         scalar=stat[:, 24 + c:25 + c], in1=g[:, :],
                                                         op0=ALU.mult, op1=ALU.mult)
                            if c == 0:
                                s.then_inc(sq_read, 1)
                    s.then_inc(pair_free[b], 1)

                def steps_of(n0):
                    for n in range(n0, n0 + CT):
                        lo(T, n + 3)
                        u = n - CT
                        unit(i * 16 + (UNITS * 8 + u), i * 4 + u // 4, u % 2, 1, (acc0, acc1)[u // 2 % 2])

                head_norm(nat_a, 2, 0, qg)
                steps_of(CT)
                head_norm(nat_b, 0, 1, kg)
                dve.wait_ge(tr_done[1], i * 7 + (M["qkv2"] + 1))
                head_norm(nat_a, 1, 2, kg)
                steps_of(2 * CT)
                softmax(i * PER_GROUP + UNITS1, Mb + 3, 2 * NT, bias_t, i * (32 * GH),
                        lambda u: lo(T, 3 * CT + u + 3) if following else None)
                assert steps[0] - before == S

            with dve.Fori(0, 3) as i:
                qkv2(i, True)
            off[0] = 0
            steps[0] += 2 * (3 + 3 * PER_GROUP)
            qkv2(3, False)
            off[0] = 0
            gate_rows(M["b_g1"])
            shift_cols(M["b_sh2"], 9)
            clear(acc1)
            dve.wait_ge(acc_bias[1], 112)
            rows_first(F_OUT2)
            with dve.Fori(0, KD // 2 - 1) as i:
                rows_pair(T_OUT2 + i * 4, F_OUT2 + i * 2, i * 2,
                          lambda j: unit(i * 4 + (UNITS * 10 + j), i * 2 + j // 2, j % 2, 1, acc1))
            i = KD // 2 - 1
            rows_pair(T_OUT2 + 4 * i, F_OUT2 + 2 * i, 2 * i,
                      lambda j: unit(4 * i + UNITS * 10 + j, 2 * i + j // 2, j % 2, 1, acc1), last=True)
            dve.wait_ge(tile_used, T_FF2 + RING)
            update(2 * NT, False)
            make_diag(12, 1)
            scale_cols(M["b_sc2"], 8, 96)
            make_diag(13, 0)

            first_chunk(T_FF2, 32, M["x7"], lambda n: None)
            clear(acc0)
            dve.wait_ge(acc_bias[0], 80)
            dve.tensor_copy(stat[:, 62:63], stat[:, 63:64]).then_inc(ff_ready, 1)

            def outer_taps(m_, col, groups, CV):
                for b in range(2):
                    gs = range(2 * b, min(2 * b + 2, groups))
                    dve.wait_ge(cv_ready, CV + gs[-1] + 1)
                    for g in gs:
                        z = ps[:, 6 + b, g % 2 * SEQ:(g % 2 + 1) * SEQ]
                        y = conv_t[:, g, 1:SEQ]
                        s = dve.scalar_tensor_tensor(out=y, in0=z[:, 0:SEQ - 1], scalar=fcw[:, 0, bass.ds(col + g, 1)],
                                                     in1=y, op0=ALU.mult, op1=ALU.add)
                    link(s, off[0])
                    for g in gs:
                        z = ps[:, 6 + b, g % 2 * SEQ:(g % 2 + 1) * SEQ]
                        y = conv_t[:, g, 0:SEQ - 1]
                        s = dve.scalar_tensor_tensor(out=y, in0=z[:, 1:SEQ], scalar=fcw[:, 2, bass.ds(col + g, 1)],
                                                     in1=y, op0=ALU.mult, op1=ALU.add)
                    s.then_inc(tr_free[b], 1)

            def times_gate(m_, i, groups):
                for b in range(2):
                    n = min(2, groups - 2 * b)
                    dve.wait_ge(tr_free[b], m_ + 1)
                    dve.wait_ge(sig_ready, i * 2 + (b + 1))
                    dve.tensor_tensor(ff[:, bass.ds(i * GH + 2 * b, n), :], conv_t[:, 2 * b:2 * b + n, :],
                                      gate_t[:, 2 * b:2 * b + n, :], ALU.mult).then_inc(ff_ready, 1)

            def gate_up_2(start, end, M_, units):
                S = 4
                with dve.Fori(start, end) as i:
                    off[0] = (i - start) * S
                    before = steps[0]
                    T = T_FF2 + CT + i * (2 * CT)
                    m_ = i * 2 + M_
                    for n in range(CT):
                        if n == 4:
                            outer_taps(m_, i * GH, GH, i * (2 * GH))
                        lo(T, n + 3)
                        units(i, n)
                    for n in range(CT, 2 * CT):
                        if n == CT + 4:
                            outer_taps(m_ + 1, i * GH + FF2 // P, GH, i * (2 * GH) + GH)
                            times_gate(m_ + 1, i, GH)
                        lo(T, n + 3)
                        units(i, n)
                    assert steps[0] - before == S
                steps[0] += (end - start - 1) * S
                off[0] = 0

            def u_g2b(i, n):
                if n % 2 == 0:
                    u = n // 2
                    unit(i * 8 + (UNITS * 11 + u), i * 4 + u // 2, u % 2, 1, acc0)

            gate_up_2(0, 4, M["ffn2a"], u_g2b)
            gate_rows(M["b_g2"])
            gate_up_2(4, NCH - 1, M["ffn2b"] - 8, lambda i, n: None)
            i = NCH - 1
            T = T_FF2 + CT + i * 2 * CT
            m_ = M["ffn2b"] - 8 + 2 * i
            for n in range(CT):
                if n == 4:
                    outer_taps(m_, i * GH, TAILC // P, i * 2 * GH)
                lo(T, n + 3)
            outer_taps(m_ + 1, i * GH + FF2 // P, TAILC // P, i * 2 * GH + TAILC // P)
            times_gate(m_ + 1, i, TAILC // P)
            K = FF2 // P
            dve.wait_ge(ff_ready, 2 * NCH + 1)
            rows_first(F_DOWN2)
            with dve.Fori(0, K // 2 - 1) as i:
                rows_pair(T_DOWN2 + i * 4, F_DOWN2 + i * 2, i * 2, none)
            i = K // 2 - 1
            lo(T_DOWN2 + 4 * i, 3)
            stage_lo(F_DOWN2 + 2 * i + 1, 1, ff[:, 2 * i + 1, :])
            lo(T_DOWN2 + 4 * i, 4)
            lo(T_DOWN2 + 4 * i, 5)
            stage_lo(F_DOWN2 + 2 * i + 2, 0, ff[:, 2 * i + 2, :])
            dve.wait_ge(tile_used, T_END + RING)
            update(3 * NT, False)

        @block.tensor
        def _(pe):
            pe.sem_inc(lo_ready, RING)
            pe.sem_inc(tile_used, RING)
            pe.sem_inc(ada_used, 2)
            for s in pair_free:
                pe.sem_inc(s, 1)

            def bank_free(b, m_):
                if not (isinstance(m_, int) and m_ == 0):
                    pe.wait_ge(tr_free[b], m_)

            def chunk_tile(T, j0, j, targets, width=C):
                s = (j0 + j) % RING
                pe.wait_ge(lo_ready, T + (j0 + j + 1 + RING))
                for (hi_, lo_, pair, use) in targets:
                    if j == 0:
                        pe.wait_ge(pair_free[pair], use + 1)
                    for kk in range(2):
                        k = 2 * j + kk
                        wh = w_hi[:, s, kk * width:(kk + 1) * width]
                        wl = w_lo[:, s, kk * width:(kk + 1) * width]
                        for t in range(NT):
                            o = ps[:, 2 * pair + t, 0:width]
                            a = slice(t * P, (t + 1) * P)
                            pe.matmul(o, hi_[:, k, a], wh, start=(k == 0), stop=False)
                            pe.matmul(o, hi_[:, k, a], wl, start=False, stop=False)
                            mm = pe.matmul(o, lo_[:, k, a], wh, start=False, stop=(k == KD - 1))
                mm.then_inc(tile_used, 1)

            def chunk(T, j0, targets, width=C, middle=None):
                for j in range(CT):
                    if j == 4 and middle is not None:
                        middle()
                    chunk_tile(T, j0, j, targets, width)

            def to_columns(src, m_, groups=GH):
                for b in range(2):
                    bank_free(b, m_)
                    for g in range(2 * b, min(2 * b + 2, groups)):
                        for t in range(NT):
                            mm = pe.transpose(ps[:, 6 + b, (g % 2 * NT + t) * P:(g % 2 * NT + t + 1) * P],
                                              src[:, t, g * P:(g + 1) * P], ident[:, :])
                    mm.then_inc(tr_done[b], 1)

            def sum_columns(acc, m_):
                for b in range(2):
                    bank_free(b, m_)
                    for k in range(8):
                        kk = 8 * b + k
                        mm = pe.matmul(ps[:, 6 + b, k:k + 1], acc[:, kk * P:(kk + 1) * P], ones[:, 0:1],
                                       start=True, stop=True)
                    mm.then_inc(tr_done[b], 1)

            def sum_rows(m_):
                for c in range(4):
                    b = c % 2
                    bank_free(b, m_ + c // 2)
                    pe.matmul(ps[:, 6 + b, :], ones[:, :], acc0[:, c * C:(c + 1) * C], start=True, stop=True)\
                        .then_inc(tr_done[b], 1)

            def scaled_rows(src, slot, m_, e, xn):
                for o in range(NT):
                    t = NT - 1 - o
                    pe.wait_ge(xn_ready, xn + o + 1)
                    bank_free(t, m_ + e)
                    for k in range(4):
                        kk = 4 * e + k
                        mm = pe.matmul(ps[:, 6 + t, k * P:(k + 1) * P], src(t)[:, kk * P:(kk + 1) * P],
                                       diag[:, slot + t, :], start=True, stop=True)
                    mm.then_inc(tr_done[t], 1)

            def first_chunk(T, targets, m_, xn, n0, extra=lambda j: None):
                rows = lambda e: scaled_rows(lambda t: x[:, t, :], 0, m_, e, xn)
                rows(0)
                rows(1)
                for j in range(CT):
                    if j == 1 or j == 3:
                        rows(2 + j // 2)
                    extra(j)
                    if j % 2 == 0:
                        pe.wait_ge(hlo_ready, n0 + j + 2)
                    chunk_tile(T, 0, j, targets)

            lat = (h_hi, h_lo)
            con = (hc_hi, hc_lo)

            pe.wait_ge(const_ready, 2)
            pe.wait_ge(vec_landed, 16 * 7)
            pe.transpose(ps[:, 6, 0:112], st_vec[:, :], ident[0:112, 0:112]).then_inc(tr_done[0], 1)
            pe.wait_ge(small_landed, 16 * 8)
            pe.transpose(ps[:, 7, 0:24], st_c24[:, :], ident[0:24, 0:24])
            for g in range(H1):
                mm = pe.transpose(ps[:, 7, 24 + g * TAPS:24 + (g + 1) * TAPS], st_cw[:, g * P:(g + 1) * P],
                                  ident[0:TAPS, 0:TAPS])
            mm.then_inc(tr_done[1], 1)
            bank_free(0, 1)
            for t in range(3):
                mm = pe.transpose(ps[:, 6, t * 86:(t + 1) * 86], st_fc[:, t, :], ident[0:86, 0:86])
            mm.then_inc(tr_done[0], 1)
            bank_free(1, 1)
            pe.transpose(ps[:, 7, 0:86], st_fc[:, 3, :], ident[0:86, 0:86]).then_inc(tr_done[1], 1)

            pe.wait_ge(ada_used, 2 + UNITS)
            sum_columns(acc1, M["a_sh1"])
            pe.wait_ge(ada_used, 2 + 2 * UNITS)
            sum_columns(acc0, M["a_sc1"])
            first_chunk(T_AG, [(*lat, 0, USE0["ag"])], M["x1"], 0, 0)
            for i in range(2):
                T = T_AG + i * (2 * CT)
                if i:
                    chunk(T, 0, [(*lat, 0, i + USE0["ag"])])
                chunk(T, CT, [(*lat, 1, i + USE1["ag"])])
                pe.wait_ge(pair_free[0], i + 2)
                to_columns(nat_b, i + M["u"])

            def attention(U, Mb, nkt, first, beside):
                def scores(u):
                    h, c = u // 2, u % 2
                    pe.matmul(ps[:, u % 2, 0:nkt * P], q_t[:, h, c * P:(c + 1) * P], k_t[:, h, 0:nkt * P],
                              start=True, stop=True).then_inc(s_done, 1)

                def values(u):
                    pe.wait_ge(tr_free[u % 2], Mb + (u // 2 + 1))
                    if u >= 2:
                        pe.wait_ge(o_used, U + (u - 1))
                    for k in range(nkt):
                        mm = pe.matmul(ps[:, 2 + u % 2, 0:P], v_n[:, k, u // 2 * HD:(u // 2 + 1) * HD],
                                       p_t[:, u % 2, k * P:(k + 1) * P], start=(k == 0), stop=(k == nkt - 1))
                    mm.then_inc(o_done, 1)

                for b in range(2):
                    pe.wait_ge(tr_free[b], Mb)
                first()
                scores(0)
                scores(1)
                for u in range(PER_GROUP):
                    beside(u)
                    pe.wait_ge(p_ready, U + (u + 1))
                    bank_free(u % 2, Mb + u // 2)
                    for k in range(nkt):
                        mm = pe.transpose(ps[:, 6 + u % 2, k * P:(k + 1) * P], prob[:, u % 2, k * P:(k + 1) * P],
                                          ident[:, :])
                    mm.then_inc(tr_done[u % 2], 1)
                    if u + 2 < PER_GROUP:
                        scores(u + 2)
                    if u >= 1:
                        values(u - 1)
                values(PER_GROUP - 1)
                pe.wait_ge(o_used, U + PER_GROUP)

            chunk(T_QKV1, 0, [(*lat, 2, USE2["q1"])])
            sum_rows(M["a_g1"])
            for i in range(2):
                T = T_QKV1 + i * (3 * CT)
                Mb = i * 6 + M["qkv1"]

                def q_columns():
                    pe.wait_ge(pair_free[2], i + (USE2["q1"] + 2))
                    to_columns(nat_a, Mb)

                def k_columns():
                    pe.wait_ge(pair_free[0], i + (USE0["k1"] + 2))
                    to_columns(nat_b, Mb + 1)
                    if i == 1:
                        pe.wait_ge(conv_step, DVE_CONV_OPS)
                        pe.wait_ge(conv_pool, POOL_CONV_OPS)
                        bank_free(0, M["ln"])
                        for g in range(H1):
                            mm = pe.matmul(ps[:, 6, 0:SEQ], mean1[:, :], ff[:, H1 + g, :], start=(g == 0), stop=(g == H1 - 1))
                        mm.then_inc(tr_done[0], 1)

                def v_written():
                    pe.wait_ge(pair_free[1], i + (USE1["v1"] + 2))

                chunk(T, CT, [(*lat, 0, i + USE0["k1"])], middle=q_columns)
                chunk(T, 2 * CT, [(*lat, 1, i + USE1["v1"])], middle=k_columns)
                if i == 0:
                    attention(0, Mb + 2, NT, v_written, lambda u: chunk_tile(T, 3 * CT, u, [(*lat, 2, USE2["q1"] + 1)]))
            pe.wait_ge(sq_ready, 1)
            bank_free(1, M["ln"])
            for g in range(H1):
                mm = pe.matmul(ps[:, 7, 0:SEQ], mean1[:, :], tmp[:, g * SEQ:(g + 1) * SEQ], start=(g == 0), stop=(g == H1 - 1))
            mm.then_inc(tr_done[1], 1)
            attention(PER_GROUP, M["att1"], NT, v_written, lambda u: None)
            pe.wait_ge(ada_used, 2 + 4 * UNITS)
            sum_columns(acc1, M["a_sh2"])

            def row_tile(T, k, F, first, last):
                pe.wait_ge(flo_ready, F + 1)
                for half in range(2):
                    s = (2 * k + half) % RING
                    pe.wait_ge(lo_ready, T + (half + 1 + RING))
                    for t in range(NT):
                        a = slice(t * P, (t + 1) * P)
                        for c in range(2):
                            o = ps[:, 4 * t + 2 * half + c, :]
                            wh, wl = w_hi[:, s, c * C:(c + 1) * C], w_lo[:, s, c * C:(c + 1) * C]
                            pe.matmul(o, f_hi[:, k % 2, a], wh, start=first, stop=False)
                            pe.matmul(o, f_hi[:, k % 2, a], wl, start=False, stop=False)
                            mm = pe.matmul(o, f_lo[:, k % 2, a], wh, start=False, stop=last)
                    mm.then_inc(tile_used, 1)

            def rows_phase(T0, F0, K, m_, uses):
                for b in range(2):
                    pe.wait_ge(tr_free[b], m_)
                for p_, u in enumerate(uses):
                    pe.wait_ge(pair_free[p_], u + 1)
                row_tile(T0, 0, F0, True, False)
                row_tile(T0 + 2, 1, F0 + 1, False, False)
                with pe.Fori(1, (K - 1) // 2) as i:
                    for k in range(2):
                        row_tile(T0 + 2 * k + i * 4, k, F0 + k + i * 2, False, False)
                for k in range((K - 1) // 2 * 2, K):
                    row_tile(T0 + 2 * k, k, F0 + k, False, k == K - 1)

            rows_phase(T_OUT1, F_OUT1, KD, M["a_sc2"], (4, 4, 2))

            pe.wait_ge(x_ready, 1)
            sum_columns(acc1, M["a_sc2"])
            pe.wait_ge(x_ready, NT)
            first_chunk(T_FF1, [(*lat, 0, USE0["gate1"])], M["x2"], 2, 8)

            def gate_up_1(start_, end, m_):
                with pe.Fori(start_, end) as i:
                    T = T_FF1 + CT + i * (2 * CT)

                    def act_columns():
                        pe.wait_ge(pair_free[1], i + (USE1["up1"] + 2))
                        to_columns(act_n, i + m_)

                    chunk(T, 0, [(*lat, 1, i + USE1["up1"])])
                    chunk(T, CT, [(*lat, 0, i + (USE0["gate1"] + 1))], middle=act_columns)

            gate_up_1(0, 4, M["ffn1a"])
            pe.wait_ge(ada_used, 2 + 6 * UNITS)
            sum_rows(M["a_g2"])
            gate_up_1(4, 8, M["ffn1b"] - 4)
            pe.wait_ge(ada_used, 2 + 7 * UNITS)
            sum_columns(acc1, M["b_sh1"])
            sum_columns(tmp, M["b_sh1"] + 1)
            gate_up_1(8, NCH - 1, M["ffn1c"] - 8)
            chunk(T_FF1 + CT + (NCH - 1) * 2 * CT, 0, [(*lat, 1, USE1["up1"] + NCH - 1)])
            pe.wait_ge(pair_free[1], USE1["up1"] + NCH + 1)
            to_columns(act_n, M["ffn1c"] + NCH - 9)
            rows_phase(T_DOWN1, F_DOWN1, FF1 // P, M["b_sc1"], (USE0["gate1"] + NCH, USE1["up1"] + NCH, 2))

            pe.wait_ge(x_ready, NT + 1)
            sum_columns(acc1, M["b_sc1"])
            sum_columns(tmp, M["b_sc1"] + 1)
            pe.wait_ge(x_ready, 2 * NT)

            def ctx_rows(e):
                scaled_rows(lambda t: ctx_n[t], 2, M["ctx"], e, 6)

            first_chunk(T_QKV2, [(*lat, 2, USE2["qkv2"])], M["lat"], 4, 16,
                        lambda j: ctx_rows(j - 5) if j >= 5 else None)
            ctx_rows(3)
            pe.wait_ge(hlo_ready, 32)

            def qkv2(i, following):
                T = T_QKV2 + i * (3 * CT)
                Mb = i * 7 + M["qkv2"]

                def q_columns():
                    pe.wait_ge(pair_free[2], i * 2 + (USE2["qkv2"] + 2))
                    to_columns(nat_a, Mb)

                def k_columns():
                    pe.wait_ge(pair_free[0], i * 2 + (USE0["qkv2"] + 2))
                    to_columns(nat_b, Mb + 1)
                    pe.wait_ge(pair_free[1], i + (USE1["kc2"] + 2))
                    to_columns(nat_a, Mb + 2)

                def v_written():
                    pe.wait_ge(pair_free[2], i * 2 + (USE2["qkv2"] + 3))
                    pe.wait_ge(pair_free[0], i * 2 + (USE0["qkv2"] + 3))

                chunk(T, CT, [(*lat, 0, i * 2 + USE0["qkv2"]), (*con, 1, i + USE1["kc2"])], middle=q_columns)
                chunk(T, 2 * CT, [(*lat, 2, i * 2 + (USE2["qkv2"] + 1)), (*con, 0, i * 2 + (USE0["qkv2"] + 1))],
                      middle=k_columns)
                attention(i * PER_GROUP + UNITS1, Mb + 3, 2 * NT, v_written,
                          lambda u: chunk_tile(T, 3 * CT, u, [(*lat, 2, i * 2 + (USE2["qkv2"] + 2))]) if following else None)

            with pe.Fori(0, 3) as i:
                qkv2(i, True)
            qkv2(3, False)
            sum_rows(M["b_g1"])
            sum_columns(acc1, M["b_sh2"])
            rows_phase(T_OUT2, F_OUT2, KD, M["b_sc2"], (USE0["gate2"], USE1["up2"], USE2["qkv2"] + 8))

            pe.wait_ge(x_ready, 2 * NT + 1)
            sum_columns(acc1, M["b_sc2"])
            pe.wait_ge(x_ready, 3 * NT)
            first_chunk(T_FF2, [(*lat, 0, USE0["gate2"])], M["x7"], 8, 32)

            def gate_columns(i, m_, groups=GH):
                pe.wait_ge(pair_free[0], i + (USE0["gate2"] + 2))
                to_columns(sig, i * 2 + m_, groups)

            def up_columns(i, m_, groups=GH):
                pe.wait_ge(pair_free[1], i + (USE1["up2"] + 2))
                to_columns(act_n, i * 2 + (m_ + 1), groups)

            for start_, end, m_ in ((0, 4, M["ffn2a"]), (4, NCH - 2, M["ffn2b"] - 8)):
                with pe.Fori(start_, end) as i:
                    T = T_FF2 + CT + i * (2 * CT)
                    chunk(T, 0, [(*lat, 1, i + USE1["up2"])], middle=lambda: gate_columns(i, m_))
                    chunk(T, CT, [(*lat, 0, i + (USE0["gate2"] + 1))], middle=lambda: up_columns(i, m_))
                if end == 4:
                    pe.wait_ge(ada_used, 2 + 12 * UNITS)
                    sum_rows(M["b_g2"])
            i = NCH - 2
            T = T_FF2 + CT + i * 2 * CT
            chunk(T, 0, [(*lat, 1, i + USE1["up2"])], middle=lambda: gate_columns(i, m_))
            chunk(T, CT, [(*lat, 0, i + USE0["gate2"] + 1)], TAILC, middle=lambda: up_columns(i, m_))
            chunk(T + 2 * CT, 0, [(*lat, 1, i + 1 + USE1["up2"])], TAILC, middle=lambda: gate_columns(i + 1, m_, TAILC // P))
            up_columns(NCH - 1, m_, TAILC // P)
            rows_phase(T_DOWN2, F_DOWN2, FF2 // P, M["ffn2b"] - 8 + 2 * NCH,
                       (USE0["gate2"] + NCH, USE1["up2"] + NCH, USE2["qkv2"] + 8))


_INS = ["x", "c", "ada_w", "ada_b", "mix_pre_g", "mix_post_g", "w_in", "conv_w", "conv_b", "conv_ln_g", "conv_ln_b",
        "w_out", "ffn_pre_g", "ffn_post_g", "w_gate", "w_up", "w_down", "c_2", "ctx_2", "c_ctx_2", "norm_mix_g_2",
        "norm_ffn_g_2", "w_ada_2", "b_ada_2", "na_w_qkv_2", "na_q_g_2", "na_k_g_2", "na_rpb_2", "na_w_o_2",
        "ffn_w_up_2", "ffn_conv_w_2", "ffn_conv_b_2", "ffn_w_down_2"]


def kernel(**inputs):
    import numpy as np
    import concourse.bacc as bacc
    from concourse.bass_utils import run_bass_kernel_spmd

    nc = bacc.Bacc("TRN2", target_bir_lowering=False, num_devices=1)
    arrays, ins = {}, {}
    for name in _INS:
        a = np.ascontiguousarray(inputs[name])
        arrays[f"in_{name}"] = a
        ins[name] = nc.dram_tensor(f"in_{name}", a.shape, mybir.dt.from_np(a.dtype), kind="ExternalInput").ap()
    out = nc.dram_tensor("out", (1, SEQ, D), F32, kind="ExternalOutput").ap()
    program(nc, ins, out)
    r = run_bass_kernel_spmd(nc, [arrays], core_ids=[0])
    return r.results[0]["out"]
```

```python
from contextlib import ExitStack

import concourse.bass as bass
from concourse import mybir

F32 = mybir.dt.float32
F32R = mybir.dt.float32r
ALU = mybir.AluOpType
ACT = mybir.ActivationFunctionType
AX = mybir.AxisListType.X

P = 128
D = 2048
KD = D // P
SEQ = 256
NT = SEQ // P
HD = 128
C = 512
GH = C // HD
TILE = 1024
RING = 4
CT = KD * C // TILE
H1 = 8
TAPS = 31
FF1 = 5632
FF2 = 5504
NCH = FF1 // C
TAILC = FF2 - (NCH - 1) * C
H2 = 16
GRID = 64
ROWS = SEQ // GRID
RPB_H, RPB_W = 15, 31
DR = 2 * ROWS - 1
LANES = 2 * GRID
NEG = -1e30
SCALE = float(HD) ** -0.5
RMS_EPS = 1e-6
LN_EPS = 1e-5

T_AG = 0
T_QKV1 = T_AG + 4 * CT
T_OUT1 = T_QKV1 + 6 * CT
T_FF1 = T_OUT1 + 2 * KD
T_DOWN1 = T_FF1 + 2 * NCH * CT
T_QKV2 = T_DOWN1 + 2 * (FF1 // P)
T_OUT2 = T_QKV2 + 12 * CT
T_FF2 = T_OUT2 + 2 * KD
T_DOWN2 = T_FF2 + 2 * NCH * CT
T_END = T_DOWN2 + 2 * (FF2 // P)

UNITS = 2 * KD


def program(nc, ins, out):
    ctx = ExitStack()
    with ctx:
        names = [0]
        base = -(-nc.sbuf_base // 64) * 64

        def at(name, shape, offset, dt=F32):
            return nc.alloc_sbuf_tensor_at(name, shape, dt, offset=base + offset)

        KB = 1024
        x = at("x", [P, NT, D], 0)
        tmp = at("tmp", [P, D], 16 * KB)
        nat_a = at("nat_a", [P, NT, C], 16 * KB)
        nat_b = at("nat_b", [P, NT, C], 20 * KB)
        prob = at("prob", [P, 2, C], 20 * KB)
        prob_1 = at("prob_1", [P, 4, SEQ], 20 * KB)
        h_hi = at("h_hi", [P, KD, SEQ], 24 * KB, F32R)
        h_lo = at("h_lo", [P, KD, SEQ], 40 * KB, F32R)
        junk = at("junk", [P, D], 40 * KB)
        raw = at("raw", [P, RING, TILE], 56 * KB)
        w_hi = at("w_hi", [P, RING, TILE], 72 * KB, F32R)
        w_lo = at("w_lo", [P, RING, TILE], 88 * KB, F32R)
        ada = at("ada", [P, 2, TILE], 104 * KB)
        start = [at(f"start{n}", [P, 2, TILE], a * KB) for n, a in enumerate((16, 104, 136, 144))]
        acc0 = at("acc0", [P, D], 112 * KB)
        acc1 = at("acc1", [P, D], 120 * KB)
        ff = at("ff", [P, 48, SEQ], 128 * KB)
        hc_hi = at("hc_hi", [P, KD, SEQ], 144 * KB, F32R)
        hc_lo = at("hc_lo", [P, KD, SEQ], 160 * KB, F32R)
        PADT = TAPS - 1 + SEQ
        u_pad = at("u_pad", [P, H1, PADT], 144 * KB)
        causal = at("causal", [P, NT, SEQ], 154 * KB)
        cvec = at("cvec", [P, 24 + H1 * TAPS], 156 * KB)
        mean1 = at("mean1", [P, P], 158 * KB)
        rstd_ln = at("rstd_ln", [P, SEQ], 159 * KB)
        st_vec = at("st_vec", [112, P], 128 * KB)
        st_c24 = at("st_c24", [24, P], 128 * KB + 512)
        st_cw = at("st_cw", [TAPS, H1 * P], 129 * KB)
        st_fc = at("st_fc", [86, 4, P], 133 * KB)
        taps = at("taps", [P, 6, SEQ], 170 * KB)
        E = 176 * KB
        q_t = at("q_t", [P, GH, SEQ], E)
        k_t = at("k_t", [P, GH, 2 * SEQ], E + 4 * KB)
        v_n = at("v_n", [P, 2 * NT, C], E + 12 * KB)
        p_t = at("p_t", [P, 2, C], E + 20 * KB)
        bias_t = at("bias_t", [P, 2, SEQ], E + 24 * KB)
        diag = at("diag", [P, 4, P], E + 24 * KB)
        ctx_n = [at("ctx_n0", [P, D], E + 8 * KB), at("ctx_n1", [P, D], E - 4 * KB)]
        scr = [at("scr0", [P, TILE], E + 4 * KB), at("scr1", [P, TILE], E + 20 * KB)]
        post1 = at("post1", [P, D], 162 * KB)
        post2 = at("post2", [P, D], E + 8 * KB)
        sig = at("sig", [P, NT, C], E)
        conv_t = at("conv_t", [P, GH, SEQ], E + 8 * KB)
        gate_t = at("gate_t", [P, GH, SEQ], E + 12 * KB)
        f_hi = at("f_hi", [P, 2, SEQ], E + 16 * KB, F32R)
        f_lo = at("f_lo", [P, 2, SEQ], E + 18 * KB, F32R)
        h_f = at("h_f", [P, 2, C], E + 20 * KB)
        tab = at("tab", [DR * H2, LANES], E + 16 * KB)
        skew_s = at("skew_s", [GRID, H2 * DR, GRID], 144 * KB)
        S0 = 202 * KB
        ident = at("ident", [P, P], S0)
        ones = at("ones", [P, P], S0 + 512)
        vecs = at("vecs", [P, 112], S0 + 1024)
        cact = at("cact", [P, 48], S0 + 1472)
        fcw = at("fcw", [P, 4, 86], S0 + 1664)
        qg = at("qg", [P, HD], S0 + 3040)
        kg = at("kg", [P, HD], S0 + 3552)
        cols = at("cols", [P, 10, KD], S0 + 4064)
        stat = at("stat", [P, 64], S0 + 4704)
        eps_rms = at("eps_rms", [P, 1], S0 + 4960)
        eps_ln = at("eps_ln", [P, 1], S0 + 4992)
        assert base + S0 + 5024 <= nc.sbuf_usable_end

        ps = ctx.enter_context(nc.psum_tensor("ps", [P, 8, C], F32))

        table_d = nc.dram_tensor("rpb_table", (H2 * DR, GRID, LANES), F32, kind="Internal").ap()
        skew_d = nc.dram_tensor("rpb_skewed", (GRID, H2 * DR, GRID), F32, kind="Internal").ap()

        TABLE_PARTS = 8
        TABLE_ROWS = H2 * DR // TABLE_PARTS
        TABLE_DMAS = H2 + 2 * TABLE_PARTS + 1

        def sem(name):
            return ctx.enter_context(nc.semaphore(name))

        raw_landed = [sem(f"raw_landed{i}") for i in range(RING)]
        hi_ready = sem("hi_ready")
        lo_ready = sem("lo_ready")
        tile_used = sem("tile_used")
        ada_landed = [sem(f"ada_landed{i}") for i in range(2)]
        start_landed = [sem(f"start_landed{i}") for i in range(4)]
        start_step = sem("start_step")
        ada_used = sem("ada_used")
        acc_clear = sem("acc_clear")
        acc_bias = [sem(f"acc_bias{i}") for i in range(3)]
        vec_landed = sem("vec_landed")
        small_landed = sem("small_landed")
        x_landed = sem("x_landed")
        ctx_landed = sem("ctx_landed")
        post_landed = sem("post_landed")
        out_landed = sem("out_landed")
        const_ready = sem("const_ready")
        pool_step = sem("pool_step")
        table_landed = sem("table_landed")
        bias_landed = [sem(f"bias_landed{i}") for i in range(2)]
        tr_done = [sem(f"tr_done{i}") for i in range(2)]
        tr_free = [sem(f"tr_free{i}") for i in range(2)]
        pair_free = [sem(f"pair_free{i}") for i in range(3)]
        cact_ready = sem("cact_ready")
        ss_ready = sem("ss_ready")
        xn_ready = sem("xn_ready")
        hhi_ready = sem("hhi_ready")
        hlo_ready = sem("hlo_ready")
        sig_ready = sem("sig_ready")
        conv_step = sem("conv_step")
        conv_prod = sem("conv_prod")
        conv_pool = sem("conv_pool")
        std_ready = sem("std_ready")
        head_ss = sem("head_ss")
        head_std = sem("head_std")
        dev_ready = sem("dev_ready")
        sq_ready = sem("sq_ready")
        sq_read = sem("sq_read")
        ln_ready = sem("ln_ready")
        silu_done = sem("silu_done")
        s_done = sem("s_done")
        max_ready = sem("max_ready")
        exp_ready = sem("exp_ready")
        p_ready = sem("p_ready")
        o_done = sem("o_done")
        o_used = sem("o_used")
        fhi_ready = sem("fhi_ready")
        flo_ready = sem("flo_ready")
        cv_ready = sem("cv_ready")
        taps_ready = sem("taps_ready")
        ff_ready = sem("ff_ready")
        x_ready = sem("x_ready")
        dve_step = sem("dve_step")
        act_step = sem("act_step")

        M, m = {}, 0
        for name, n in (("vec", 2), ("start", 6), ("att1a", 4), ("a_g1", 2),
                        ("ln", 1), ("att1", 4), ("a_sh2", 1), ("a_sc2", 1), ("x2", 4), ("a_g2", 2),
                        ("b_sh1", 2), ("b_sc1", 2), ("lat", 4), ("ctx", 4),
                        ("qkv2", 28), ("b_g1", 2), ("b_sh2", 1), ("b_sc2", 1), ("x7", 4),
                        ("b_g2", 2), ("end", 0)):
            M[name] = m
            m += n
        USE0 = {"a0": 0, "k1": 1, "gate1": 3, "qkv2": 3 + NCH, "gate2": 11 + NCH}
        USE1 = {"g": 0, "v1": 2, "up1": 4, "kc2": 4 + NCH, "up2": 8 + NCH}
        USE2 = {"a1": 0, "q1": 1, "qkv2": 3}
        F_OUT1, F_DOWN1 = 0, KD
        F_OUT2 = F_DOWN1 + FF1 // P
        F_DOWN2 = F_OUT2 + KD
        UNITS1 = 16
        PER_GROUP = 2 * GH

        CONV_PRODUCTS = [(tap, pair) for tap in range(TAPS) for pair in range(2)] + [(tap, 2) for tap in range(TAPS)]
        CONV_SUMS = 3 * (TAPS - 1)
        DVE_CONV = (6, 7)
        DVE_CONV_OPS = len(DVE_CONV) * TAPS

        def conv_operands(c, tap):
            return (ff[:, H1 + c, :], u_pad[:, c, tap:tap + SEQ],
                    cvec[:, 3 * H1 + c * TAPS + tap:3 * H1 + c * TAPS + tap + 1])

        def prob_of(u, nkt):
            return prob_1[:, u % 4, :] if nkt == NT else prob[:, u % 2, :]

        HALVES = 2
        HK = KD // HALVES
        BLOCKS = KD // 2
        HOPS = 2 * KD
        HTILES = 3 * HK // 2
        START_TILES = HALVES * HTILES

        EARLY_UNITS = 2 * UNITS - 7 * CT

        block = ctx.enter_context(nc.Block())

        @block.sync
        def _(sp):
            def tile_cols(T, j, w, j2, col, width=C):
                s = j % RING
                dst = raw[:, s, 0:2 * width].rearrange("p (k n) -> p k n", k=2)
                src = w.rearrange("(k p) n -> p k n", p=P)[:, 2 * j2:2 * j2 + 2, bass.ds(col, width)]
                sp.wait_ge(lo_ready, T + j + 1)
                sp.dma_start(dst, src).then_inc(raw_landed[s], 16)

            def tile_rows(T, j, w, row):
                s = j % RING
                src = w[bass.ds(row, P), j % 2 * TILE:(j % 2 + 1) * TILE]
                sp.wait_ge(lo_ready, T + j + 1)
                sp.dma_start(raw[:, s, :], src).then_inc(raw_landed[s], 16)

            def unit(w, sec, n, row, half):
                src = w[bass.ds(row, P), sec * D + half * TILE:sec * D + (half + 1) * TILE]
                sp.wait_ge(ada_used, n + 1)
                sp.dma_start(ada[:, half, :], src).then_inc(ada_landed[half], 16)

            def bias_row(n, which, b, sec):
                acc = (acc0, acc1, tmp)[which]
                sp.wait_ge(acc_clear, n)
                sp.dma_start(acc[0:1, :], b[0:1, sec * D:(sec + 1) * D]).then_inc(acc_bias[which], 16)

            w_in, w_out1, w_gate, w_up1, w_down1 = (ins[k][0] for k in ("w_in", "w_out", "w_gate", "w_up", "w_down"))
            w_qkv, w_o2, w_up2, w_down2 = (ins[k][0] for k in ("na_w_qkv_2", "na_w_o_2", "ffn_w_up_2", "ffn_w_down_2"))
            ada1, ada2 = ins["ada_w"][0], ins["w_ada_2"][0]
            b1, b2 = ins["ada_b"], ins["b_ada_2"]

            bias_row(1, 1, b1, 0)
            bias_row(2, 0, b1, 1)
            def ag_col(i, g):
                return (3 + g) * H1 * HD + C * i

            sp.wait_ge(vec_landed, 16 * 7)
            def start_tile(n):
                tile_cols(T_AG, n, w_in, n // 3, ag_col(*((0, 0), (0, 1), (1, 0))[n % 3]))

            for s in range(HALVES):
                for p_ in range(BLOCKS * s, BLOCKS * (s + 1)):
                    q = p_ % BLOCKS
                    if q == BLOCKS - 1:
                        for n in range(RING):
                            start_tile(HTILES * s + n)
                    for sec in range(2):
                        slot = p_ % 2 * 2 + sec
                        if p_ >= 2:
                            sp.wait_ge(start_step, 4 * (p_ - 1))
                        src = ada1[2 * q * P:2 * (q + 1) * P, sec * D + s * TILE:sec * D + (s + 1) * TILE]
                        sp.dma_start(start[slot][:, :, :], src.rearrange("(k p) n -> p k n", p=P))\
                            .then_inc(start_landed[slot], 16)
                    if s and 1 <= q <= RING:
                        start_tile(HTILES * s - RING + q - 1)
                for n in range(RING, 2 * RING):
                    start_tile(HTILES * s + n)

            def qkv1(i, j):
                tile_cols(T_QKV1 + 3 * CT * i, j, w_in, j % CT, j // CT * H1 * HD + C * i)

            def mixer_unit(n):
                unit(ada1, 2 + n // UNITS, UNITS * 2 + n, n % UNITS // 2 * P, n % 2)

            bias_row(3, 0, b1, 2)
            bias_row(4, 1, b1, 3)
            sp.wait_ge(start_step, HALVES * HOPS)
            for n in range(EARLY_UNITS):
                mixer_unit(n)
                if n % 2:
                    start_tile(START_TILES - RING + n // 2)
            for j in range(3):
                tile_cols(T_AG, START_TILES + j, w_in, j, ag_col(1, 1))
            for n in range(CT):
                if n + 3 < CT:
                    tile_cols(T_AG, START_TILES + n + 3, w_in, n + 3, ag_col(1, 1))
                else:
                    qkv1(0, n + 3 - CT)
                mixer_unit(EARLY_UNITS + n)
            for i in range(2):
                for n in range(3 * CT):
                    j = n + 3
                    if j < 3 * CT:
                        qkv1(i, j)
                    elif i == 0:
                        qkv1(1, j - 3 * CT)
                    else:
                        tile_rows(T_OUT1, j - 3 * CT, w_out1, (j - 3 * CT) // 2 * P)
                    mixer_unit(EARLY_UNITS + CT + 3 * CT * i + n)

            def rows_pairs(T0, w, pairs, per_pair=0, sec=0, n0=0, ada_w=None, start=0):
                with sp.Fori(start, pairs) as i:
                    for j in range(4):
                        tile_rows(T0 + i * 4, j + 3, w, i * (2 * P) + (j + 3) // 2 * P)
                        if j < per_pair:
                            unit(ada_w, sec, n0 + i * per_pair + j, i * (per_pair // 2 * P) + j // 2 * P, j % 2)

            bias_row(5, 1, b1, 4)
            rows_pairs(T_OUT1, w_out1, KD // 2 - 1, 4, 4, UNITS * 4, ada1)

            def gate_up(T0, w_g, w_u, off):
                def one(i, j):
                    if j < CT:
                        tile_cols(T0 + CT + i * (2 * CT), j, w_u, j, off + i * C)
                    else:
                        tile_cols(T0 + CT + i * (2 * CT), j, w_g, j - CT, i * C + C)
                return one

            def last_pair_of_rows(T0, w, K, units, head):
                i = K // 2 - 1
                for j in range(4):
                    if j == 0:
                        tile_rows(T0 + 4 * i, 3, w, (2 * i + 1) * P)
                    else:
                        head(j - 1)
                    units(j)

            last_pair_of_rows(T_OUT1, w_out1, KD,
                              lambda j: unit(ada1, 4, UNITS * 5 - 4 + j, (KD - 2 + j // 2) * P, j % 2),
                              lambda j: tile_cols(T_FF1, j, w_gate, j, 0))

            one = gate_up(T_FF1, w_gate, w_up1, 0)
            for j in range(3, CT):
                tile_cols(T_FF1, j, w_gate, j, 0)
            for j in range(3):
                one(0, j)
            bias_row(6, 0, b1, 5)

            def ff1_loop(start, end, w, sec, n0):
                with sp.Fori(start, end) as i:
                    for n in range(2 * CT):
                        j = n + 3
                        if j < 2 * CT:
                            one(i, j)
                        else:
                            one(i + 1, j - 2 * CT)
                        if w is not None and n % 2 == 0:
                            u = n // 2
                            unit(w, sec, n0 + (i - start) * 8 + u, (i - start) * (4 * P) + u // 2 * P, u % 2)

            ff1_loop(0, 4, ada1, 5, UNITS * 5)
            bias_row(7, 1, b2, 0)
            bias_row(8, 2, b2, 0)
            ff1_loop(4, 8, ada2, 0, UNITS * 6)
            ff1_loop(8, NCH - 1, None, 0, 0)
            for j in range(3, CT):
                one(NCH - 1, j)
            for j in range(3):
                tile_rows(T_DOWN1, j, w_down1, j // 2 * P)
            bias_row(9, 1, b2, 1)
            bias_row(10, 2, b2, 1)
            rows_pairs(T_DOWN1, w_down1, 16, 2, 1, UNITS * 7, ada2)
            rows_pairs(T_DOWN1, w_down1, FF1 // P // 2 - 1, start=16)

            def qkv2(i, j):
                tile_cols(T_QKV2 + i * (3 * CT), j, w_qkv, j % CT, i * C + j // CT * D)

            last_pair_of_rows(T_DOWN1, w_down1, FF1 // P, lambda j: None, lambda j: qkv2(0, j))

            def qkv2_group(i, following, n0=0):
                for n in range(n0, 3 * CT):
                    j = n + 3
                    if j < 3 * CT:
                        qkv2(i, j)
                    else:
                        following(j - 3 * CT)
                    if n >= CT:
                        u = n - CT
                        unit(ada2, 2 + u // 2 % 2, i * 16 + (UNITS * 8 + u), i * (4 * P) + u // 4 * P, u % 2)

            for n in range(CT):
                qkv2(0, n + 3)
            bias_row(11, 0, b2, 2)
            bias_row(12, 1, b2, 3)
            qkv2_group(0, lambda j: qkv2(1, j), CT)
            with sp.Fori(1, 3) as i:
                qkv2_group(i, lambda j: qkv2(i + 1, j))
            qkv2_group(3, lambda j: tile_rows(T_OUT2, j, w_o2, j // 2 * P))
            bias_row(13, 1, b2, 4)
            rows_pairs(T_OUT2, w_o2, KD // 2 - 1, 4, 4, UNITS * 10, ada2)
            last_pair_of_rows(T_OUT2, w_o2, KD,
                              lambda j: unit(ada2, 4, UNITS * 11 - 4 + j, (KD - 2 + j // 2) * P, j % 2),
                              lambda j: tile_cols(T_FF2, j, w_up2, j, 0))
            one = gate_up(T_FF2, w_up2, w_up2, FF2)
            for j in range(3, CT):
                tile_cols(T_FF2, j, w_up2, j, 0)
            for j in range(3):
                one(0, j)
            bias_row(14, 0, b2, 5)
            ff1_loop(0, 4, ada2, 5, UNITS * 11)
            ff1_loop(4, NCH - 2, None, 0, 0)
            LASTP = NCH - 2
            TT = T_FF2 + CT + LASTP * 2 * CT

            def tail(j):
                if j < CT:
                    one(LASTP, j)
                elif j < 2 * CT:
                    tile_cols(TT, j, w_up2, j - CT, (NCH - 1) * C, TAILC)
                elif j < 3 * CT:
                    tile_cols(TT, j, w_up2, j - 2 * CT, FF2 + (NCH - 1) * C, TAILC)

            for j in range(3, 3 * CT):
                tail(j)
            for j in range(3):
                tile_rows(T_DOWN2, j, w_down2, j // 2 * P)
            rows_pairs(T_DOWN2, w_down2, FF2 // P // 2 - 1)
            LP = FF2 // P // 2 - 1
            for j in range(3, 6):
                tile_rows(T_DOWN2 + 4 * LP, j, w_down2, (2 * LP + j // 2) * P)
            for o in range(NT):
                t = NT - 1 - o
                sp.wait_ge(x_ready, 3 * NT + o + 1)
                sp.dma_start(out[0, t * P:(t + 1) * P, :], x[:, t, :]).then_inc(out_landed, 16)
            sp.wait_ge(out_landed, 16 * NT)

        @block.gpsimd
        def _(pool):
            steps = [0]

            def link(ins_):
                steps[0] += 1
                ins_.then_inc(pool_step, 1)
                pool.wait_ge(pool_step, steps[0])

            link(pool.memset(ident[:, :], 0.0))
            pool.memset(eps_rms[:, :], RMS_EPS)
            pool.memset(eps_ln[:, :], LN_EPS)
            pool.memset(ones[:, :], 1.0).then_inc(const_ready, 1)
            pool.affine_select(out=ident[:, :], in_=ident[:, :], compare_op=ALU.not_equal, fill=1.0, base=0,
                               pattern=[[-1, P]], channel_multiplier=1).then_inc(const_ready, 1)
            pool.memset(mean1[:, :], 1.0 / (H1 * HD)).then_inc(const_ready, 1)
            link(pool.memset(causal[:, :, :], 0.0))
            pool.affine_select(out=causal[:, :, :], in_=causal[:, :, :], compare_op=ALU.is_ge, fill=NEG, base=0,
                               pattern=[[P, NT], [-1, SEQ]], channel_multiplier=1).then_inc(const_ready, 1)

            for j in range(START_TILES):
                pool.wait_ge(hi_ready, T_AG + j + 1)
                pool.tensor_tensor(w_lo[:, j % RING, :], raw[:, j % RING, :], w_hi[:, j % RING, :].bitcast(F32),
                                   ALU.subtract).then_inc(lo_ready, 1)

            pool.wait_ge(start_step, HALVES * HOPS)
            pool.memset(u_pad[:, :, 0:TAPS - 1], 0.0).then_inc(const_ready, 1)

            def add_product(a, r, pair, ahead, behind):
                dst = ff[:, H1 + 2 * pair:H1 + 2 * pair + 2, :]
                pool.wait_ge(conv_prod, a + (ahead + 1))
                pool.wait_ge(conv_pool, a + (3 - behind))
                pool.tensor_tensor(dst, dst, taps[:, 2 * (r % 3):2 * (r % 3) + 2, :], ALU.add).then_inc(conv_pool, 1)

            with pool.Fori(0, 2 * (TAPS - 1) // 6) as i:
                for r in range(6):
                    add_product(i * 6 + r, r, r % 2, 2, 2)
            with pool.Fori(2 * (TAPS - 1) // 3, CONV_SUMS // 3) as i:
                for r in range(3):
                    add_product(i * 3 + r, r, 2, 3, 1)

            pool.wait_ge(x_ready, NT)
            link(pool.memset(tab[:, :], 0.0))
            rpb = ins["na_rpb_2"][0]
            lo_dr, lane = RPB_H // 2 - (ROWS - 1), GRID - 1 - RPB_W // 2
            for h in range(H2):
                pool.dma_start(tab[h * DR:(h + 1) * DR, lane:lane + RPB_W],
                               rpb[h, lo_dr:lo_dr + DR, :]).then_inc(table_landed, 16)
            pool.wait_ge(table_landed, 16 * H2)
            for n in range(TABLE_PARTS):
                h = slice(n * TABLE_ROWS, (n + 1) * TABLE_ROWS)
                pool.dma_start(table_d[h], tab[h, :].unsqueeze(1).broadcast_to([TABLE_ROWS, GRID, LANES]))\
                    .then_inc(table_landed, 16)
                pool.wait_ge(table_landed, 16 * (H2 + n + 1))
            for n in range(TABLE_PARTS):
                src = bass.AP(table_d.tensor, n * TABLE_ROWS * GRID * LANES + GRID - 1,
                              [[LANES - 1, GRID], [GRID * LANES, TABLE_ROWS], [1, GRID]])
                pool.dma_start(skew_s[:, n * TABLE_ROWS:(n + 1) * TABLE_ROWS, :], src).then_inc(table_landed, 16)
                pool.wait_ge(table_landed, 16 * (H2 + TABLE_PARTS + n + 1))
            W, WH = 16, 8
            v = skew_s[:, :, 0:GRID - W]
            link(pool.affine_select(out=v, in_=v, compare_op=ALU.is_ge, fill=NEG, base=WH,
                                    pattern=[[0, H2 * DR], [1, GRID - W]], channel_multiplier=-1))
            v = skew_s[:, :, W:GRID]
            link(pool.affine_select(out=v, in_=v, compare_op=ALU.is_gt, fill=NEG, base=WH - W,
                                    pattern=[[0, H2 * DR], [-1, GRID - W]], channel_multiplier=1))
            pool.dma_start(skew_d, skew_s[:, :, :]).then_inc(table_landed, 16)
            pool.wait_ge(table_landed, 16 * TABLE_DMAS)

            pool.wait_ge(hlo_ready, 32)

            def unit_bias(i, u):
                c = u % 2
                pool.wait_ge(max_ready, i * PER_GROUP + (UNITS1 + u - 1))
                for r in range(2):
                    src = skew_d[:, bass.ds(i * (GH * DR) + (u // 2 * DR + ROWS - 1 - 2 * c - r), ROWS), :]
                    pool.dma_start(bias_t[r * GRID:(r + 1) * GRID, c, :],
                                   src.rearrange("p a b -> p (a b)")).then_inc(bias_landed[c], 16)

            with pool.Fori(0, 4) as i:
                for u in range(PER_GROUP):
                    unit_bias(i, u)

        @block.scalar
        def _(act):
            steps = [0]

            def link(ins_):
                steps[0] += 1
                ins_.then_inc(act_step, 1)
                act.wait_ge(act_step, steps[0])

            def hi(T, j):
                s = j % RING
                act.wait_ge(raw_landed[s], T * (16 // RING) + 16 * (j // RING + 1))
                act.wait_ge(tile_used, T + j + 1)
                act.activation(w_hi[:, s, :], raw[:, s, :], ACT.Copy).then_inc(hi_ready, 1)

            def chunk_wait(T, j):
                act.wait_ge(tile_used, T + (j + RING))

            act.wait_ge(const_ready, 1)
            rows = ("c", "c_2", "c_ctx_2", "mix_pre_g", "ffn_pre_g", "norm_mix_g_2", "norm_ffn_g_2")
            for n, name in enumerate(rows):
                v = ins[name]
                v = v.rearrange("(r n) -> r n", n=P) if len(v.shape) == 1 else v.rearrange("a (r n) -> (a r) n", n=P)
                act.dma_start(st_vec[KD * n:KD * (n + 1), :], v).then_inc(vec_landed, 16)
            act.dma_start(x[:, :, :], ins["x"][0].rearrange("(t p) d -> p t d", p=P)).then_inc(x_landed, 16)
            for n, name in enumerate(("conv_b", "conv_ln_g", "conv_ln_b")):
                act.dma_start(st_c24[H1 * n:H1 * (n + 1), :], ins[name].rearrange("a (r n) -> (a r) n", n=P))\
                    .then_inc(small_landed, 16)
            act.dma_start(st_cw[:, :], ins["conv_w"][0]).then_inc(small_landed, 16)
            act.dma_start(st_fc[:, 0:3, :], ins["ffn_conv_w_2"][0].rearrange("t (r n) -> r t n", n=P)).then_inc(small_landed, 16)
            act.dma_start(st_fc[:, 3, :], ins["ffn_conv_b_2"][0].rearrange("(r n) -> r n", n=P)).then_inc(small_landed, 16)
            act.dma_start(qg[:, :], ins["na_q_g_2"][0:1, :].to_broadcast([P, HD])).then_inc(small_landed, 16)
            act.dma_start(kg[:, :], ins["na_k_g_2"][0:1, :].to_broadcast([P, HD])).then_inc(small_landed, 16)

            act.wait_ge(tr_done[0], 1)
            act.activation(cact[:, :], ps[:, 6, 0:48], ACT.Silu).then_inc(cact_ready, 1)
            act.activation(vecs[:, :], ps[:, 6, 0:112], ACT.Copy).then_inc(tr_free[0], 1)
            act.wait_ge(tr_done[1], 1)
            act.activation(cvec[:, :], ps[:, 7, 0:24 + H1 * TAPS], ACT.Copy).then_inc(tr_free[1], 1)
            act.wait_ge(tr_done[0], 2)
            act.activation(fcw[:, 0:3, :], ps[:, 6, 0:258].rearrange("p (t r) -> p t r", t=3), ACT.Copy).then_inc(tr_free[0], 1)
            act.wait_ge(tr_done[1], 2)
            act.activation(fcw[:, 3, :], ps[:, 7, 0:86], ACT.Copy).then_inc(tr_free[1], 1)
            link(act.activation(stat[:, 63:64], ones[:, 0:1], ACT.Copy))

            def row_squares(n, src, hold=None):
                if hold is not None:
                    act.wait_ge(*hold)
                act.activation(junk[:, :], src, ACT.Square, accum_out=stat[:, 32 + n % 4:33 + n % 4]).then_inc(ss_ready, 1)
                act.wait_ge(ss_ready, n + 1)
                act.activation(stat[:, 36 + n % 4:37 + n % 4], stat[:, 32 + n % 4:33 + n % 4], ACT.Sqrt,
                               scale=1.0 / D, bias=eps_rms[:, :]).then_inc(std_ready, 1)

            def modulated(n0, m_, e, idx):
                for o in range(NT):
                    t = NT - 1 - o
                    n = n0 + 2 * e + o
                    act.wait_ge(tr_done[t], m_ + e + 1)
                    if n >= 2:
                        act.wait_ge(hlo_ready, n - 1)
                    for k in range(4):
                        kk = 4 * e + k
                        s = act.activation(h_f[:, o, k * P:(k + 1) * P], ps[:, 6 + t, k * P:(k + 1) * P], ACT.Identity,
                                           scale=cols[:, idx, kk:kk + 1], bias=cols[:, idx + 1, kk:kk + 1])
                    s.then_inc(tr_free[t], 1)

            def first_chunk(T, n0, m_, idx, extra=lambda n: None):
                modulated(n0, m_, 0, idx)
                for n in range(CT):
                    if n < 3:
                        modulated(n0, m_, n + 1, idx)
                    extra(n)
                    hi(T, n + 3)

            act.wait_ge(x_landed, 16)
            for t in range(NT):
                row_squares(t, x[:, NT - 1 - t, :])
            for s in range(HALVES):
                for n in range(RING):
                    hi(T_AG, HTILES * s + n)
                for e in (2 * s, 2 * s + 1):
                    modulated(0, M["start"] + 1 + s, e, 0)
                for n in range(RING, HTILES):
                    hi(T_AG, HTILES * s + n)
            for j in range(3):
                hi(T_AG, START_TILES + j)

            def sigmoid_of_g(tiles):
                chunk_wait(T_AG, tiles)
                for t in range(NT):
                    s = act.activation(nat_a[:, t, :], ps[:, 2 + t, :], ACT.Sigmoid)
                s.then_inc(pair_free[1], 1)

            products = [0, 0]

            def conv_products(times):
                for _ in range(times):
                    if products[0] == len(CONV_PRODUCTS):
                        return
                    tap, pair = CONV_PRODUCTS[products[0]]
                    a = products[1]
                    products[0] += 1
                    products[1] += tap > 0
                    if tap and a >= 3:
                        act.wait_ge(conv_pool, a)
                    for c in (2 * pair, 2 * pair + 1):
                        dst, src, wv = conv_operands(c, tap)
                        if tap == 0:
                            s = act.activation(dst, src, ACT.Identity, scale=wv, bias=cvec[:, c:c + 1])
                        else:
                            s = act.activation(taps[:, a % 3 * 2 + c % 2, :], src, ACT.Copy, scale=wv)
                    s.then_inc(conv_prod, 1)

            sigmoid_of_g(START_TILES)
            act.wait_ge(const_ready, 5)
            for n in range(CT):
                if n == 4:
                    act.dma_start(post1[:, :], ins["mix_post_g"][0:1, :].to_broadcast([P, D])).then_inc(post_landed, 16)
                    act.wait_ge(pair_free[0], 2)
                hi(T_AG, START_TILES + n + 3)
                if n > 4:
                    conv_products(2)
            sigmoid_of_g(START_TILES + CT)

            def attention(U, Mb, nkt, head, beside):
                def exp(u):
                    act.wait_ge(max_ready, U + (u + 1))
                    act.activation(prob_of(u, nkt), prob_of(u, nkt), ACT.Exp,
                                   bias=stat[:, u % 2:u % 2 + 1], accum_out=stat[:, 4 + u % 2:5 + u % 2]).then_inc(exp_ready, 1)

                def out_of(u):
                    act.wait_ge(o_done, U + (u + 1))
                    act.activation(ff[:, head(u // 2), u % 2 * P:(u % 2 + 1) * P],
                                   ps[:, 2 + u % 2, 0:P].unsqueeze(1), ACT.Copy).then_inc(o_used, 1)

                exp(0)
                for u in range(PER_GROUP):
                    if u + 1 < PER_GROUP:
                        exp(u + 1)
                    beside(u)
                    act.wait_ge(tr_done[u % 2], Mb + (u // 2 + 1))
                    act.activation(p_t[:, u % 2, 0:nkt * P], ps[:, 6 + u % 2, 0:nkt * P], ACT.Copy).then_inc(tr_free[u % 2], 1)
                    if u >= 1:
                        out_of(u - 1)
                out_of(PER_GROUP - 1)

            for n in range(CT):
                conv_products(1)
                hi(T_QKV1, n + 3)
                conv_products(1)
            act.wait_ge(pair_free[2], 2)
            for i in range(2):
                T = T_QKV1 + i * (3 * CT)

                def evacuate(dst, b):
                    for t in range(NT):
                        s = act.activation(dst[:, t, :], ps[:, 2 * b + t, :], ACT.Copy)
                    s.then_inc(pair_free[b], 1)

                def evacuate_columns(dst, pair):
                    for b in range(2):
                        s = act.activation(dst[:, 2 * b:2 * b + 2, 0:SEQ],
                                           ps[:, 2 * pair + b, :].rearrange("p (g n) -> p g n", g=2), ACT.Copy)
                    s.then_inc(pair_free[pair], 1)

                chunk_wait(T, CT)
                evacuate_columns(q_t, 2)
                for n in range(CT, 2 * CT):
                    conv_products(1)
                    hi(T, n + 3)
                    conv_products(1)
                chunk_wait(T, 2 * CT)
                evacuate_columns(k_t, 0)
                for n in range(2 * CT, 3 * CT):
                    if i == 1 and n == 3 * CT - 1:
                        act.wait_ge(dev_ready, 1)
                        act.activation(tmp[:, :], ff[:, 8:16, :].rearrange("p g n -> p (g n)"), ACT.Square).then_inc(sq_ready, 1)
                    conv_products(1)
                    hi(T, n + 3)
                    conv_products(1)
                chunk_wait(T, 3 * CT)
                evacuate(v_n, 1)

                def beside_first(u):
                    hi(T, 3 * CT + u + 3)
                    conv_products(2)

                if i == 0:
                    attention(0, M["att1a"], NT, lambda h: slice(h, h + 1), beside_first)
                    continue
                act.wait_ge(tr_done[1], M["ln"] + 1)
                act.activation(rstd_ln[:, :], ps[:, 7, 0:SEQ], ACT.Sqrt, bias=eps_ln[:, :]).then_inc(tr_free[1], 1)

                assert products[0] == len(CONV_PRODUCTS)
                attention(PER_GROUP, M["att1"], NT, lambda h: slice(GH + h, GH + h + 1), lambda u: None)

            def scaled_silu():
                act.wait_ge(ln_ready, 1)
                for g in range(H1):
                    act.activation(ff[:, 8 + g, :], ff[:, 8 + g, :], ACT.Silu,
                                   scale=cvec[:, H1 + g:H1 + g + 1], bias=cvec[:, 2 * H1 + g:2 * H1 + g + 1])\
                        .then_inc(silu_done, 1)
                act.wait_ge(silu_done, H1)

            def stage_hi(F, k, src):
                act.activation(f_hi[:, k % 2, :], src, ACT.Copy).then_inc(fhi_ready, 1)

            def rows_phase(T0, F0, K, after_first=lambda: None):
                def one_k(k):
                    return ff[:, bass.ds(k, 1), :].rearrange("p o n -> p (o n)")

                act.wait_ge(tile_used, T0 + RING)
                stage_hi(F0, 0, one_k(0))
                after_first()
                with act.Fori(0, K // 2 - 1) as i:
                    T = T0 + i * 4
                    hi(T, 3)
                    stage_hi(F0, 1, one_k(i * 2 + 1))
                    hi(T, 4)
                    hi(T, 5)
                    stage_hi(F0, 0, one_k(i * 2 + 2))
                    hi(T, 6)
                T = T0 + 4 * (K // 2 - 1)
                hi(T, 3)
                stage_hi(F0, 1, one_k(K // 2 * 2 - 1))
                if K % 2 == 0:
                    for j in range(4, 7):
                        hi(T, j)
                else:
                    hi(T, 4)
                    hi(T, 5)
                    stage_hi(F0, 0, one_k(K - 1))

            def y_squares(n, Tend):
                act.wait_ge(tile_used, Tend + RING)
                for o in range(NT):
                    t = NT - 1 - o
                    row_squares(n + o, ps[:, 4 * t:4 * t + 4, :].rearrange("p b n -> p (b n)"))

            def x_squares(n, done):
                for o in range(NT):
                    row_squares(n + o, x[:, NT - 1 - o, :], (x_ready, done + o + 1))

            act.wait_ge(o_used, UNITS1)
            rows_phase(T_OUT1, F_OUT1, KD, scaled_silu)
            y_squares(2, T_FF1)

            x_squares(4, 0)
            first_chunk(T_FF1, 8, M["x2"], 2)

            def gate_act():
                for t in range(NT):
                    s = act.activation(sig[:, t, :], ps[:, t, :], ACT.Silu)
                s.then_inc(pair_free[0], 1)

            chunk_wait(T_FF1, CT)
            gate_act()
            act.dma_start(post2[:, :], ins["ffn_post_g"][0:1, :].to_broadcast([P, D])).then_inc(post_landed, 16)
            with act.Fori(0, NCH - 1) as i:
                T = T_FF1 + CT + i * (2 * CT)
                for n in range(2 * CT):
                    hi(T, n + 3)
                chunk_wait(T, 2 * CT)
                act.wait_ge(pair_free[1], i + (USE1["up1"] + 2))
                gate_act()
            T = T_FF1 + CT + (NCH - 1) * 2 * CT
            for n in range(CT):
                hi(T, n + 3)
            act.wait_ge(pair_free[1], USE1["up1"] + NCH + 1)
            for t in range(NT):
                act.dma_start(ctx_n[t][:, :], ins["ctx_2"][0, t * P:(t + 1) * P, :]).then_inc(ctx_landed, 16)
            rows_phase(T_DOWN1, F_DOWN1, FF1 // P)
            y_squares(6, T_QKV2)

            x_squares(8, NT)
            row_squares(10, ctx_n[1][:, :], (ctx_landed, 16 * NT))
            row_squares(11, ctx_n[0][:, :])
            first_chunk(T_QKV2, 16, M["lat"], 4, lambda n: modulated(24, M["ctx"], n - 4, 6) if n >= 4 else None)

            def qkv2(i, following):
                T = T_QKV2 + i * (3 * CT)
                Mb = i * 7 + M["qkv2"]
                SQ = i * 3 + 1

                def squares(b, n):
                    act.wait_ge(sq_read, SQ + n)
                    act.activation(p_t[:, :, :], ps[:, 2 * b:2 * b + 2, :], ACT.Square).then_inc(sq_ready, 1)
                    act.wait_ge(head_ss, i * 3 + (n + 1))
                    act.activation(stat[:, 16:24], stat[:, 8:16], ACT.Sqrt, scale=1.0 / HD,
                                   bias=eps_rms[:, :]).then_inc(head_std, 1)

                def transposed(dst, m_, at_):
                    for b in range(2):
                        act.wait_ge(tr_done[b], m_ + 1)
                        act.activation(dst[:, 2 * b:2 * b + 2, at_:at_ + SEQ],
                                       ps[:, 6 + b, :].rearrange("p (g n) -> p g n", g=2), ACT.Copy).then_inc(tr_free[b], 1)

                chunk_wait(T, CT)
                squares(2, 0)
                for n in range(CT, 2 * CT):
                    if n == CT + 4:
                        transposed(q_t, Mb, 0)
                    hi(T, n + 3)
                chunk_wait(T, 2 * CT)
                squares(0, 1)
                squares(1, 2)
                for n in range(2 * CT, 3 * CT):
                    if n == 2 * CT + 4:
                        transposed(k_t, Mb + 1, 0)
                        transposed(k_t, Mb + 2, SEQ)
                    hi(T, n + 3)
                chunk_wait(T, 3 * CT)
                for half, b in ((0, 2), (1, 0)):
                    for t in range(NT):
                        s = act.activation(v_n[:, NT * half + t, :], ps[:, 2 * b + t, :], ACT.Copy)
                    s.then_inc(pair_free[b], 1)
                attention(i * PER_GROUP + UNITS1, Mb + 3, 2 * NT, lambda h: bass.ds(i * GH + h, 1),
                          lambda u: hi(T, 3 * CT + u + 3) if following else None)

            with act.Fori(0, 3) as i:
                qkv2(i, True)
            qkv2(3, False)

            act.wait_ge(o_used, UNITS1 + 32)
            rows_phase(T_OUT2, F_OUT2, KD)

            x_squares(12, 2 * NT)
            first_chunk(T_FF2, 32, M["x7"], 8)

            def middle_tap(pair, col, groups):
                for b in range(2):
                    for g in range(2 * b, min(2 * b + 2, groups)):
                        act.activation(conv_t[:, g, :], ps[:, 2 * pair + b, g % 2 * SEQ:(g % 2 + 1) * SEQ], ACT.Identity,
                                       scale=fcw[:, 1, bass.ds(col + g, 1)],
                                       bias=fcw[:, 3, bass.ds(col + g, 1)]).then_inc(cv_ready, 1)

            def gate_silu(done, groups):
                for b in range(2):
                    act.wait_ge(taps_ready, done + (b + 1))
                    act.activation(gate_t[:, 2 * b:min(2 * b + 2, groups), :],
                                   conv_t[:, 2 * b:min(2 * b + 2, groups), :], ACT.Silu).then_inc(sig_ready, 1)

            UC = FF2 // P
            def gate_2(i, T, groups):
                for n in range(CT, 2 * CT):
                    hi(T, n + 3)
                    if n == CT:
                        act.wait_ge(ff_ready, i * 2 + 1)
                        middle_tap(0, i * GH, groups)
                    if n == CT + 3:
                        gate_silu(i * 4, groups)

            with act.Fori(0, NCH - 1) as i:
                T = T_FF2 + i * (2 * CT)
                gate_2(i, T, GH)
                for n in range(2 * CT, 3 * CT):
                    hi(T, n + 3)
                    if n == 2 * CT:
                        middle_tap(1, i * GH + UC, GH)
            T = T_FF2 + (NCH - 1) * 2 * CT
            gate_2(NCH - 1, T, TAILC // P)
            chunk_wait(T, 2 * CT)
            middle_tap(1, GH * (NCH - 1) + UC, TAILC // P)
            act.wait_ge(ff_ready, 2 * NCH + 1)
            rows_phase(T_DOWN2, F_DOWN2, FF2 // P)

        @block.vector
        def _(dve):
            steps = [0]

            def link(ins_, off=0):
                steps[0] += 1
                ins_.then_inc(dve_step, 1)
                dve.wait_ge(dve_step, off + steps[0])

            def lo(T, j):
                s = j % RING
                dve.wait_ge(hi_ready, T + (j + 1))
                dve.tensor_tensor(w_lo[:, s, :], raw[:, s, :], w_hi[:, s, :].bitcast(F32), ALU.subtract).then_inc(lo_ready, 1)

            def unit(n, k, half, vec, acc, then_ctx=None):
                dve.wait_ge(ada_landed[half], n * 8 + (16 - 8 * half - 16 * UNITS))
                dve.wait_ge(ada_used, n + 1)
                a = acc[:, half * TILE:(half + 1) * TILE]
                ins_ = dve.scalar_tensor_tensor(out=a, in0=ada[:, half, :], scalar=cact[:, bass.ds(k + vec * KD, 1)],
                                                in1=a, op0=ALU.mult, op1=ALU.add)
                if then_ctx is not None:
                    a2 = then_ctx[:, half * TILE:(half + 1) * TILE]
                    ins_ = dve.scalar_tensor_tensor(out=a2, in0=ada[:, half, :], scalar=cact[:, bass.ds(k + 2 * KD, 1)],
                                                    in1=a2, op0=ALU.mult, op1=ALU.add)
                ins_.then_inc(ada_used, 1)

            def clear(acc):
                dve.memset(acc[:, :], 0.0).then_inc(acc_clear, 1)

            def shift_cols(M_, idx):
                for b in range(2):
                    dve.wait_ge(tr_done[b], M_ + 1)
                    dve.tensor_copy(cols[:, idx, 8 * b:8 * b + 8], ps[:, 6 + b, 0:8]).then_inc(tr_free[b], 1)

            def scale_cols(M_, idx, g):
                for b in range(2):
                    dve.wait_ge(tr_done[b], M_ + 1)
                    dve.scalar_tensor_tensor(out=cols[:, idx, 8 * b:8 * b + 8], in0=ps[:, 6 + b, 0:8], scalar=1.0,
                                             in1=vecs[:, g + 8 * b:g + 8 * b + 8], op0=ALU.add, op1=ALU.mult)\
                        .then_inc(tr_free[b], 1)

            def gate_rows(M_, post=None):
                for c in range(4):
                    b = c % 2
                    dve.wait_ge(tr_done[b], M_ + c // 2 + 1)
                    dst = acc0[:, c * C:(c + 1) * C]
                    if post is not None:
                        ins_ = dve.tensor_tensor(dst, ps[:, 6 + b, :], post[:, c * C:(c + 1) * C], ALU.mult)
                    else:
                        ins_ = dve.tensor_copy(dst, ps[:, 6 + b, :])
                    ins_.then_inc(tr_free[b], 1)

            def rows_rstd(n):
                dve.wait_ge(std_ready, n + 1)
                r = stat[:, 40 + n % 4:41 + n % 4]
                link(dve.reciprocal(r, stat[:, 36 + n % 4:37 + n % 4]))
                return r

            def make_diag(n, slot):
                r = rows_rstd(n)
                dve.tensor_scalar(diag[:, slot, :], ident[:, :], r, None, ALU.mult).then_inc(xn_ready, 1)

            def split(n0, m_, e, hi_, lo_):
                for o in range(NT):
                    t = NT - 1 - o
                    n = n0 + 2 * e + o
                    f = h_f[:, o, :].rearrange("p (k n) -> p k n", k=4)
                    at_ = (slice(None), slice(4 * e, 4 * e + 4), slice(t * P, (t + 1) * P))
                    dve.wait_ge(tr_free[t], m_ + e + 1)
                    dve.tensor_copy(hi_[at_], f).then_inc(hhi_ready, 1)
                    dve.wait_ge(hhi_ready, n + 1)
                    dve.tensor_tensor(lo_[at_], f, hi_[at_].bitcast(F32), ALU.subtract).then_inc(hlo_ready, 1)

            def first_chunk(T, n0, m_, units, extra=lambda n: None):
                split(n0, m_, 0, h_hi, h_lo)
                for n in range(CT):
                    if n < 3:
                        split(n0, m_, n + 1, h_hi, h_lo)
                    extra(n)
                    lo(T, n + 3)
                    units(n)

            clear(acc1)
            clear(acc0)
            dve.wait_ge(cact_ready, 1)
            dve.wait_ge(acc_bias[0], 16)
            dve.wait_ge(acc_bias[1], 16)
            for s in range(HALVES):
                for o in range(HOPS * s, HOPS * (s + 1)):
                    p_, kt, sec = o // 4, o // 2 % 2, o % 2
                    slot, k = p_ % 2 * 2 + sec, p_ % BLOCKS * 2 + kt
                    if kt == 0:
                        dve.wait_ge(start_landed[slot], 16 * (p_ // 2 + 1))
                    if o >= 2:
                        dve.wait_ge(start_step, o - 1)
                    a = (acc1, acc0)[sec][:, s * TILE:(s + 1) * TILE]
                    dve.scalar_tensor_tensor(out=a, in0=start[slot][:, kt, :], scalar=cact[:, k:k + 1],
                                             in1=a, op0=ALU.mult, op1=ALU.add).then_inc(start_step, 1)
                if s == 0:
                    dve.wait_ge(const_ready, 2)
                    make_diag(0, 1)
                    make_diag(1, 0)
                m_ = M["start"] + 3 * s
                ks = slice(HK * s, HK * (s + 1))
                dve.wait_ge(tr_done[0], m_ + 1)
                dve.tensor_copy(cols[:, 1, ks], ps[:, 6, 0:HK]).then_inc(tr_free[0], 1)
                dve.wait_ge(tr_done[1], m_ + 1)
                dve.scalar_tensor_tensor(out=cols[:, 0, ks], in0=ps[:, 7, 0:HK], scalar=1.0,
                                         in1=vecs[:, 48 + HK * s:48 + HK * (s + 1)], op0=ALU.add, op1=ALU.mult)\
                    .then_inc(tr_free[1], 1)
                for e in (2 * s, 2 * s + 1):
                    split(0, M["start"] + 1 + s, e, h_hi, h_lo)
            clear(acc0)
            clear(acc1)

            def conv_in(i, a, pair):
                dve.wait_ge(pair_free[1], i + 2)
                for t in range(NT):
                    s = dve.tensor_tensor(u_pad[:, i * GH + 2 * t:i * GH + 2 * t + 2, TAPS - 1:PADT],
                                          ps[:, a + t, :].rearrange("p (g n) -> p g n", g=2),
                                          nat_a[:, t, :].rearrange("p (g n) -> p g n", g=2), ALU.mult)
                s.then_inc(pair_free[pair], 1)

            def mixer_unit(n):
                unit(UNITS * 2 + n, n % UNITS // 2, n % 2, 0, (acc0, acc1)[n // UNITS])

            dve.wait_ge(acc_bias[0], 32)
            dve.wait_ge(acc_bias[1], 32)
            for n in range(EARLY_UNITS):
                mixer_unit(n)
            dve.wait_ge(lo_ready, START_TILES + RING)
            for j in range(3):
                lo(T_AG, START_TILES + j)
            dve.wait_ge(start_step, HALVES * HOPS)
            conv_in(0, 0, 0)
            for n in range(CT):
                lo(T_AG, START_TILES + n + 3)
                mixer_unit(EARLY_UNITS + n)
            conv_in(1, 4, 2)

            def softmax(U, Mb, nkt, bias, landed, beside):
                def max_of(u):
                    b = u % 2
                    dve.wait_ge(s_done, U + (u + 1))
                    slots = 4 if nkt == NT else 2
                    if u >= slots:
                        dve.wait_ge(tr_done[b], Mb + ((u - slots) // 2 + 1))
                    pr = prob_of(u, nkt)
                    if landed is not None:
                        dve.wait_ge(bias_landed[b], landed + 32 * (u // 2 + 1))
                    if nkt > NT:
                        dve.tensor_scalar(pr[:, SEQ:2 * SEQ], ps[:, b, SEQ:2 * SEQ], SCALE, None, ALU.mult)
                    link(dve.scalar_tensor_tensor(out=pr[:, 0:SEQ], in0=ps[:, b, 0:SEQ], scalar=SCALE,
                                                  in1=bias[:, b, :], op0=ALU.mult, op1=ALU.add), off[0])
                    link(dve.tensor_reduce(stat[:, 2 + b:3 + b], pr, AX, ALU.max), off[0])
                    dve.tensor_scalar(stat[:, b:b + 1], stat[:, 2 + b:3 + b], -1.0, None, ALU.mult).then_inc(max_ready, 1)

                max_of(0)
                for u in range(PER_GROUP):
                    if u + 1 < PER_GROUP:
                        max_of(u + 1)
                    b = u % 2
                    dve.wait_ge(exp_ready, U + u + 1)
                    link(dve.reciprocal(stat[:, 6 + b:7 + b], stat[:, 4 + b:5 + b]), off[0])
                    pr = prob_of(u, nkt)
                    dve.tensor_scalar(pr, pr, stat[:, 6 + b:7 + b], None, ALU.mult).then_inc(p_ready, 1)
                    beside(u)

            off = [0]
            dve.wait_ge(const_ready, 5)
            taps_done = [0]

            def conv_taps():
                o = taps_done[0]
                if o == DVE_CONV_OPS:
                    return
                taps_done[0] += 1
                tap, c = o // len(DVE_CONV), DVE_CONV[o % len(DVE_CONV)]
                dst, src, wv = conv_operands(c, tap)
                if tap == 0:
                    s = dve.tensor_scalar(dst, src, wv, cvec[:, c:c + 1], ALU.mult, ALU.add)
                else:
                    dve.wait_ge(conv_step, o - len(DVE_CONV) + 1)
                    s = dve.scalar_tensor_tensor(out=dst, in0=src, scalar=wv, in1=dst, op0=ALU.mult, op1=ALU.add)
                s.then_inc(conv_step, 1)

            for n in range(CT):
                lo(T_QKV1, n + 3)
                mixer_unit(EARLY_UNITS + CT + n)
            dve.wait_ge(pair_free[2], 2)
            cv = ff[:, H1:2 * H1, :]
            for i in range(2):
                T = T_QKV1 + i * (3 * CT)
                for n in range(CT, 3 * CT):
                    if i == 1 and n == 2 * CT + 6:
                        dve.wait_ge(tr_done[0], M["ln"] + 1)
                        dve.tensor_tensor(cv, cv, ps[:, 6, 0:SEQ].unsqueeze(1).to_broadcast([P, H1, SEQ]), ALU.subtract)\
                            .then_inc(dev_ready, 1)
                        dve.wait_ge(dev_ready, 1)
                        dve.tensor_copy(stat[:, 62:63], ps[:, 6, 0:1]).then_inc(tr_free[0], 1)
                    conv_taps()
                    lo(T, n + 3)
                    conv_taps()
                    mixer_unit(EARLY_UNITS + CT + 3 * CT * i + n)

                def beside(u):
                    lo(T, 3 * CT + u + 3)
                    conv_taps()
                    mixer_unit(EARLY_UNITS + 4 * CT + u)

                if i == 0:
                    softmax(0, M["att1a"], NT, causal, None, beside)
                    dve.wait_ge(post_landed, 16)
                    gate_rows(M["a_g1"], post1)
            assert taps_done[0] == DVE_CONV_OPS
            dve.wait_ge(tr_free[1], M["ln"] + 1)
            link(dve.reciprocal(rstd_ln[:, :], rstd_ln[:, :]))
            dve.tensor_tensor(cv, cv, rstd_ln[:, :].unsqueeze(1).to_broadcast([P, H1, SEQ]), ALU.mult).then_inc(ln_ready, 1)
            softmax(PER_GROUP, M["att1"], NT, causal, None, lambda u: None)


            def stage_lo(F, k, src):
                dve.wait_ge(fhi_ready, F + 1)
                dve.tensor_tensor(f_lo[:, k % 2, :], src, f_hi[:, k % 2, :].bitcast(F32), ALU.subtract).then_inc(flo_ready, 1)

            def rows_pair(T, F, k0, units, last=False):
                def one_k(k):
                    return ff[:, bass.ds(k, 1), :].rearrange("p o n -> p (o n)")

                lo(T, 3)
                units(0)
                stage_lo(F + 1, 1, one_k(k0 + 1))
                lo(T, 4)
                units(1)
                lo(T, 5)
                units(2)
                if not last:
                    stage_lo(F + 2, 0, one_k(k0 + 2))
                lo(T, 6)
                units(3)

            def rows_first(F0):
                stage_lo(F0, 0, ff[:, 0, :])

            none = lambda j: None
            rows_first(F_OUT1)
            shift_cols(M["a_sh2"], 3)
            clear(acc1)
            dve.wait_ge(acc_bias[1], 48)
            with dve.Fori(0, KD // 2 - 1) as i:
                rows_pair(T_OUT1 + i * 4, F_OUT1 + i * 2, i * 2,
                          lambda j: unit(i * 4 + (UNITS * 4 + j), i * 2 + j // 2, j % 2, 0, acc1))
            i = KD // 2 - 1
            rows_pair(T_OUT1 + 4 * i, F_OUT1 + 2 * i, 2 * i,
                      lambda j: unit(4 * i + UNITS * 4 + j, 2 * i + j // 2, j % 2, 0, acc1), last=True)

            def update(done, norm, n=0):
                for o in range(NT):
                    t = NT - 1 - o
                    if norm:
                        r = rows_rstd(n + o)
                    if o:
                        dve.wait_ge(x_ready, done + o)
                    for half in range(2):
                        y = ps[:, 4 * t + 2 * half:4 * t + 2 * half + 2, :].rearrange("p b n -> p (b n)")
                        g = acc0[:, half * TILE:(half + 1) * TILE]
                        if norm:
                            s = dve.scalar_tensor_tensor(out=scr[half][:, :], in0=y, scalar=r, in1=g,
                                                         op0=ALU.mult, op1=ALU.mult)
                        else:
                            s = dve.tensor_tensor(scr[half][:, :], y, g, ALU.mult)
                    link(s)
                    for half in range(2):
                        xt = x[:, t, half * TILE:(half + 1) * TILE]
                        s = dve.tensor_tensor(xt, xt, scr[half][:, :], ALU.add)
                    s.then_inc(x_ready, 1)

            update(0, True, 2)
            make_diag(4, 1)
            scale_cols(M["a_sc2"], 2, 64)
            make_diag(5, 0)
            first_chunk(T_FF1, 8, M["x2"], lambda n: None)

            def gate_up_1(start, end, units):
                with dve.Fori(start, end) as i:
                    T = T_FF1 + CT + i * (2 * CT)
                    for n in range(CT):
                        lo(T, n + 3)
                        units(i, n)
                    up_act(i)
                    for n in range(CT, 2 * CT):
                        lo(T, n + 3)
                        units(i, n)

            def up_act(i):
                dve.wait_ge(tile_used, T_FF1 + 2 * CT + RING + i * (2 * CT))
                dve.wait_ge(pair_free[0], i + (USE0["gate1"] + 2))
                for b in range(2):
                    s = dve.tensor_tensor(ff[:, bass.ds(i * GH + 2 * b, 2), :],
                                          ps[:, 2 + b, :].rearrange("p (g n) -> p g n", g=2),
                                          sig[:, b, :].rearrange("p (g n) -> p g n", g=2), ALU.mult)
                s.then_inc(pair_free[1], 1)

            clear(acc0)
            dve.wait_ge(acc_bias[0], 48)

            def u_g2(i, n):
                if n % 2 == 0:
                    u = n // 2
                    unit(i * 8 + (UNITS * 5 + u), i * 4 + u // 2, u % 2, 0, acc0)

            gate_up_1(0, 4, u_g2)
            dve.wait_ge(post_landed, 32)
            gate_rows(M["a_g2"], post2)
            dve.wait_ge(table_landed, 16 * TABLE_DMAS)
            clear(acc1)
            clear(tmp)
            dve.wait_ge(acc_bias[1], 64)
            dve.wait_ge(acc_bias[2], 16)

            def u_sh1(i, n):
                if n % 2 == 0:
                    u = n // 2
                    unit(i * 8 + (UNITS * 6 + u - 32), i * 4 + (u // 2 - 16), u % 2, 1, acc1, tmp)

            gate_up_1(4, 8, u_sh1)
            shift_cols(M["b_sh1"], 5)
            shift_cols(M["b_sh1"] + 1, 7)
            clear(acc1)
            clear(tmp)
            gate_up_1(8, NCH - 1, lambda i, n: None)
            T = T_FF1 + CT + (NCH - 1) * 2 * CT
            for n in range(CT):
                lo(T, n + 3)
            up_act(NCH - 1)
            dve.wait_ge(acc_bias[1], 80)
            dve.wait_ge(acc_bias[2], 32)

            rows_first(F_DOWN1)
            with dve.Fori(0, 16) as i:
                rows_pair(T_DOWN1 + i * 4, F_DOWN1 + i * 2, i * 2,
                          lambda j: unit(i * 2 + (UNITS * 7 + j), i, j, 1, acc1, tmp) if j < 2 else None)
            with dve.Fori(16, FF1 // P // 2 - 1) as i:
                rows_pair(T_DOWN1 + i * 4, F_DOWN1 + i * 2, i * 2, none)
            i = FF1 // P // 2 - 1
            rows_pair(T_DOWN1 + 4 * i, F_DOWN1 + 2 * i, 2 * i, none, last=True)
            update(NT, True, 6)
            make_diag(8, 1)
            scale_cols(M["b_sc1"], 4, 80)
            scale_cols(M["b_sc1"] + 1, 6, 80)
            make_diag(9, 0)

            def ctx_rows(n):
                if n == 0:
                    make_diag(10, 3)
                    make_diag(11, 2)
                elif n >= 4:
                    split(24, M["ctx"], n - 4, hc_hi, hc_lo)

            first_chunk(T_QKV2, 16, M["lat"], lambda n: None, ctx_rows)
            clear(acc0)
            clear(acc1)
            dve.wait_ge(acc_bias[0], 64)
            dve.wait_ge(acc_bias[1], 96)
            dve.tensor_copy(stat[:, 62:63], stat[:, 63:64]).then_inc(sq_read, 1)

            def qkv2(i, following):
                T = T_QKV2 + i * (3 * CT)
                Mb = i * 7 + M["qkv2"]
                S = 3 + 3 * PER_GROUP
                off[0] = i * S if following else 0
                before = steps[0]

                def head_norm(dst, b, n, g):
                    dve.wait_ge(sq_ready, i * 3 + (n + 2))
                    ss = stat[:, 8:16]
                    dve.tensor_reduce(ss, p_t[:, :, :].rearrange("p t (h n) -> p (t h) n", n=HD), AX, ALU.add)\
                        .then_inc(head_ss, 1)
                    dve.wait_ge(head_std, i * 3 + (n + 1))
                    link(dve.reciprocal(stat[:, 24:32], stat[:, 16:24]), off[0])
                    for t in range(NT):
                        for h in range(GH):
                            c = t * GH + h
                            s = dve.scalar_tensor_tensor(out=dst[:, t, h * HD:(h + 1) * HD],
                                                         in0=ps[:, 2 * b + t, h * HD:(h + 1) * HD],
                                                         scalar=stat[:, 24 + c:25 + c], in1=g[:, :],
                                                         op0=ALU.mult, op1=ALU.mult)
                            if c == 0:
                                s.then_inc(sq_read, 1)
                    s.then_inc(pair_free[b], 1)

                def steps_of(n0):
                    for n in range(n0, n0 + CT):
                        lo(T, n + 3)
                        u = n - CT
                        unit(i * 16 + (UNITS * 8 + u), i * 4 + u // 4, u % 2, 1, (acc0, acc1)[u // 2 % 2])

                head_norm(nat_a, 2, 0, qg)
                steps_of(CT)
                head_norm(nat_b, 0, 1, kg)
                dve.wait_ge(tr_done[1], i * 7 + (M["qkv2"] + 1))
                head_norm(nat_a, 1, 2, kg)
                steps_of(2 * CT)
                softmax(i * PER_GROUP + UNITS1, Mb + 3, 2 * NT, bias_t, i * (32 * GH),
                        lambda u: lo(T, 3 * CT + u + 3) if following else None)
                assert steps[0] - before == S

            with dve.Fori(0, 3) as i:
                qkv2(i, True)
            off[0] = 0
            steps[0] += 2 * (3 + 3 * PER_GROUP)
            qkv2(3, False)
            off[0] = 0
            rows_first(F_OUT2)
            gate_rows(M["b_g1"])
            shift_cols(M["b_sh2"], 9)
            clear(acc1)
            dve.wait_ge(acc_bias[1], 112)
            with dve.Fori(0, KD // 2 - 1) as i:
                rows_pair(T_OUT2 + i * 4, F_OUT2 + i * 2, i * 2,
                          lambda j: unit(i * 4 + (UNITS * 10 + j), i * 2 + j // 2, j % 2, 1, acc1))
            i = KD // 2 - 1
            rows_pair(T_OUT2 + 4 * i, F_OUT2 + 2 * i, 2 * i,
                      lambda j: unit(4 * i + UNITS * 10 + j, 2 * i + j // 2, j % 2, 1, acc1), last=True)
            dve.wait_ge(tile_used, T_FF2 + RING)
            update(2 * NT, False)
            make_diag(12, 1)
            scale_cols(M["b_sc2"], 8, 96)
            make_diag(13, 0)

            first_chunk(T_FF2, 32, M["x7"], lambda n: None)
            clear(acc0)
            dve.wait_ge(acc_bias[0], 80)
            dve.tensor_copy(stat[:, 62:63], stat[:, 63:64]).then_inc(ff_ready, 1)

            def outer_taps(pair, done, col, groups, CV, bs=(0, 1)):
                for b in bs:
                    gs = range(2 * b, min(2 * b + 2, groups))
                    dve.wait_ge(cv_ready, CV + gs[-1] + 1)
                    for g in gs:
                        z = ps[:, 2 * pair + b, g % 2 * SEQ:(g % 2 + 1) * SEQ]
                        y = conv_t[:, g, 1:SEQ]
                        s = dve.scalar_tensor_tensor(out=y, in0=z[:, 0:SEQ - 1], scalar=fcw[:, 0, bass.ds(col + g, 1)],
                                                     in1=y, op0=ALU.mult, op1=ALU.add)
                    link(s, off[0])
                    for g in gs:
                        z = ps[:, 2 * pair + b, g % 2 * SEQ:(g % 2 + 1) * SEQ]
                        y = conv_t[:, g, 0:SEQ - 1]
                        s = dve.scalar_tensor_tensor(out=y, in0=z[:, 1:SEQ], scalar=fcw[:, 2, bass.ds(col + g, 1)],
                                                     in1=y, op0=ALU.mult, op1=ALU.add)
                    s.then_inc(taps_ready, 1)
                if 1 not in bs:
                    return
                dve.wait_ge(taps_ready, done + 2)
                dve.tensor_copy(stat[:, 62:63], stat[:, 63:64]).then_inc(pair_free[pair], 1)

            def times_gate(i, groups):
                for b in range(2):
                    n = min(2, groups - 2 * b)
                    dve.wait_ge(sig_ready, i * 2 + (b + 1))
                    dve.tensor_tensor(ff[:, bass.ds(i * GH + 2 * b, n), :], conv_t[:, 2 * b:2 * b + n, :],
                                      gate_t[:, 2 * b:2 * b + n, :], ALU.mult).then_inc(ff_ready, 1)

            def gate_up_2(start, end, units):
                S = 4
                with dve.Fori(start, end) as i:
                    off[0] = (i - start) * S
                    before = steps[0]
                    T = T_FF2 + i * (2 * CT)
                    for n in range(CT, 2 * CT):
                        lo(T, n + 3)
                        if n - CT in (0, 2):
                            outer_taps(0, i * 4, i * GH, GH, i * (2 * GH), ((n - CT) // 2,))
                        units(i, n - CT)
                    for n in range(2 * CT, 3 * CT):
                        lo(T, n + 3)
                        if n - 2 * CT in (0, 2):
                            outer_taps(1, i * 4 + 2, i * GH + FF2 // P, GH, i * (2 * GH) + GH, ((n - 2 * CT) // 2,))
                        if n == 2 * CT + 4:
                            times_gate(i, GH)
                        units(i, n - CT)
                    assert steps[0] - before == S
                steps[0] += (end - start - 1) * S
                off[0] = 0

            def u_g2b(i, n):
                if n % 2 == 0:
                    u = n // 2
                    unit(i * 8 + (UNITS * 11 + u), i * 4 + u // 2, u % 2, 1, acc0)

            gate_up_2(0, 4, u_g2b)
            gate_rows(M["b_g2"])
            gate_up_2(4, NCH - 1, lambda i, n: None)
            i = NCH - 1
            T = T_FF2 + i * 2 * CT
            for n in range(CT, 2 * CT):
                lo(T, n + 3)
                if n == CT:
                    outer_taps(0, i * 4, i * GH, TAILC // P, i * 2 * GH)
            outer_taps(1, i * 4 + 2, i * GH + FF2 // P, TAILC // P, i * 2 * GH + TAILC // P)
            times_gate(i, TAILC // P)
            K = FF2 // P
            dve.wait_ge(ff_ready, 2 * NCH + 1)
            rows_first(F_DOWN2)
            with dve.Fori(0, K // 2 - 1) as i:
                rows_pair(T_DOWN2 + i * 4, F_DOWN2 + i * 2, i * 2, none)
            i = K // 2 - 1
            lo(T_DOWN2 + 4 * i, 3)
            stage_lo(F_DOWN2 + 2 * i + 1, 1, ff[:, 2 * i + 1, :])
            lo(T_DOWN2 + 4 * i, 4)
            lo(T_DOWN2 + 4 * i, 5)
            stage_lo(F_DOWN2 + 2 * i + 2, 0, ff[:, 2 * i + 2, :])
            dve.wait_ge(tile_used, T_END + RING)
            update(3 * NT, False)

        @block.tensor
        def _(pe):
            pe.sem_inc(lo_ready, RING)
            pe.sem_inc(tile_used, RING)
            pe.sem_inc(ada_used, 2 + 2 * UNITS)
            pe.sem_inc(conv_pool, 2)
            for s in pair_free:
                pe.sem_inc(s, 1)

            def bank_free(b, m_):
                if not (isinstance(m_, int) and m_ == 0):
                    pe.wait_ge(tr_free[b], m_)

            def chunk_tile(T, j0, j, targets, width=C):
                s = (j0 + j) % RING
                pe.wait_ge(lo_ready, T + (j0 + j + 1 + RING))
                for (hi_, lo_, pair, use) in targets:
                    if j == 0:
                        pe.wait_ge(pair_free[pair], use + 1)
                    for kk in range(2):
                        k = 2 * j + kk
                        wh = w_hi[:, s, kk * width:(kk + 1) * width]
                        wl = w_lo[:, s, kk * width:(kk + 1) * width]
                        for t in range(NT):
                            o = ps[:, 2 * pair + t, 0:width]
                            a = slice(t * P, (t + 1) * P)
                            pe.matmul(o, hi_[:, k, a], wh, start=(k == 0), stop=False)
                            pe.matmul(o, hi_[:, k, a], wl, start=False, stop=False)
                            mm = pe.matmul(o, lo_[:, k, a], wh, start=False, stop=(k == KD - 1))
                mm.then_inc(tile_used, 1)

            def chunk(T, j0, targets, width=C, middle=None):
                for j in range(CT):
                    if j == 4 and middle is not None:
                        middle()
                    chunk_tile(T, j0, j, targets, width)

            def columns_tile(T, j0, j, pair, use, width=C):
                s = (j0 + j) % RING
                pe.wait_ge(lo_ready, T + (j0 + j + 1 + RING))
                if j == 0:
                    pe.wait_ge(pair_free[pair], use + 1)
                for kk in range(2):
                    k = 2 * j + kk
                    for g in range(width // P):
                        o = ps[:, 2 * pair + g // 2, g % 2 * SEQ:(g % 2 + 1) * SEQ]
                        a = slice(kk * width + g * P, kk * width + (g + 1) * P)
                        pe.matmul(o, w_hi[:, s, a], h_hi[:, k, :], start=(k == 0 and g % 2 == 0), stop=False)
                        pe.matmul(o, w_hi[:, s, a], h_lo[:, k, :], start=False, stop=False)
                        mm = pe.matmul(o, w_lo[:, s, a], h_hi[:, k, :], start=False,
                                       stop=(k == KD - 1 and (g % 2 == 1 or g == width // P - 1)))
                mm.then_inc(tile_used, 1)

            def columns_chunk(T, j0, pair, use, width=C):
                for j in range(CT):
                    columns_tile(T, j0, j, pair, use, width)

            def to_columns(src, m_, groups=GH):
                for b in range(2):
                    bank_free(b, m_)
                    for g in range(2 * b, min(2 * b + 2, groups)):
                        for t in range(NT):
                            mm = pe.transpose(ps[:, 6 + b, (g % 2 * NT + t) * P:(g % 2 * NT + t + 1) * P],
                                              src[:, t, g * P:(g + 1) * P], ident[:, :])
                    mm.then_inc(tr_done[b], 1)

            def sum_columns(acc, m_):
                for b in range(2):
                    bank_free(b, m_)
                    for k in range(8):
                        kk = 8 * b + k
                        mm = pe.matmul(ps[:, 6 + b, k:k + 1], acc[:, kk * P:(kk + 1) * P], ones[:, 0:1],
                                       start=True, stop=True)
                    mm.then_inc(tr_done[b], 1)

            def sum_rows(m_):
                for c in range(4):
                    b = c % 2
                    bank_free(b, m_ + c // 2)
                    pe.matmul(ps[:, 6 + b, :], ones[:, :], acc0[:, c * C:(c + 1) * C], start=True, stop=True)\
                        .then_inc(tr_done[b], 1)

            def scaled_rows(src, slot, m_, e, xn):
                for o in range(NT):
                    t = NT - 1 - o
                    pe.wait_ge(xn_ready, xn + o + 1)
                    bank_free(t, m_ + e)
                    for k in range(4):
                        kk = 4 * e + k
                        mm = pe.matmul(ps[:, 6 + t, k * P:(k + 1) * P], src(t)[:, kk * P:(kk + 1) * P],
                                       diag[:, slot + t, :], start=True, stop=True)
                    mm.then_inc(tr_done[t], 1)

            def first_chunk(T, tile, m_, xn, n0, extra=lambda j: None):
                rows = lambda e: scaled_rows(lambda t: x[:, t, :], 0, m_, e, xn)
                rows(0)
                rows(1)
                for j in range(CT):
                    if j == 1 or j == 3:
                        rows(2 + j // 2)
                    extra(j)
                    if j % 2 == 0:
                        pe.wait_ge(hlo_ready, n0 + j + 2)
                    tile(T, 0, j)

            lat = (h_hi, h_lo)
            con = (hc_hi, hc_lo)

            pe.wait_ge(const_ready, 2)
            pe.wait_ge(vec_landed, 16 * 7)
            pe.transpose(ps[:, 6, 0:112], st_vec[:, :], ident[0:112, 0:112]).then_inc(tr_done[0], 1)
            pe.wait_ge(small_landed, 16 * 8)
            pe.transpose(ps[:, 7, 0:24], st_c24[:, :], ident[0:24, 0:24])
            for g in range(H1):
                mm = pe.transpose(ps[:, 7, 24 + g * TAPS:24 + (g + 1) * TAPS], st_cw[:, g * P:(g + 1) * P],
                                  ident[0:TAPS, 0:TAPS])
            mm.then_inc(tr_done[1], 1)
            bank_free(0, 1)
            for t in range(3):
                mm = pe.transpose(ps[:, 6, t * 86:(t + 1) * 86], st_fc[:, t, :], ident[0:86, 0:86])
            mm.then_inc(tr_done[0], 1)
            bank_free(1, 1)
            pe.transpose(ps[:, 7, 0:86], st_fc[:, 3, :], ident[0:86, 0:86]).then_inc(tr_done[1], 1)

            for s in range(HALVES):
                m_ = M["start"] + 3 * s
                pe.wait_ge(start_step, HOPS * (s + 1))
                for b, acc in ((0, acc1), (1, acc0)):
                    bank_free(b, m_)
                    for k in range(HK):
                        kk = HK * s + k
                        mm = pe.matmul(ps[:, 6 + b, k:k + 1], acc[:, kk * P:(kk + 1) * P], ones[:, 0:1], start=True, stop=True)
                    mm.then_inc(tr_done[b], 1)
                for e in (2 * s, 2 * s + 1):
                    scaled_rows(lambda t: x[:, t, :], 0, M["start"] + 1 + s, e, 0)
                for n in range(HTILES):
                    j = HK // 2 * s + n // 3
                    if n % 3 == 0 and j % 2 == 0:
                        pe.wait_ge(hlo_ready, j + 2)
                    columns_tile(T_AG, HTILES * s + n - j, j, n % 3, 0)

            columns_chunk(T_AG, START_TILES, 1, 1)

            def attention(U, Mb, nkt, first, beside):
                def scores(u):
                    h, c = u // 2, u % 2
                    pe.matmul(ps[:, u % 2, 0:nkt * P], q_t[:, h, c * P:(c + 1) * P], k_t[:, h, 0:nkt * P],
                              start=True, stop=True).then_inc(s_done, 1)

                def values(u):
                    pe.wait_ge(tr_free[u % 2], Mb + (u // 2 + 1))
                    if u >= 2:
                        pe.wait_ge(o_used, U + (u - 1))
                    for k in range(nkt):
                        mm = pe.matmul(ps[:, 2 + u % 2, 0:P], v_n[:, k, u // 2 * HD:(u // 2 + 1) * HD],
                                       p_t[:, u % 2, k * P:(k + 1) * P], start=(k == 0), stop=(k == nkt - 1))
                    mm.then_inc(o_done, 1)

                for b in range(2):
                    pe.wait_ge(tr_free[b], Mb)
                first()
                scores(0)
                scores(1)
                for u in range(PER_GROUP):
                    if u + 2 < PER_GROUP:
                        pe.wait_ge(max_ready, U + (u + 1))
                        scores(u + 2)
                    beside(u)
                    pe.wait_ge(p_ready, U + (u + 1))
                    bank_free(u % 2, Mb + u // 2)
                    for k in range(nkt):
                        mm = pe.transpose(ps[:, 6 + u % 2, k * P:(k + 1) * P], prob_of(u, nkt)[:, k * P:(k + 1) * P],
                                          ident[:, :])
                    mm.then_inc(tr_done[u % 2], 1)
                    if u >= 1:
                        values(u - 1)
                values(PER_GROUP - 1)
                pe.wait_ge(o_used, U + PER_GROUP)

            columns_chunk(T_QKV1, 0, 2, USE2["q1"])
            for i in range(2):
                T = T_QKV1 + i * (3 * CT)

                def conv_mean():
                    if i == 1:
                        pe.wait_ge(conv_step, DVE_CONV_OPS)
                        pe.wait_ge(conv_pool, 2 + CONV_SUMS)
                        bank_free(0, M["ln"])
                        for g in range(H1):
                            mm = pe.matmul(ps[:, 6, 0:SEQ], mean1[:, :], ff[:, H1 + g, :], start=(g == 0), stop=(g == H1 - 1))
                        mm.then_inc(tr_done[0], 1)

                def qkv_written():
                    pe.wait_ge(pair_free[2], i + (USE2["q1"] + 2))
                    pe.wait_ge(pair_free[0], i + (USE0["k1"] + 2))
                    pe.wait_ge(pair_free[1], i + (USE1["v1"] + 2))

                columns_chunk(T, CT, 0, i + USE0["k1"])
                chunk(T, 2 * CT, [(*lat, 1, i + USE1["v1"])], middle=conv_mean)
                if i == 0:
                    attention(0, M["att1a"], NT, qkv_written, lambda u: columns_tile(T, 3 * CT, u, 2, USE2["q1"] + 1))
                    pe.wait_ge(ada_used, 2 + 3 * UNITS)
                    sum_rows(M["a_g1"])
            pe.wait_ge(sq_ready, 1)
            bank_free(1, M["ln"])
            for g in range(H1):
                mm = pe.matmul(ps[:, 7, 0:SEQ], mean1[:, :], tmp[:, g * SEQ:(g + 1) * SEQ], start=(g == 0), stop=(g == H1 - 1))
            mm.then_inc(tr_done[1], 1)
            attention(PER_GROUP, M["att1"], NT, qkv_written, lambda u: None)
            pe.wait_ge(ada_used, 2 + 4 * UNITS)
            sum_columns(acc1, M["a_sh2"])

            def row_tile(T, k, F, first, last):
                pe.wait_ge(flo_ready, F + 1)
                for half in range(2):
                    s = (2 * k + half) % RING
                    pe.wait_ge(lo_ready, T + (half + 1 + RING))
                    for t in range(NT):
                        a = slice(t * P, (t + 1) * P)
                        for c in range(2):
                            o = ps[:, 4 * t + 2 * half + c, :]
                            wh, wl = w_hi[:, s, c * C:(c + 1) * C], w_lo[:, s, c * C:(c + 1) * C]
                            pe.matmul(o, f_hi[:, k % 2, a], wh, start=first, stop=False)
                            pe.matmul(o, f_hi[:, k % 2, a], wl, start=False, stop=False)
                            mm = pe.matmul(o, f_lo[:, k % 2, a], wh, start=False, stop=last)
                    mm.then_inc(tile_used, 1)

            def rows_phase(T0, F0, K, m_, uses):
                for b in range(2):
                    pe.wait_ge(tr_free[b], m_)
                for p_, u in enumerate(uses):
                    pe.wait_ge(pair_free[p_], u + 1)
                row_tile(T0, 0, F0, True, False)
                row_tile(T0 + 2, 1, F0 + 1, False, False)
                with pe.Fori(1, (K - 1) // 2) as i:
                    for k in range(2):
                        row_tile(T0 + 2 * k + i * 4, k, F0 + k + i * 2, False, False)
                for k in range((K - 1) // 2 * 2, K):
                    row_tile(T0 + 2 * k, k, F0 + k, False, k == K - 1)

            rows_phase(T_OUT1, F_OUT1, KD, M["a_sc2"], (3, 4, 3))

            pe.wait_ge(x_ready, 1)
            sum_columns(acc1, M["a_sc2"])
            pe.wait_ge(x_ready, NT)
            first_chunk(T_FF1, lambda *a: columns_tile(*a, 0, USE0["gate1"]), M["x2"], 2, 8)

            def gate_up_1(start_, end):
                with pe.Fori(start_, end) as i:
                    T = T_FF1 + CT + i * (2 * CT)
                    columns_chunk(T, 0, 1, i + USE1["up1"])
                    columns_chunk(T, CT, 0, i + (USE0["gate1"] + 1))

            gate_up_1(0, 4)
            pe.wait_ge(ada_used, 2 + 6 * UNITS)
            sum_rows(M["a_g2"])
            gate_up_1(4, 8)
            pe.wait_ge(ada_used, 2 + 7 * UNITS)
            sum_columns(acc1, M["b_sh1"])
            sum_columns(tmp, M["b_sh1"] + 1)
            gate_up_1(8, NCH - 1)
            columns_chunk(T_FF1 + CT + (NCH - 1) * 2 * CT, 0, 1, USE1["up1"] + NCH - 1)
            rows_phase(T_DOWN1, F_DOWN1, FF1 // P, M["b_sc1"], (USE0["gate1"] + NCH, USE1["up1"] + NCH, 3))

            pe.wait_ge(x_ready, NT + 1)
            sum_columns(acc1, M["b_sc1"])
            sum_columns(tmp, M["b_sc1"] + 1)
            pe.wait_ge(x_ready, 2 * NT)

            def ctx_rows(e):
                scaled_rows(lambda t: ctx_n[t], 2, M["ctx"], e, 6)

            first_chunk(T_QKV2, lambda *a: chunk_tile(*a, [(*lat, 2, USE2["qkv2"])]), M["lat"], 4, 16,
                        lambda j: ctx_rows(j - 5) if j >= 5 else None)
            ctx_rows(3)
            pe.wait_ge(hlo_ready, 32)

            def qkv2(i, following):
                T = T_QKV2 + i * (3 * CT)
                Mb = i * 7 + M["qkv2"]

                def q_columns():
                    pe.wait_ge(pair_free[2], i * 2 + (USE2["qkv2"] + 2))
                    to_columns(nat_a, Mb)

                def k_columns():
                    pe.wait_ge(pair_free[0], i * 2 + (USE0["qkv2"] + 2))
                    to_columns(nat_b, Mb + 1)
                    pe.wait_ge(pair_free[1], i + (USE1["kc2"] + 2))
                    to_columns(nat_a, Mb + 2)

                def v_written():
                    pe.wait_ge(pair_free[2], i * 2 + (USE2["qkv2"] + 3))
                    pe.wait_ge(pair_free[0], i * 2 + (USE0["qkv2"] + 3))

                chunk(T, CT, [(*lat, 0, i * 2 + USE0["qkv2"]), (*con, 1, i + USE1["kc2"])], middle=q_columns)
                chunk(T, 2 * CT, [(*lat, 2, i * 2 + (USE2["qkv2"] + 1)), (*con, 0, i * 2 + (USE0["qkv2"] + 1))],
                      middle=k_columns)
                attention(i * PER_GROUP + UNITS1, Mb + 3, 2 * NT, v_written,
                          lambda u: chunk_tile(T, 3 * CT, u, [(*lat, 2, i * 2 + (USE2["qkv2"] + 2))]) if following else None)

            with pe.Fori(0, 3) as i:
                qkv2(i, True)
            qkv2(3, False)
            sum_rows(M["b_g1"])
            sum_columns(acc1, M["b_sh2"])
            rows_phase(T_OUT2, F_OUT2, KD, M["b_sc2"], (USE0["gate2"], USE1["up2"], USE2["qkv2"] + 8))

            pe.wait_ge(x_ready, 2 * NT + 1)
            sum_columns(acc1, M["b_sc2"])
            pe.wait_ge(x_ready, 3 * NT)
            first_chunk(T_FF2, lambda *a: columns_tile(*a, 0, USE0["gate2"]), M["x7"], 8, 32)

            for start_, end in ((0, 4), (4, NCH - 2)):
                with pe.Fori(start_, end) as i:
                    T = T_FF2 + CT + i * (2 * CT)
                    columns_chunk(T, 0, 1, i + USE1["up2"])
                    columns_chunk(T, CT, 0, i + (USE0["gate2"] + 1))
                if end == 4:
                    pe.wait_ge(ada_used, 2 + 12 * UNITS)
                    sum_rows(M["b_g2"])
            i = NCH - 2
            T = T_FF2 + CT + i * 2 * CT
            columns_chunk(T, 0, 1, i + USE1["up2"])
            columns_chunk(T, CT, 0, i + USE0["gate2"] + 1, TAILC)
            columns_chunk(T + 2 * CT, 0, 1, i + 1 + USE1["up2"], TAILC)
            rows_phase(T_DOWN2, F_DOWN2, FF2 // P, M["end"],
                       (USE0["gate2"] + NCH, USE1["up2"] + NCH, USE2["qkv2"] + 8))


_INS = ["x", "c", "ada_w", "ada_b", "mix_pre_g", "mix_post_g", "w_in", "conv_w", "conv_b", "conv_ln_g", "conv_ln_b",
        "w_out", "ffn_pre_g", "ffn_post_g", "w_gate", "w_up", "w_down", "c_2", "ctx_2", "c_ctx_2", "norm_mix_g_2",
        "norm_ffn_g_2", "w_ada_2", "b_ada_2", "na_w_qkv_2", "na_q_g_2", "na_k_g_2", "na_rpb_2", "na_w_o_2",
        "ffn_w_up_2", "ffn_conv_w_2", "ffn_conv_b_2", "ffn_w_down_2"]


def kernel(**inputs):
    import numpy as np
    import concourse.bacc as bacc
    from concourse.bass_utils import run_bass_kernel_spmd

    nc = bacc.Bacc("TRN2", target_bir_lowering=False, num_devices=1)
    arrays, ins = {}, {}
    for name in _INS:
        a = np.ascontiguousarray(inputs[name])
        arrays[f"in_{name}"] = a
        ins[name] = nc.dram_tensor(f"in_{name}", a.shape, mybir.dt.from_np(a.dtype), kind="ExternalInput").ap()
    out = nc.dram_tensor("out", (1, SEQ, D), F32, kind="ExternalOutput").ap()
    program(nc, ins, out)
    r = run_bass_kernel_spmd(nc, [arrays], core_ids=[0])
    return r.results[0]["out"]
```
